# Optimizing a Trainium2 kernel written in Bass

```python
import math
import jax, jax.numpy as jnp
from jax import lax
import numpy as np
import jax
import jax.numpy as jnp

D_MODEL = 1024
BATCH = 1
SEQ = 256
DEPTH = 2

D_MIX = D_MODEL
N_MIXERS = 4
D_GROUP = D_MIX // N_MIXERS

MLA_HEADS = 4
MLA_Q_RANK = D_MODEL // 4
MLA_KV_RANK = D_MODEL // 8
MLA_NOPE = 64
MLA_ROPE = 32
MLA_V = D_GROUP // MLA_HEADS
ROPE_THETA = 10000.0

CONV_WIDTH = 3
CONV_CH = D_GROUP

POOL_WINDOWS = (2, 4, 8, 16)
POOL_GROUPS = len(POOL_WINDOWS)
POOL_CH = D_GROUP // POOL_GROUPS

SWA_HEADS = 4
SWA_KV_HEADS = 2
SWA_HEAD_DIM = D_GROUP // SWA_HEADS
SWA_WINDOW = 128

BLOCK = 128

D_FF = -(-8 * D_MODEL // (3 * 256)) * 256

RMS_EPS = 1e-6

IN_SPLITS = (MLA_Q_RANK, MLA_KV_RANK, MLA_ROPE,
             CONV_CH, CONV_CH, CONV_CH,
             D_GROUP,
             SWA_HEADS * SWA_HEAD_DIM,
             SWA_KV_HEADS * SWA_HEAD_DIM,
             SWA_KV_HEADS * SWA_HEAD_DIM)
D_IN = sum(IN_SPLITS)


def _split_points():
    pts, acc = [], 0
    for w in IN_SPLITS[:-1]:
        acc += w
        pts.append(acc)
    return pts

def _alibi_slopes(n):
    return np.asarray([2.0 ** (-8.0 * (i + 1) / n) for i in range(n)], dtype=np.float32)

def rmsnorm(x, g):
    xf = x.astype(jnp.float32)
    y = xf * lax.rsqrt(jnp.mean(xf * xf, axis=-1, keepdims=True) + RMS_EPS)
    return (y * g.astype(jnp.float32)).astype(x.dtype)

def rope_tables(seq, dim, dtype):
    inv = 1.0 / (ROPE_THETA ** (jnp.arange(0, dim, 2, dtype=jnp.float32) / dim))
    ang = jnp.arange(seq, dtype=jnp.float32)[:, None] * inv[None, :]
    return jnp.cos(ang).astype(dtype), jnp.sin(ang).astype(dtype)

def apply_rope(x, cos, sin):
    x1, x2 = jnp.split(x, 2, axis=-1)
    c = cos[:, None, :]
    s = sin[:, None, :]
    return jnp.concatenate([x1 * c - x2 * s, x1 * s + x2 * c], axis=-1)

def mla_attention(c_q, c_kv, k_r, q_norm_g, kv_norm_g, w_uq, w_ukv, cos, sin):
    b, s, _ = c_q.shape
    dqk = MLA_NOPE + MLA_ROPE
    q = (rmsnorm(c_q, q_norm_g) @ w_uq).reshape(b, s, MLA_HEADS, dqk)
    q_nope, q_rot = q[..., :MLA_NOPE], q[..., MLA_NOPE:]
    q_rot = apply_rope(q_rot, cos, sin)
    kv = (rmsnorm(c_kv, kv_norm_g) @ w_ukv).reshape(b, s, MLA_HEADS, MLA_NOPE + MLA_V)
    k_nope, v = kv[..., :MLA_NOPE], kv[..., MLA_NOPE:]
    k_rot = apply_rope(k_r[:, :, None, :], cos, sin)
    k = jnp.concatenate([k_nope, jnp.broadcast_to(k_rot, (b, s, MLA_HEADS, MLA_ROPE))], axis=-1)
    q = jnp.concatenate([q_nope, q_rot], axis=-1) * (1.0 / math.sqrt(dqk))
    nb = s // BLOCK
    qb = q.reshape(b, nb, BLOCK, MLA_HEADS, dqk).transpose(1, 0, 2, 3, 4)
    key_pos = jnp.arange(s)

    def one_block(args):
        q_blk, i = args
        sc = jnp.einsum('bqhd,bkhd->bhqk', q_blk, k).astype(jnp.float32)
        q_pos = i * BLOCK + jnp.arange(BLOCK)
        causal = key_pos[None, :] <= q_pos[:, None]
        sc = jnp.where(causal[None, None], sc, -jnp.inf)
        p = jax.nn.softmax(sc, axis=-1).astype(v.dtype)
        return jnp.einsum('bhqk,bkhd->bqhd', p, v)

    out = lax.map(one_block, (qb, jnp.arange(nb)))
    return out.transpose(1, 0, 2, 3, 4).reshape(b, s, MLA_HEADS * MLA_V)

def short_gated_conv(gate_b, gate_c, u, conv_w):
    z = gate_c * u
    y = lax.conv_general_dilated(
        z, conv_w[:, None, :].astype(z.dtype), window_strides=(1,),
        padding=[(CONV_WIDTH - 1, 0)], dimension_numbers=('NWC', 'WIO', 'NWC'),
        feature_group_count=CONV_CH)
    return gate_b * y

def multiscale_pool(u, pool_w, pool_scale):
    b, s, _ = u.shape
    uf = u.astype(jnp.float32)
    cs = jnp.cumsum(uf, axis=1)
    pos = jnp.arange(s)
    outs = []
    for g, w in enumerate(POOL_WINDOWS):
        cs_g = cs[:, :, g * POOL_CH:(g + 1) * POOL_CH]
        lag = jnp.pad(cs_g, ((0, 0), (w, 0), (0, 0)))[:, :s]
        count = jnp.minimum(pos + 1, w).astype(jnp.float32)[None, :, None]
        outs.append((cs_g - lag) / count)
    pooled = jnp.stack(outs, axis=2) - uf.reshape(b, s, POOL_GROUPS, POOL_CH)
    mixed = jnp.einsum('bsgc,gcd->bsgd', pooled.astype(u.dtype), pool_w)
    return mixed.reshape(b, s, D_GROUP) * pool_scale

def swa_sink_attention(q, k, v, sinks, slopes):
    b, s, _, hd = q.shape
    grp = SWA_HEADS // SWA_KV_HEADS
    nb = s // BLOCK
    qb = q.reshape(b, nb, BLOCK, SWA_KV_HEADS, grp, hd)
    kb = k.reshape(b, nb, BLOCK, SWA_KV_HEADS, hd)
    vb = v.reshape(b, nb, BLOCK, SWA_KV_HEADS, hd)

    def with_prev(t):
        prev = jnp.pad(t, ((0, 0), (1, 0), (0, 0), (0, 0), (0, 0)))[:, :nb]
        return jnp.concatenate([prev, t], axis=2)

    kk, vv = with_prev(kb), with_prev(vb)
    sc = jnp.einsum('bnqkgd,bnskd->bnkgqs', qb, kk).astype(jnp.float32) * (1.0 / math.sqrt(hd))
    blk = jnp.arange(nb)[:, None] * BLOCK
    q_pos = blk + jnp.arange(BLOCK)[None, :]
    k_pos = blk - BLOCK + jnp.arange(2 * BLOCK)[None, :]
    dist = q_pos[:, :, None] - k_pos[:, None, :]
    valid = (dist >= 0) & (dist < SWA_WINDOW) & (k_pos[:, None, :] >= 0)
    sl = jnp.asarray(slopes).reshape(SWA_KV_HEADS, grp)
    bias = -sl[None, None, :, :, None, None] * dist.astype(jnp.float32)[None, :, None, None, :, :]
    sc = jnp.where(valid[None, :, None, None], sc + bias, -jnp.inf)
    sink = jnp.broadcast_to(
        sinks.astype(jnp.float32).reshape(SWA_KV_HEADS, grp)[None, None, :, :, None, None],
        sc.shape[:-1] + (1,))
    p = jax.nn.softmax(jnp.concatenate([sc, sink], axis=-1), axis=-1)[..., :-1].astype(v.dtype)
    out = jnp.einsum('bnkgqs,bnskd->bnqkgd', p, vv)
    return out.reshape(b, s, SWA_HEADS * hd)

def first_inputs(seed: int = 0) -> dict:
    key = jax.random.key(seed)
    ks = jax.random.split(key, 17)
    f32 = jnp.float32

    def dense(k, shape, fan_in):
        return jax.random.normal(k, shape, f32) * fan_in ** -0.5

    def gain(k, shape):
        return 1.0 + 0.05 * jax.random.normal(k, shape, f32)

    return {
        "x": jax.random.normal(ks[0], (BATCH, SEQ, D_MODEL), f32),
        "attn_norm": gain(ks[1], (DEPTH, D_MODEL)),
        "w_in": dense(ks[2], (DEPTH, D_MODEL, D_IN), D_MODEL),
        "mla_q_norm": gain(ks[3], (DEPTH, MLA_Q_RANK)),
        "w_uq": dense(ks[4], (DEPTH, MLA_Q_RANK, MLA_HEADS * (MLA_NOPE + MLA_ROPE)), MLA_Q_RANK),
        "mla_kv_norm": gain(ks[5], (DEPTH, MLA_KV_RANK)),
        "w_ukv": dense(ks[6], (DEPTH, MLA_KV_RANK, MLA_HEADS * (MLA_NOPE + MLA_V)), MLA_KV_RANK),
        "conv_w": dense(ks[7], (DEPTH, CONV_WIDTH, CONV_CH), CONV_WIDTH),
        "pool_w": dense(ks[8], (DEPTH, POOL_GROUPS, POOL_CH, POOL_CH), POOL_CH),
        "pool_scale": gain(ks[9], (DEPTH, D_GROUP)),
        "swa_sinks": 0.5 * jax.random.normal(ks[10], (DEPTH, SWA_HEADS), f32),
        "mix_norm": gain(ks[11], (DEPTH, D_MIX)),
        "w_o": dense(ks[12], (DEPTH, D_MIX, D_MODEL), D_MIX),
        "ffn_norm": gain(ks[13], (DEPTH, D_MODEL)),
        "w_gate_up": dense(ks[14], (DEPTH, D_MODEL, 2 * D_FF), D_MODEL),
        "w_down": dense(ks[15], (DEPTH, D_FF, D_MODEL), D_FF),
        "final_norm": gain(ks[16], (D_MODEL,)),
    }

def first_block(x, attn_norm, w_in, mla_q_norm, w_uq, mla_kv_norm, w_ukv, conv_w, pool_w,
              pool_scale, swa_sinks, mix_norm, w_o, ffn_norm, w_gate_up, w_down, final_norm):
    b, s, _ = x.shape
    cos, sin = rope_tables(s, MLA_ROPE, x.dtype)
    slopes = _alibi_slopes(SWA_HEADS)
    pts = _split_points()
    for l in range(DEPTH):
        h = rmsnorm(x, attn_norm[l])
        proj = h @ w_in[l]
        (c_q, c_kv, k_r, g_b, g_c, u_conv, u_pool,
         q_sw, k_sw, v_sw) = jnp.split(proj, pts, axis=-1)
        y_a = mla_attention(c_q, c_kv, k_r, mla_q_norm[l], mla_kv_norm[l],
                            w_uq[l], w_ukv[l], cos, sin)
        y_b = short_gated_conv(g_b, g_c, u_conv, conv_w[l])
        y_c = multiscale_pool(u_pool, pool_w[l], pool_scale[l])
        y_d = swa_sink_attention(q_sw.reshape(b, s, SWA_HEADS, SWA_HEAD_DIM),
                                 k_sw.reshape(b, s, SWA_KV_HEADS, SWA_HEAD_DIM),
                                 v_sw.reshape(b, s, SWA_KV_HEADS, SWA_HEAD_DIM),
                                 swa_sinks[l], slopes)
        groups = jnp.stack([y_a, y_b, y_c, y_d], axis=2)
        gf = groups.astype(jnp.float32)
        gf = gf * lax.rsqrt(jnp.mean(gf * gf, axis=-1, keepdims=True) + RMS_EPS)
        mixed = (gf.reshape(b, s, D_MIX) * mix_norm[l].astype(jnp.float32)).astype(x.dtype)
        x = x + mixed @ w_o[l]
        h2 = rmsnorm(x, ffn_norm[l])
        gate, up = jnp.split(h2 @ w_gate_up[l], 2, axis=-1)
        x = x + (jax.nn.silu(gate) * up) @ w_down[l]
    return rmsnorm(x, final_norm)


CHUNK = 64

SSD_HEAD_DIM = 64
SSD_WIDTH = D_MODEL // 2
SSD_HEADS = SSD_WIDTH // SSD_HEAD_DIM
SSD_GROUPS = 2
SSD_HPG = SSD_HEADS // SSD_GROUPS
SSD_STATE = 64
SSD_CONV = 4
SSD_XBC = SSD_WIDTH + 2 * SSD_GROUPS * SSD_STATE

RWKV_HEAD_DIM = 64
RWKV_WIDTH = D_MODEL // 4
RWKV_HEADS = RWKV_WIDTH // RWKV_HEAD_DIM
RWKV_DECAY_RANK = 32
RWKV_ICLR_RANK = 32
RWKV_GATE_RANK = 64
RWKV_SPLITS = [RWKV_WIDTH, RWKV_WIDTH, RWKV_WIDTH, RWKV_DECAY_RANK, RWKV_ICLR_RANK, RWKV_GATE_RANK]
RWKV_IN = sum(RWKV_SPLITS)
RWKV_GN_EPS = 64e-5

GLA_VALUE_DIM = 64
GLA_WIDTH = D_MODEL // 4
GLA_HEADS = GLA_WIDTH // GLA_VALUE_DIM
GLA_KEY_DIM = GLA_VALUE_DIM // 2
GLA_QK_WIDTH = GLA_HEADS * GLA_KEY_DIM
GLA_GATE_RANK = 16
GLA_GATE_TEMP = 16.0

MIX_WIDTH = SSD_WIDTH + RWKV_WIDTH + GLA_WIDTH
IN_SPLITS_2 = [SSD_WIDTH, SSD_XBC, SSD_HEADS, RWKV_IN, GLA_QK_WIDTH, GLA_QK_WIDTH, GLA_WIDTH, GLA_WIDTH, GLA_GATE_RANK]
N_IN = sum(IN_SPLITS_2)

N_GROUPS = 4
EXPERTS_PER_GROUP = 8
N_EXPERTS = N_GROUPS * EXPERTS_PER_GROUP
TOP_K = 2
EXPERT_FF = 512
ROW_BLOCK = 256

DEEPNORM_ALPHA = (2 * DEPTH) ** 0.25
DEEPNORM_BETA = (8 * DEPTH) ** -0.25
LN_EPS = 1e-5


F32 = jnp.float32

def _split(t, sizes):
    idx = [int(i) for i in np.cumsum(sizes)[:-1]]
    return jnp.split(t, idx, axis=-1)

def layer_norm(x, g, b):
    xf = x.astype(F32)
    mu = jnp.mean(xf, -1, keepdims=True)
    var = jnp.mean(jnp.square(xf - mu), -1, keepdims=True)
    return ((xf - mu) * lax.rsqrt(var + LN_EPS) * g + b).astype(x.dtype)

def causal_depthwise_conv(x, w, b):
    k, c = w.shape
    y = lax.conv_general_dilated(x, w[:, None, :], window_strides=(1,), padding=[(k - 1, 0)],
                                 dimension_numbers=('NWC', 'WIO', 'NWC'), feature_group_count=c)
    return y + b

def ssd_chunked_scan(x, a_dt, bm, cm):
    bsz, seq = x.shape[0], x.shape[1]
    nc = seq // CHUNK
    x = x.reshape(bsz, nc, CHUNK, *x.shape[2:])
    a_dt = a_dt.reshape(bsz, nc, CHUNK, *a_dt.shape[2:])
    bm = bm.reshape(bsz, nc, CHUNK, *bm.shape[2:])
    cm = cm.reshape(bsz, nc, CHUNK, *cm.shape[2:])
    a_cs = jnp.cumsum(a_dt, axis=2)
    mask = jnp.tril(jnp.ones((CHUNK, CHUNK), bool))[:, :, None, None]
    seg = jnp.exp(jnp.where(mask, a_cs[:, :, :, None] - a_cs[:, :, None, :], -jnp.inf))
    cb = jnp.einsum('bclgn,bcsgn->bclsg', cm, bm)
    y_diag = jnp.einsum('bclsgh,bcsghp->bclghp', cb[..., None] * seg, x)
    to_end = jnp.exp(a_cs[:, :, -1:] - a_cs)
    states = jnp.einsum('bclgn,bclghp->bcghpn', bm, to_end[..., None] * x)
    chunk_decay = jnp.exp(a_cs[:, :, -1])

    def step(s, inp):
        st, dec = inp
        return s * dec[..., None, None] + st, s

    s0 = jnp.zeros_like(states[:, 0])
    _, prev = lax.scan(step, s0, (jnp.moveaxis(states, 1, 0), jnp.moveaxis(chunk_decay, 1, 0)))
    prev = jnp.moveaxis(prev, 0, 1)
    y_off = jnp.einsum('bclgn,bcghpn->bclghp', cm, prev) * jnp.exp(a_cs)[..., None]
    return (y_diag + y_off).reshape(bsz, seq, *x.shape[3:])

def ssd_mixer(z, xbc, dt_raw, conv_w, conv_b, dt_bias, a_log, d_skip, norm_g):
    bsz, seq, _ = xbc.shape
    xbc = jax.nn.silu(causal_depthwise_conv(xbc, conv_w, conv_b))
    xh, bm, cm = _split(xbc, [SSD_WIDTH, SSD_GROUPS * SSD_STATE, SSD_GROUPS * SSD_STATE])
    xh = xh.astype(F32).reshape(bsz, seq, SSD_GROUPS, SSD_HPG, SSD_HEAD_DIM)
    bm = bm.astype(F32).reshape(bsz, seq, SSD_GROUPS, SSD_STATE)
    cm = cm.astype(F32).reshape(bsz, seq, SSD_GROUPS, SSD_STATE)
    dt = jax.nn.softplus((dt_raw + dt_bias).astype(F32)).reshape(bsz, seq, SSD_GROUPS, SSD_HPG)
    a = -jnp.exp(a_log.astype(F32)).reshape(SSD_GROUPS, SSD_HPG)
    y = ssd_chunked_scan(xh * dt[..., None], dt * a, bm, cm)
    y = y + d_skip.astype(F32).reshape(SSD_GROUPS, SSD_HPG)[:, :, None] * xh
    y = y.reshape(bsz, seq, SSD_WIDTH) * jax.nn.silu(z.astype(F32))
    y = y.reshape(bsz, seq, SSD_GROUPS, SSD_WIDTH // SSD_GROUPS)
    y = y * lax.rsqrt(jnp.mean(y * y, -1, keepdims=True) + RMS_EPS)
    return y.reshape(bsz, seq, SSD_WIDTH) * norm_g

def rwkv7_mixer(p, mu, w0, w2, a0, a2, g2, k_k, k_a, r_k, ln_g, ln_b):
    bsz, seq, _ = p.shape
    prev = jnp.pad(p, ((0, 0), (1, 0), (0, 0)))[:, :seq]
    p = p + (prev - p) * mu
    r, k, v, w_lr, a_lr, g_lr = _split(p, RWKV_SPLITS)
    w = -jax.nn.softplus(-(w0 + jnp.tanh(w_lr) @ w2).astype(F32)) - 0.5
    decay = jnp.exp(-jnp.exp(w))
    a = jax.nn.sigmoid((a0 + a_lr @ a2).astype(F32))
    g = (jax.nn.sigmoid(g_lr) @ g2).astype(F32)

    def heads(t):
        return t.astype(F32).reshape(bsz, seq, RWKV_HEADS, RWKV_HEAD_DIM)

    r, k, v, decay, a = heads(r), heads(k), heads(v), heads(decay), heads(a)
    kk = k * k_k.astype(F32).reshape(RWKV_HEADS, RWKV_HEAD_DIM)
    kk = kk * lax.rsqrt(jnp.sum(kk * kk, -1, keepdims=True) + 1e-12)
    k = k * (1.0 + (a - 1.0) * k_a.astype(F32).reshape(RWKV_HEADS, RWKV_HEAD_DIM))

    def step(state, inp):
        r_t, w_t, k_t, v_t, kk_t, a_t = inp
        sa = jnp.einsum('bhvk,bhk->bhv', state, -kk_t)
        state = (state * w_t[:, :, None, :] + sa[..., None] * (kk_t * a_t)[:, :, None, :]
                 + v_t[..., None] * k_t[:, :, None, :])
        return state, jnp.einsum('bhvk,bhk->bhv', state, r_t)

    s0 = jnp.zeros((bsz, RWKV_HEADS, RWKV_HEAD_DIM, RWKV_HEAD_DIM), F32)
    tm = lambda t: jnp.moveaxis(t, 1, 0)
    _, y = lax.scan(step, s0, (tm(r), tm(decay), tm(k), tm(v), tm(kk), tm(a)))
    y = jnp.moveaxis(y, 0, 1)
    mean = jnp.mean(y, -1, keepdims=True)
    var = jnp.mean(jnp.square(y - mean), -1, keepdims=True)
    y = ((y - mean) * lax.rsqrt(var + RWKV_GN_EPS)).reshape(bsz, seq, RWKV_WIDTH) * ln_g + ln_b
    bonus = jnp.sum(r * k * r_k.astype(F32), -1, keepdims=True) * v
    return (y + bonus.reshape(bsz, seq, RWKV_WIDTH)) * g

def gla_mixer(q, k, v, g, a_lr, w_a2, b_a, norm_g):
    bsz, seq, _ = q.shape
    nc = seq // CHUNK
    log_a = jax.nn.log_sigmoid((a_lr @ w_a2 + b_a).astype(F32)) / GLA_GATE_TEMP

    def chunks(t, d):
        return jnp.moveaxis(t.astype(F32).reshape(bsz, nc, CHUNK, GLA_HEADS, d), 1, 0)

    qc = chunks(q, GLA_KEY_DIM) * (GLA_KEY_DIM ** -0.5)
    kc = chunks(k, GLA_KEY_DIM)
    vc = chunks(v, GLA_VALUE_DIM)
    lac = chunks(log_a, GLA_KEY_DIM)
    mask = jnp.tril(jnp.ones((CHUNK, CHUNK), bool))[None, :, :, None, None]

    def step(state, inp):
        q_c, k_c, v_c, la_c = inp
        cum = jnp.cumsum(la_c, axis=1)
        o_inter = jnp.einsum('bihd,bhde->bihe', q_c * jnp.exp(cum), state)
        rel = jnp.exp(jnp.where(mask, cum[:, :, None] - cum[:, None, :], -jnp.inf))
        scores = jnp.einsum('bijhd,bjhd->bhij', q_c[:, :, None] * rel, k_c)
        o_intra = jnp.einsum('bhij,bjhe->bihe', scores, v_c)
        last = cum[:, -1]
        k_dec = k_c * jnp.exp(last[:, None] - cum)
        state = state * jnp.exp(last)[..., None] + jnp.einsum('bjhd,bjhe->bhde', k_dec, v_c)
        return state, o_inter + o_intra

    s0 = jnp.zeros((bsz, GLA_HEADS, GLA_KEY_DIM, GLA_VALUE_DIM), F32)
    _, o = lax.scan(step, s0, (qc, kc, vc, lac))
    o = jnp.moveaxis(o, 0, 1).reshape(bsz, seq, GLA_HEADS, GLA_VALUE_DIM)
    o = o * lax.rsqrt(jnp.mean(o * o, -1, keepdims=True) + RMS_EPS)
    return o.reshape(bsz, seq, GLA_WIDTH) * norm_g * jax.nn.silu(g.astype(F32))

def hybrid_mixer(x, w_in, ssd_conv_w, ssd_conv_b, ssd_dt_bias, ssd_a_log, ssd_d, ssd_norm_g,
                 rwkv_mu, rwkv_w0, rwkv_w2, rwkv_a0, rwkv_a2, rwkv_g2, rwkv_k_k, rwkv_k_a, rwkv_r_k,
                 rwkv_ln_g, rwkv_ln_b, gla_w_a2, gla_b_a, gla_norm_g, w_out):
    p = x @ w_in
    s_z, s_xbc, s_dt, rw, gq, gk, gv, gg, ga = _split(p, IN_SPLITS_2)
    y_ssd = ssd_mixer(s_z, s_xbc, s_dt, ssd_conv_w, ssd_conv_b, ssd_dt_bias, ssd_a_log, ssd_d, ssd_norm_g)
    y_rwkv = rwkv7_mixer(rw, rwkv_mu, rwkv_w0, rwkv_w2, rwkv_a0, rwkv_a2, rwkv_g2, rwkv_k_k, rwkv_k_a,
                         rwkv_r_k, rwkv_ln_g, rwkv_ln_b)
    y_gla = gla_mixer(gq, gk, gv, gg, ga, gla_w_a2, gla_b_a, gla_norm_g)
    y = jnp.concatenate([y_ssd, y_rwkv, y_gla], axis=-1).astype(x.dtype)
    return y @ w_out

def grouped_expert_mlp(xt, expert_id, gate, w_gate, w_up, w_down):
    n_tok, d = xt.shape
    n_assign = expert_id.size
    e_flat = expert_id.reshape(-1)
    order = jnp.argsort(e_flat)
    e_sorted = e_flat[order]
    counts = jnp.bincount(e_flat, length=N_EXPERTS)
    padded = (counts + ROW_BLOCK - 1) // ROW_BLOCK * ROW_BLOCK
    pad_end = jnp.cumsum(padded)
    pad_start = pad_end - padded
    start = jnp.cumsum(counts) - counts
    dest = pad_start[e_sorted] + jnp.arange(n_assign, dtype=jnp.int32) - start[e_sorted]
    n_blocks = -(-n_assign // ROW_BLOCK) + N_EXPERTS
    n_rows = n_blocks * ROW_BLOCK
    row_tok = jnp.full((n_rows,), n_tok, jnp.int32).at[dest].set((order // TOP_K).astype(jnp.int32))
    row_gate = jnp.zeros((n_rows,), xt.dtype).at[dest].set(gate.reshape(-1)[order].astype(xt.dtype))
    block_start = jnp.arange(n_blocks, dtype=jnp.int32) * ROW_BLOCK
    block_expert = jnp.minimum(jnp.searchsorted(pad_end, block_start, side='right'), N_EXPERTS - 1)
    x_pad = jnp.concatenate([xt, jnp.zeros((1, d), xt.dtype)], axis=0)
    xs = x_pad[row_tok].reshape(n_blocks, ROW_BLOCK, d)

    def block_mlp(args):
        xb, e = args
        h = jax.nn.silu(xb @ w_gate[e]) * (xb @ w_up[e])
        return h @ w_down[e]

    ys = lax.map(block_mlp, (xs, block_expert)).reshape(n_rows, d)
    out = jnp.zeros((n_tok + 1, d), ys.dtype).at[row_tok].add(ys * row_gate[:, None])
    return out[:n_tok]

def hierarchical_moe(x, w_rg, b_rg, w_re, b_re, w_gate, w_up, w_down):
    bsz, seq, d = x.shape
    xt = x.reshape(-1, d)
    n_tok = xt.shape[0]
    g_prob = jax.nn.softmax((xt @ w_rg + b_rg).astype(F32), axis=-1)
    g_w, g_idx = lax.top_k(g_prob, 1)
    e_logits = (xt @ w_re + b_re).astype(F32).reshape(n_tok, N_GROUPS, EXPERTS_PER_GROUP)
    e_logits = jnp.take_along_axis(e_logits, g_idx[:, :, None], axis=1)[:, 0]
    e_prob = jax.nn.softmax(e_logits, axis=-1)
    e_w, e_local = lax.top_k(e_prob, TOP_K)
    e_w = e_w / jnp.sum(e_w, -1, keepdims=True)
    gate = g_w * e_w
    expert_id = g_idx * EXPERTS_PER_GROUP + e_local
    y = grouped_expert_mlp(xt, expert_id, gate, w_gate, w_up, w_down)
    return y.reshape(bsz, seq, d).astype(x.dtype)

def second_inputs(seed: int = 0) -> dict:
    key = jax.random.key(seed)
    ks = iter(jax.random.split(key, 48))
    L = DEPTH

    def nrm(shape, scale):
        return scale * jax.random.normal(next(ks), shape, F32)

    def gain(shape):
        return 1.0 + nrm(shape, 0.02)

    x = nrm((BATCH, SEQ, D_MODEL), 1.0)
    ln_in_g = gain((D_MODEL,))
    ln_in_b = nrm((D_MODEL,), 0.02)
    w_in = nrm((L, D_MODEL, N_IN), D_MODEL ** -0.5)
    ssd_conv_w = nrm((L, SSD_CONV, SSD_XBC), SSD_CONV ** -0.5)
    ssd_conv_b = nrm((L, SSD_XBC), 0.02)
    dt = jnp.exp(jax.random.uniform(next(ks), (L, SSD_HEADS), F32, math.log(1e-3), math.log(1e-1)))
    ssd_dt_bias = dt + jnp.log(-jnp.expm1(-dt))
    ssd_a_log = jnp.log(jax.random.uniform(next(ks), (L, SSD_HEADS), F32, 1.0, 16.0))
    ssd_d = 1.0 + nrm((L, SSD_HEADS), 0.1)
    ssd_norm_g = gain((L, SSD_WIDTH))
    rwkv_mu = jax.random.uniform(next(ks), (L, RWKV_IN), F32)
    rwkv_w0 = jnp.linspace(-6.5, -1.5, RWKV_WIDTH, dtype=F32)[None, :] + nrm((L, RWKV_WIDTH), 0.1)
    rwkv_w2 = nrm((L, RWKV_DECAY_RANK, RWKV_WIDTH), 0.1)
    rwkv_a0 = nrm((L, RWKV_WIDTH), 0.1)
    rwkv_a2 = nrm((L, RWKV_ICLR_RANK, RWKV_WIDTH), 0.1)
    rwkv_g2 = nrm((L, RWKV_GATE_RANK, RWKV_WIDTH), RWKV_GATE_RANK ** -0.5)
    rwkv_k_k = 1.0 + nrm((L, RWKV_WIDTH), 0.1)
    rwkv_k_a = 1.0 + nrm((L, RWKV_WIDTH), 0.1)
    rwkv_r_k = nrm((L, RWKV_HEADS, RWKV_HEAD_DIM), 0.1)
    rwkv_ln_g = gain((L, RWKV_WIDTH))
    rwkv_ln_b = nrm((L, RWKV_WIDTH), 0.02)
    gla_w_a2 = nrm((L, GLA_GATE_RANK, GLA_QK_WIDTH), GLA_GATE_RANK ** -0.5)
    gla_b_a = nrm((L, GLA_QK_WIDTH), 0.1)
    gla_norm_g = gain((L, GLA_WIDTH))
    w_out = nrm((L, MIX_WIDTH, D_MODEL), DEEPNORM_BETA * MIX_WIDTH ** -0.5)
    ln1_g = gain((L, D_MODEL))
    ln1_b = nrm((L, D_MODEL), 0.02)
    moe_w_rg = nrm((L, D_MODEL, N_GROUPS), D_MODEL ** -0.5)
    moe_b_rg = nrm((L, N_GROUPS), 0.01)
    moe_w_re = nrm((L, D_MODEL, N_EXPERTS), D_MODEL ** -0.5)
    moe_b_re = nrm((L, N_EXPERTS), 0.01)
    moe_w_gate = nrm((L, N_EXPERTS, D_MODEL, EXPERT_FF), D_MODEL ** -0.5)
    moe_w_up = nrm((L, N_EXPERTS, D_MODEL, EXPERT_FF), D_MODEL ** -0.5)
    moe_w_down = nrm((L, N_EXPERTS, EXPERT_FF, D_MODEL), DEEPNORM_BETA * EXPERT_FF ** -0.5)
    ln2_g = gain((L, D_MODEL))
    ln2_b = nrm((L, D_MODEL), 0.02)
    return {'x': x, 'ln_in_g': ln_in_g, 'ln_in_b': ln_in_b, 'w_in': w_in,
            'ssd_conv_w': ssd_conv_w, 'ssd_conv_b': ssd_conv_b, 'ssd_dt_bias': ssd_dt_bias,
            'ssd_a_log': ssd_a_log, 'ssd_d': ssd_d, 'ssd_norm_g': ssd_norm_g,
            'rwkv_mu': rwkv_mu, 'rwkv_w0': rwkv_w0, 'rwkv_w2': rwkv_w2, 'rwkv_a0': rwkv_a0,
            'rwkv_a2': rwkv_a2, 'rwkv_g2': rwkv_g2, 'rwkv_k_k': rwkv_k_k, 'rwkv_k_a': rwkv_k_a,
            'rwkv_r_k': rwkv_r_k, 'rwkv_ln_g': rwkv_ln_g, 'rwkv_ln_b': rwkv_ln_b,
            'gla_w_a2': gla_w_a2, 'gla_b_a': gla_b_a, 'gla_norm_g': gla_norm_g,
            'w_out': w_out, 'ln1_g': ln1_g, 'ln1_b': ln1_b,
            'moe_w_rg': moe_w_rg, 'moe_b_rg': moe_b_rg, 'moe_w_re': moe_w_re, 'moe_b_re': moe_b_re,
            'moe_w_gate': moe_w_gate, 'moe_w_up': moe_w_up, 'moe_w_down': moe_w_down,
            'ln2_g': ln2_g, 'ln2_b': ln2_b}

def second_block(x, ln_in_g, ln_in_b, w_in, ssd_conv_w, ssd_conv_b, ssd_dt_bias, ssd_a_log, ssd_d,
              ssd_norm_g, rwkv_mu, rwkv_w0, rwkv_w2, rwkv_a0, rwkv_a2, rwkv_g2, rwkv_k_k, rwkv_k_a,
              rwkv_r_k, rwkv_ln_g, rwkv_ln_b, gla_w_a2, gla_b_a, gla_norm_g, w_out, ln1_g, ln1_b,
              moe_w_rg, moe_b_rg, moe_w_re, moe_b_re, moe_w_gate, moe_w_up, moe_w_down, ln2_g, ln2_b):
    h = layer_norm(x, ln_in_g, ln_in_b)
    for i in range(DEPTH):
        mix = hybrid_mixer(h, w_in[i], ssd_conv_w[i], ssd_conv_b[i], ssd_dt_bias[i], ssd_a_log[i],
                           ssd_d[i], ssd_norm_g[i], rwkv_mu[i], rwkv_w0[i], rwkv_w2[i], rwkv_a0[i],
                           rwkv_a2[i], rwkv_g2[i], rwkv_k_k[i], rwkv_k_a[i], rwkv_r_k[i], rwkv_ln_g[i],
                           rwkv_ln_b[i], gla_w_a2[i], gla_b_a[i], gla_norm_g[i], w_out[i])
        h = layer_norm(DEEPNORM_ALPHA * h + mix, ln1_g[i], ln1_b[i])
        ffn = hierarchical_moe(h, moe_w_rg[i], moe_b_rg[i], moe_w_re[i], moe_b_re[i],
                               moe_w_gate[i], moe_w_up[i], moe_w_down[i])
        h = layer_norm(DEEPNORM_ALPHA * h + ffn, ln2_g[i], ln2_b[i])
    return h


def setup_inputs(seed=0):
    out = dict(first_inputs(seed))
    for name, value in second_inputs(seed + 1).items():
        if name != "x":
            out[name + "_2"] = value
    return out


def reference(
    x, attn_norm, w_in, mla_q_norm, w_uq, mla_kv_norm, w_ukv, conv_w, pool_w, pool_scale,
    swa_sinks, mix_norm, w_o, ffn_norm, w_gate_up, w_down, final_norm, ln_in_g_2, ln_in_b_2,
    w_in_2, ssd_conv_w_2, ssd_conv_b_2, ssd_dt_bias_2, ssd_a_log_2, ssd_d_2, ssd_norm_g_2,
    rwkv_mu_2, rwkv_w0_2, rwkv_w2_2, rwkv_a0_2, rwkv_a2_2, rwkv_g2_2, rwkv_k_k_2, rwkv_k_a_2,
    rwkv_r_k_2, rwkv_ln_g_2, rwkv_ln_b_2, gla_w_a2_2, gla_b_a_2, gla_norm_g_2, w_out_2, ln1_g_2,
    ln1_b_2, moe_w_rg_2, moe_b_rg_2, moe_w_re_2, moe_b_re_2, moe_w_gate_2, moe_w_up_2,
    moe_w_down_2, ln2_g_2, ln2_b_2,
):
    x = first_block(
        x, attn_norm, w_in, mla_q_norm, w_uq, mla_kv_norm, w_ukv, conv_w, pool_w, pool_scale,
        swa_sinks, mix_norm, w_o, ffn_norm, w_gate_up, w_down, final_norm,
    )
    return second_block(
        x, ln_in_g_2, ln_in_b_2, w_in_2, ssd_conv_w_2, ssd_conv_b_2, ssd_dt_bias_2, ssd_a_log_2,
        ssd_d_2, ssd_norm_g_2, rwkv_mu_2, rwkv_w0_2, rwkv_w2_2, rwkv_a0_2, rwkv_a2_2, rwkv_g2_2,
        rwkv_k_k_2, rwkv_k_a_2, rwkv_r_k_2, rwkv_ln_g_2, rwkv_ln_b_2, gla_w_a2_2, gla_b_a_2,
        gla_norm_g_2, w_out_2, ln1_g_2, ln1_b_2, moe_w_rg_2, moe_b_rg_2, moe_w_re_2, moe_b_re_2,
        moe_w_gate_2, moe_w_up_2, moe_w_down_2, ln2_g_2, ln2_b_2,
    )


_drawn_inputs = setup_inputs


def setup_inputs(seed=0):
    import zlib

    import numpy as np

    out = dict(_drawn_inputs(seed))
    spreads = {}
    factors = {'ssd_conv_b_2': 4.088,
     'ssd_norm_g_2': 4.958,
     'rwkv_w2_2': 4.193,
     'rwkv_a0_2': 4.867,
     'rwkv_ln_g_2': 22.036,
     'rwkv_ln_b_2': 8.0,
     'gla_b_a_2': 5.821,
     'gla_norm_g_2': 8.0,
     'moe_b_rg_2': 22.44,
     'moe_b_re_2': 5.044}
    for name, (base, spread) in spreads.items():
        noise = np.random.default_rng([zlib.crc32(name.encode()), seed]).standard_normal(out[name].shape)
        drawn = base * np.exp(spread * noise) if base else spread * noise
        out[name] = jnp.asarray(drawn.astype(out[name].dtype))
    for name, factor in factors.items():
        out[name] = (out[name] * factor).astype(out[name].dtype)
    return out
```

```python
from contextlib import ExitStack

import numpy as np

import concourse.bass as bass
from concourse import mybir

F32 = mybir.dt.float32
BF16 = mybir.dt.bfloat16
ALU = mybir.AluOpType
ACT = mybir.ActivationFunctionType
AX = mybir.AxisListType

P = 128
D = 1024
S = 256
DT = D // P
SB = S // P
DEPTH = 2
RMS_EPS = 1e-6
LN_EPS = 1e-5
NEG = -1.0e30

HEADS = 4
NOPE, ROPE, HD = 64, 32, 64
MLA_SCALE = float(1.0 / np.sqrt(NOPE + ROPE))
SWA_SCALE = float(1.0 / np.sqrt(HD))
SWA_WINDOW = 128
D_FF = 2816
FT = D_FF // P
IN1_WIDTHS = [128] * 3 + [64] + [128] * 11 + [128]
IN1_OFF = [sum(IN1_WIDTHS[:i]) for i in range(len(IN1_WIDTHS))]
IN1_COLS = sum(IN1_WIDTHS)
T_CQ, T_CKV, T_KR, T_GB, T_GC, T_UC, T_UP, T_QS, T_KS = 0, 2, 3, 4, 6, 8, 10, 12, 14
N_IN1_TILES = 15

V1 = dict(attn_norm=(0, 8), q_norm=(8, 2), kv_norm=(10, 1), conv_w=(11, 6), pool_scale=(17, 2),
          mix_norm=(19, 8), ffn_norm=(27, 8), sinks=(35, 4))
N_V1 = 39

C = 32
NCH = S // C
CPB = P // C
IN2_TILES = 21
N_GA = 16
N_TOKM = 8 + 256
IN2_COLS = IN2_TILES * P + N_GA + N_TOKM
N_GROUPS, EPG, N_EXP, EFF = 4, 8, 32, 512
N_ROUTE = N_GROUPS + N_EXP
SLOTS = 64
N_OVER = 2 * S // SLOTS
N_PASS = N_EXP + N_OVER
I32 = mybir.dt.int32
ALPHA = float((2 * DEPTH) ** 0.25)
V2 = dict(conv_w=(0, 24), conv_b=(24, 6), dt_bias=(30, 8), a_log=(38, 8), ssd_d=(46, 4), ssd_norm=(50, 4),
          mu=(54, 7), w0=(61, 2), a0=(63, 2), k_k=(65, 2), k_a=(67, 2), r_k=(69, 2), ln_g=(71, 2), ln_b=(73, 2),
          b_a=(75, 1), gla_norm=(76, 2), ln1_g=(78, 8), ln1_b=(86, 8), ln2_g=(94, 8), ln2_b=(102, 8),
          b_route=(110, 36))
N_V2 = 146

CONST = {}


def const_pack():
    r, c = np.arange(P)[:, None], np.arange(P)[None, :]
    same = r // C == c // C
    inv = (1.0 / (np.float32(10000.0) ** (np.arange(0, ROPE, 2, dtype=np.float32) / np.float32(ROPE))))
    ang = np.arange(S, dtype=np.float32)[None, :] * inv.astype(np.float32)[:, None]
    cos, sin = np.cos(ang).astype(np.float32), np.sin(ang).astype(np.float32)
    rope = np.zeros((P, S), np.float32)
    rope[64:96] = np.concatenate([cos, cos])
    rope[96:128] = np.concatenate([-sin, sin])
    q, k = np.arange(P)[:, None] + P, np.arange(2 * P)[None, :]
    dist = q - k
    slopes = [2.0 ** (-8.0 * (i + 1) / HEADS) for i in range(HEADS)]
    swa = [np.where((dist >= 0) & (dist < SWA_WINDOW), -s * dist, NEG) for s in slopes]
    mla = np.where(dist >= 0, 0.0, NEG)
    t = np.arange(S) + 1
    invc = np.stack([np.concatenate([np.tile(1.0 / np.minimum(t, w), (64, 1)) for w in ws])
                     for ws in ((2, 4), (8, 16))], 1)
    gla_heads = (np.arange(P)[:, None] // 32 == np.arange(256)[None, :] // 64)
    parts = [("ident", r == c), ("ones", np.ones((P, P))), ("ones64", r // 64 == c // 64),
             ("le3", np.concatenate([r <= c, np.ones((P, P)), r <= c], 1)), ("lt", r < c), ("gt", r > c), ("cu_incl", same & (r <= c)), ("cu_strict", same & (r < c)),
             ("cl_strict", same & (r > c)), ("rope", rope), ("mla", mla), ("swa", np.concatenate(swa, 1)),
             ("invc", invc.reshape(P, 2 * S)), ("keep", np.tile((np.arange(2 * S) % C != 0), (P, 1))),
             ("gla_heads", gla_heads), ("rank", np.tile(64.0 - np.arange(64.0), (P, 1))), ("slots", np.tile(np.arange(P) % SLOTS, (P, 1))),
             ("steps", np.tile(np.repeat(np.arange(N_OVER), N_EXP), (P, 1))),
             ("experts", np.tile(np.arange(N_OVER * N_EXP) % N_EXP, (P, 1)))]
    at = 0
    for name, m in parts:
        CONST[name] = (at, m.shape[1])
        at += m.shape[1]
    return np.ascontiguousarray(np.concatenate([np.asarray(m, np.float32) for _, m in parts], 1))


CONST_ARRAY = const_pack()
N_CONST = CONST_ARRAY.shape[1]


class Chain:

    def __init__(self, eng, sem):
        self.eng, self.sem, self.n = eng, sem, 0

    def link(self, ins):
        self.n += 1
        ins.then_inc(self.sem, 1)
        self.eng.wait_ge(self.sem, self.n)


class Stage:

    def __init__(self, nc, name):
        self.nc, self.name, self.ctx, self.sems = nc, name, ExitStack(), []

    def __enter__(self):
        return self

    def __exit__(self, *a):
        for s in self.sems:
            self.nc.sync.sem_clear(s)
        self.ctx.close()

    def sem(self, name):
        s = self.ctx.enter_context(self.nc.semaphore(f"{self.name}_{name}"))
        self.sems.append(s)
        return s

    def sb(self, name, shape, dt=F32):
        return self.ctx.enter_context(self.nc.sbuf_tensor(f"{self.name}_{name}", shape, dt))

    def ps(self, name, shape, dt=F32):
        return self.ctx.enter_context(self.nc.psum_tensor(f"{self.name}_{name}", shape, dt))


def bc(ap, n, axis):
    ap = ap.unsqueeze(axis)
    return ap.broadcast_to([n if i == axis else d for i, d in enumerate(ap.shape)])


def norm_engines(k, st, x, out, gain, eps, bias=None, tag="n"):
    sq = st.sb(tag + "_sq", [P, DT, S])
    lnv = st.sb(tag + "_lnv", [P, S])
    rstd = st.sb(tag + "_rstd", [P, S])
    mean = st.sb(tag + "_mean", [P, S])
    psum = st.ps(tag + "_ps", [P, 2, 512])
    squares = st.sem(tag + "_squares")
    sums = st.sem(tag + "_sums")
    mean_ready = st.sem(tag + "_mean_ready")
    rstd_ready = st.sem(tag + "_rstd_ready")
    ln_done = st.sem(tag + "_ln_done")
    normed = st.sem(tag + "_normed")
    ln = bias is not None
    src = out if ln else x
    extra = 1 if ln else 0

    def vector(dve, ch):
        if ln:
            dve.wait_ge(sums, 1)
            ch.link(dve.tensor_scalar(mean[:], psum[:, 0, 0:S], 1.0 / D, None, ALU.mult))
            ch.link(dve.tensor_tensor(out[:], x[:], bc(mean[:], DT, 1), ALU.subtract))
        dve.tensor_tensor(sq[:], src[:], src[:], ALU.mult).then_inc(squares, 1)
        dve.wait_ge(rstd_ready, 1)
        for t in range(DT):
            ins = dve.scalar_tensor_tensor(out[:, t], src[:, t], gain[:, t:t + 1], rstd[:], ALU.mult, ALU.mult)
            if ln:
                ch.link(ins)
                ins = dve.tensor_scalar(out[:, t], out[:, t], bias[:, t:t + 1], None, ALU.add)
            ins.then_inc(normed, 1)

    def scalar(act):
        act.wait_ge(sums, 1 + extra)
        act.activation(lnv[:], psum[:, 1, 0:S], ACT.Ln, bias=k.eps[eps], scale=1.0 / D).then_inc(ln_done, 1)
        act.wait_ge(ln_done, 1)
        act.activation(rstd[:], lnv[:], ACT.Exp, scale=-0.5).then_inc(rstd_ready, 1)

    def tensor(pe):
        if ln:
            for t in range(DT):
                ins = pe.matmul(psum[:, 0, 0:S], k.c("ones"), x[:, t], start=t == 0, stop=t == DT - 1)
            ins.then_inc(sums, 1)
        pe.wait_ge(squares, 1)
        for t in range(DT):
            ins = pe.matmul(psum[:, 1, 0:S], k.c("ones"), sq[:, t], start=t == 0, stop=t == DT - 1)
        ins.then_inc(sums, 1)

    return vector, scalar, tensor, normed


class Kit:

    def __init__(self, nc, ctx):
        self.nc = nc
        self.x = ctx.enter_context(nc.sbuf_tensor("x_resid", [P, DT, S], F32))
        self.const = ctx.enter_context(nc.sbuf_tensor("const", [P, N_CONST], F32))
        self.eps_sb = ctx.enter_context(nc.sbuf_tensor("eps_sb", [P, 5], F32))
        self.eps = {RMS_EPS: self.eps_sb[:, 0:1], LN_EPS: self.eps_sb[:, 1:2], 64e-5: self.eps_sb[:, 2:3],
                    1e-12: self.eps_sb[:, 3:4], 1.0: self.eps_sb[:, 4:5]}

    def c(self, name):
        at, n = CONST[name]
        return self.const[:, at:at + n]


def stage_load(nc, k, x_in, const_in):
    with Stage(nc, "load") as st:
        loaded = st.sem("loaded")
        eps_set = st.sem("eps_set")
        with nc.Block() as block:

            @block.sync
            def _(sp):
                sp.dma_start(k.x[:], x_in.rearrange("p (t s) -> p t s", t=DT)).then_inc(loaded, 16)
                sp.dma_start(k.const[:], const_in).then_inc(loaded, 16)
                sp.wait_ge(loaded, 32)

            @block.vector
            def _(dve):
                for i, e in enumerate((RMS_EPS, LN_EPS, 64e-5, 1e-12, 1.0)):
                    dve.memset(k.eps_sb[:, i:i + 1], e).then_inc(eps_set, 1)
                dve.wait_ge(eps_set, 5)


def stage_project1(nc, k, L, w_dram, v_dram, vecs, proj, vtok):
    with Stage(nc, "project1") as st:
        h = st.sb("h", [P, DT, S])
        w = st.sb("w_in", [P, DT * IN1_COLS])
        ps = st.ps("ps", [P, 4, 512])
        vec_loaded = st.sem("vec_loaded")
        w_loaded = [st.sem(f"w_loaded{i}") for i in range(8)]
        mm_done = st.sem("mm_done")
        copied = st.sem("copied")
        dve_step = st.sem("dve_step")
        n_vec, n_act, n_pe, normed = norm_engines(k, st, k.x, h, vecs[:, V1["attn_norm"][0]:], RMS_EPS)
        pairs = [(2 * j, 2 * j + 1) for j in range(7)] + [(14, None)]

        def wt(t):
            return w[:, DT * IN1_OFF[t]:DT * (IN1_OFF[t] + IN1_WIDTHS[t])].rearrange("p (k c) -> p k c", k=DT)

        with nc.Block() as block:

            @block.sync
            def _(sp):
                sp.dma_start(vecs[:], v_dram[bass.ds(L, 1)].rearrange("a p n -> (a p) n")).then_inc(vec_loaded, 16)
                for i in range(8):
                    a, b = DT * IN1_OFF[2 * i], DT * (IN1_OFF[2 * i + 1] + IN1_WIDTHS[2 * i + 1])
                    sp.dma_start(w[:, a:b], w_dram[bass.ds(L, 1), :, a:b].rearrange("a p n -> (a p) n"))\
                        .then_inc(w_loaded[i], 16)

            @block.vector
            def _(dve):
                dve.wait_ge(vec_loaded, 16)
                n_vec(dve, Chain(dve, dve_step))

            @block.scalar
            def _(act):
                n_act(act)
                for j, (a, b) in enumerate(pairs):
                    act.wait_ge(mm_done, j + 1)
                    if j == 1:
                        act.activation(proj[:, 2], ps[:, j % 4, 0:S], ACT.Copy)
                        act.activation(proj[64:128, 3], ps[64:128, j % 4, S:2 * S], ACT.Copy).then_inc(copied, 1)
                    elif b is None:
                        act.activation(proj[:, a], ps[:, j % 4, 0:S], ACT.Copy)
                        act.activation(vtok[:].rearrange("p b f -> p (b f)"), ps[:, j % 4, S:2 * S], ACT.Copy)\
                            .then_inc(copied, 1)
                    else:
                        act.activation(proj[:, a:a + 2].rearrange("p a s -> p (a s)"), ps[:, j % 4], ACT.Copy)\
                            .then_inc(copied, 1)

            @block.tensor
            def _(pe):
                n_pe(pe)
                pe.wait_ge(normed, DT)
                for j, (a, b) in enumerate(pairs):
                    pe.wait_ge(w_loaded[j], 16)
                    if j >= 4:
                        pe.wait_ge(copied, j - 3)
                    for i, t in enumerate((a, b)):
                        if t is None:
                            for blk in range(SB):
                                for kk in range(DT):
                                    ins = pe.matmul(ps[:, j % 4, S + blk * P:S + (blk + 1) * P],
                                                    h[:, kk, blk * P:(blk + 1) * P], wt(15)[:, kk],
                                                    start=kk == 0, stop=kk == DT - 1)
                            continue
                        lo = 64 if t == 3 else 0
                        for kk in range(DT):
                            ins = pe.matmul(ps[lo:P, j % 4, i * S:(i + 1) * S], wt(t)[:, kk], h[:, kk],
                                            start=kk == 0, stop=kk == DT - 1)
                    ins.then_inc(mm_done, 1)


def stage_mixers1(nc, k, L, proj, vtok, vecs, wuq_dram, wukv_dram, poolw_dram, y):
    with Stage(nc, "mixers1") as st:
        wuq = st.sb("wuq", [P, 2, HEADS, P])
        wukv = st.sb("wukv", [P, 2, 256])
        poolw = st.sb("poolw", [P, 2, 64])
        cn = st.sb("cn", [P, 3, S])
        sq = st.sb("sqc", [P, 3, S])
        lnv = st.sb("lnvc", [P, 2, S])
        rstd = st.sb("rstdc", [P, 2, S])
        qT = st.sb("qT", [P, HEADS, S])
        kT = st.sb("kT", [P, HEADS, S])
        rot = st.sb("rot", [P, HEADS, S])
        vm = st.sb("vm", [P, SB, 256])
        prob = st.sb("prob", [P, 2, HEADS, S])
        probT = st.sb("probT", [P, HEADS * SB, P])
        mx = st.sb("mx", [P, 2, HEADS])
        nmx = st.sb("nmx", [P, 2, HEADS])
        den = st.sb("den", [P, 2, HEADS])
        snk = st.sb("snk", [P, 2, HEADS])
        rden = st.sb("rden", [P, 2, HEADS])
        zc = st.sb("zc", [P, 2, S + 2])
        ct = st.sb("ct", [P, 2, S])
        up = st.sb("up", [P, 2, S + 16])
        s2 = st.sb("s2", [P, 2, S + 16])
        s4 = st.sb("s4", [P, 2, S + 16])
        s8 = st.sb("s8", [P, 2, S + 16])
        s16 = st.sb("s16", [P, 2, S + 16])
        pooled = st.sb("pooled", [P, 2, S])
        psA = st.ps("psA", [P, 4, 512])
        psT = st.ps("psT", [P, 2, 512])
        psY = st.ps("psY", [P, 512])
        psX = st.ps("psX", [P, 512])
        w_loaded = st.sem("w_loaded")
        squares = st.sem("squares")
        sums = st.sem("sums")
        ln_done = st.sem("ln_done")
        rstd_ready = st.sem("rstd_ready")
        latent_ready = st.sem("latent_ready")
        q_done = st.sem("q_done")
        k_done = st.sem("k_done")
        v_done = st.sem("v_done")
        kv_copied = st.sem("kv_copied")
        q_copied = st.sem("q_copied")
        rope_ready = st.sem("rope_ready")
        scores_done = st.sem("scores_done")
        scores_read = st.sem("scores_read")
        max_ready = st.sem("max_ready")
        exp_done = st.sem("exp_done")
        probs_ready = st.sem("probs_ready")
        transposed = st.sem("transposed")
        probT_ready = st.sem("probT_ready")
        attended = st.sem("attended")
        y_copied = st.sem("y_copied")
        pool_ready = st.sem("pool_ready")
        pool_mixed = st.sem("pool_mixed")
        dve_step = st.sem("dve_step")
        gp_step = st.sem("gp_step")
        units = [(1, 0), (1, 1), (0, 0), (0, 1)]
        vec = lambda n, i=0: vecs[:, V1[n][0] + i:V1[n][0] + i + 1]

        with nc.Block() as block:

            @block.sync
            def _(sp):
                sp.dma_start(wuq[:], wuq_dram[bass.ds(L, 1)].rearrange("a p (k h c) -> (a p) k h c", k=2, h=HEADS))\
                    .then_inc(w_loaded, 16)
                sp.dma_start(wukv[:], wukv_dram[bass.ds(L, 1)].rearrange("a p (k c) -> (a p) k c", k=2))\
                    .then_inc(w_loaded, 16)
                sp.dma_start(poolw[:], poolw_dram[bass.ds(L, 1)].rearrange("a p (k c) -> (a p) k c", k=2))\
                    .then_inc(w_loaded, 16)

            @block.gpsimd
            def _(gp):
                ch = Chain(gp, gp_step)
                gp.memset(zc[:, :, 0:2], 0.0)
                gp.memset(up[:, :, 0:16], 0.0)
                gp.memset(s2[:, :, 0:16], 0.0)
                gp.memset(s4[:, :, 0:16], 0.0)
                gp.memset(s8[:, :, 0:16], 0.0)
                ch.link(gp.tensor_tensor(zc[:, :, 2:], proj[:, T_GC:T_GC + 2], proj[:, T_UC:T_UC + 2], ALU.mult))
                ch.link(gp.tensor_copy(up[:, :, 16:], proj[:, T_UP:T_UP + 2]))
                for t in range(2):
                    yt = y[:, 2 + t]
                    ch.link(gp.tensor_scalar(yt, zc[:, t, 0:S], vec("conv_w", t), None, ALU.mult))
                    for tap in (1, 2):
                        ch.link(gp.tensor_scalar(ct[:, t], zc[:, t, tap:tap + S], vec("conv_w", 2 * tap + t), None,
                                                 ALU.mult))
                        ch.link(gp.tensor_tensor(yt, yt, ct[:, t], ALU.add))
                    ch.link(gp.tensor_tensor(yt, yt, proj[:, T_GB + t], ALU.mult))
                for a, b, w in ((up, s2, 1), (s2, s4, 2), (s4, s8, 4), (s8, s16, 8)):
                    ch.link(gp.tensor_tensor(b[:, :, 16:], a[:, :, 16:], a[:, :, 16 - w:S + 16 - w], ALU.add))
                invc = k.c("invc").rearrange("p (t s) -> p t s", t=2)
                for i, s in enumerate((s2, s4, s8, s16)):
                    rows, t = slice(64 * (i % 2), 64 * (i % 2) + 64), i // 2
                    ch.link(gp.tensor_tensor(pooled[rows, t], s[rows, t, 16:], invc[rows, t], ALU.mult))
                gp.tensor_tensor(pooled[:], pooled[:], up[:, :, 16:], ALU.subtract).then_inc(pool_ready, 1)

            @block.vector
            def _(dve):
                ch = Chain(dve, dve_step)
                dve.tensor_tensor(sq[:], proj[:, 0:3], proj[:, 0:3], ALU.mult).then_inc(squares, 1)
                dve.wait_ge(rstd_ready, 1)
                for t in range(3):
                    dve.scalar_tensor_tensor(cn[:, t], proj[:, t], vec("q_norm", t) if t < 2 else vec("kv_norm"),
                                             rstd[:, 0 if t < 2 else 1], ALU.mult, ALU.mult).then_inc(latent_ready, 1)
                cos, sin = k.c("rope")[64:96, :], k.c("rope")[96:128, :]
                dve.wait_ge(q_done, 1)
                psq = psA[:].rearrange("p b (h s) -> p (b h) s", h=2)
                ch.link(dve.tensor_tensor(rot[64:96], psq[96:128, 0:HEADS], bc(sin, HEADS, 1), ALU.mult))
                ch.link(dve.tensor_tensor(qT[64:96], psq[64:96, 0:HEADS], bc(cos, HEADS, 1), ALU.mult))
                dve.tensor_tensor(qT[64:96], qT[64:96], rot[64:96], ALU.add).then_inc(rope_ready, 1)
                dve.wait_ge(rope_ready, 1)
                ch.link(dve.tensor_tensor(rot[64:96, 0], proj[96:128, T_KR], sin, ALU.mult))
                ch.link(dve.tensor_tensor(rot[64:96, 1], proj[64:96, T_KR], cos, ALU.mult))
                dve.tensor_tensor(kT[64:96], bc(rot[64:96, 0], HEADS, 1), bc(rot[64:96, 1], HEADS, 1), ALU.add)\
                    .then_inc(rope_ready, 1)
                dve.wait_ge(pool_mixed, 1)
                for t in range(2):
                    dve.tensor_scalar(y[:, 4 + t], psX[:, t * S:(t + 1) * S], vec("pool_scale", t), None, ALU.mult)

                def soften(u):
                    mla, blk = units[u]
                    n, pr = P * (blk + 1), prob[:, u % 2]
                    if mla:
                        bias = bc(k.c("mla")[:, 2 * P - n:], HEADS, 1)
                    else:
                        bias = k.c("swa").rearrange("p (h c) -> p h c", h=HEADS)[:, :, 2 * P - n:]
                    dve.wait_ge(scores_done, u + 1)
                    sc = psA[:, 2 * (u % 2):2 * (u % 2) + 2].rearrange("p b (h c) -> p (b h) c", h=2)
                    if not mla:
                        pass
                    ins = dve.scalar_tensor_tensor(pr[:, :, 0:n], sc[:, :, 0:n], MLA_SCALE if mla else SWA_SCALE, bias,
                                                   ALU.mult, ALU.add)
                    ins.then_inc(scores_read, 1)
                    dve.wait_ge(scores_read, u + 1)
                    ch.link(dve.reduce_max(mx[:, u % 2], pr[:, :, 0:n], AX.X))
                    if not mla:
                        sinks = vecs[:, V1["sinks"][0]:V1["sinks"][0] + HEADS]
                        ch.link(dve.tensor_tensor(mx[:, u % 2], mx[:, u % 2], sinks, ALU.max))
                        ch.link(dve.tensor_tensor(snk[:, u % 2], sinks, mx[:, u % 2], ALU.subtract))
                    dve.tensor_scalar(nmx[:, u % 2], mx[:, u % 2], -1.0, None, ALU.mult).then_inc(max_ready, 1)

                def normalise(u):
                    mla, blk = units[u]
                    n, pr = P * (blk + 1), prob[:, u % 2]
                    dve.wait_ge(exp_done, u + 1)
                    if not mla:
                        ch.link(dve.tensor_tensor(den[:, u % 2], den[:, u % 2], snk[:, u % 2], ALU.add))
                    ch.link(dve.reciprocal(rden[:, u % 2], den[:, u % 2]))
                    dve.tensor_tensor(pr[:, :, 0:n], pr[:, :, 0:n], bc(rden[:, u % 2], n, 2), ALU.mult)\
                        .then_inc(probs_ready, 1)

                soften(0)
                for u in range(4):
                    if u < 3:
                        if u >= 1:
                            dve.wait_ge(transposed, u)
                        soften(u + 1)
                    normalise(u)

            @block.scalar
            def _(act):
                act.wait_ge(sums, 1)
                act.activation(lnv[:, 0], psX[:, 0:S], ACT.Ln, bias=k.eps[RMS_EPS], scale=1.0 / 256).then_inc(ln_done, 1)
                act.activation(lnv[:, 1], psX[:, S:2 * S], ACT.Ln, bias=k.eps[RMS_EPS], scale=1.0 / 128)\
                    .then_inc(ln_done, 1)
                act.wait_ge(ln_done, 2)
                act.activation(rstd[:], lnv[:], ACT.Exp, scale=-0.5).then_inc(rstd_ready, 1)
                act.wait_ge(q_done, 1)
                act.wait_ge(rope_ready, 1)
                psq = psA[:].rearrange("p b (h s) -> p (b h) s", h=2)
                act.activation(qT[0:64], psq[0:64, 0:HEADS], ACT.Copy).then_inc(q_copied, 1)
                act.wait_ge(k_done, 1)
                act.activation(kT[0:64], psq[0:64, HEADS:], ACT.Copy).then_inc(kv_copied, 1)
                act.wait_ge(v_done, 1)
                act.activation(vm[:].rearrange("p b f -> p (b f)"), psY[:], ACT.Copy).then_inc(kv_copied, 1)

                def exps(u):
                    mla, blk = units[u]
                    n, pr = P * (blk + 1), prob[:, u % 2]
                    act.wait_ge(max_ready, u + 1)
                    for h in range(HEADS):
                        ins = act.activation(pr[:, h, 0:n], pr[:, h, 0:n], ACT.Exp, bias=nmx[:, u % 2, h:h + 1],
                                             accum_out=den[:, u % 2, h:h + 1])
                    if not mla:
                        ins = act.activation(snk[:, u % 2], snk[:, u % 2], ACT.Exp)
                    ins.then_inc(exp_done, 1)

                exps(0)
                for u in range(4):
                    mla, blk = units[u]
                    if u < 3:
                        exps(u + 1)
                    nt = HEADS * (blk + 1)
                    act.wait_ge(transposed, u + 1)
                    act.activation(probT[:, 0:nt].rearrange("p t q -> p (t q)"),
                                   psT[:].rearrange("p b n -> p (b n)")[:, 0:nt * P], ACT.Copy).then_inc(probT_ready, 1)
                    act.wait_ge(attended, u + 1)
                    act.activation(y[:, 0 if mla else 6:2 if mla else 8, blk * P:(blk + 1) * P],
                                   psY[:].rearrange("p (t s) -> p t s", t=2)[:, :, 0:P], ACT.Copy).then_inc(y_copied, 1)

            @block.tensor
            def _(pe):
                pe.wait_ge(squares, 1)
                for t in range(2):
                    pe.matmul(psX[:, 0:S], k.c("ones"), sq[:, t], start=t == 0, stop=t == 1)
                pe.matmul(psX[:, S:2 * S], k.c("ones"), sq[:, 2], start=True, stop=True).then_inc(sums, 1)
                pe.wait_ge(w_loaded, 48)
                pe.wait_ge(latent_ready, 3)
                psq = psA[:].rearrange("p b (h s) -> p (b h) s", h=2)
                for h in range(HEADS):
                    for t in range(2):
                        ins = pe.matmul(psq[:, h], wuq[:, t, h], cn[:, t], start=t == 0, stop=t == 1)
                ins.then_inc(q_done, 1)
                for h in range(HEADS):
                    ins = pe.matmul(psq[0:64, HEADS + h], wukv[:, 0, h * 64:(h + 1) * 64], cn[:, 2], start=True, stop=True)
                ins.then_inc(k_done, 1)
                for blk in range(SB):
                    ins = pe.matmul(psY[:, blk * S:(blk + 1) * S], cn[:, 2, blk * P:(blk + 1) * P], wukv[:, 1],
                                    start=True, stop=True)
                ins.then_inc(v_done, 1)
                pe.wait_ge(ln_done, 2)
                pe.wait_ge(pool_ready, 1)
                for g in range(4):
                    rows, t = slice(64 * (g % 2), 64 * (g % 2) + 64), g // 2
                    ins = pe.matmul(psX[rows, t * S:(t + 1) * S], poolw[rows, t], pooled[rows, t], start=True, stop=True)
                ins.then_inc(pool_mixed, 1)

                def scores(u):
                    mla, blk = units[u]
                    n = P * (blk + 1)
                    qs = slice(blk * P, (blk + 1) * P)
                    sc = psA[:, 2 * (u % 2):2 * (u % 2) + 2].rearrange("p b (h c) -> p (b h) c", h=2)
                    if u >= 2:
                        pe.wait_ge(scores_read, u - 1)
                    for h in range(HEADS):
                        if mla:
                            ins = pe.matmul(sc[:, h, 0:n], qT[0:96, h, qs], kT[0:96, h, 0:n], start=True, stop=True)
                        else:
                            rows = slice(64 * (h // 2), 64 * (h // 2) + 64)
                            ins = pe.matmul(sc[:, h, 0:n], proj[rows, T_QS + h % 2, qs], proj[rows, T_KS, 0:n],
                                            start=True, stop=True)
                    ins.then_inc(scores_done, 1)

                pe.wait_ge(q_copied, 1)
                pe.wait_ge(kv_copied, 2)
                pe.wait_ge(rope_ready, 2)
                scores(0)
                scores(1)
                for u in range(4):
                    mla, blk = units[u]
                    pe.wait_ge(probs_ready, u + 1)
                    if u >= 1:
                        pe.wait_ge(probT_ready, u)
                    for h in range(HEADS):
                        for kb in range(blk + 1):
                            at = (h * (blk + 1) + kb) * P
                            ins = pe.transpose(psT[:, at // 512, at % 512:at % 512 + P],
                                               prob[:, u % 2, h, kb * P:(kb + 1) * P], k.c("ident"))
                    ins.then_inc(transposed, 1)
                    if u < 2:
                        scores(u + 2)
                    pe.wait_ge(probT_ready, u + 1)
                    if u >= 1:
                        pe.wait_ge(y_copied, u)
                    for h in range(HEADS):
                        rows = slice(64 * (h % 2), 64 * (h % 2) + 64)
                        for kb in range(blk + 1):
                            v = vm[:, kb, h * 64:(h + 1) * 64] if mla else vtok[:, kb, (h // 2) * 64:(h // 2) * 64 + 64]
                            ins = pe.matmul(psY[rows, (h // 2) * S:(h // 2) * S + P], v, probT[:, h * (blk + 1) + kb],
                                            start=kb == 0, stop=kb == blk)
                    ins.then_inc(attended, 1)


def stage_output1(nc, k, L, vecs, y, wo_dram):
    with Stage(nc, "output1") as st:
        w = st.sb("w_o", [P, DT, DT, P])
        sq = st.sb("sq", [P, DT, S])
        lnv = st.sb("lnv", [P, 4, S])
        rstd = st.sb("rstd", [P, 4, S])
        yn = st.sb("yn", [P, DT, S])
        psG = st.ps("psG", [P, 2, 512])
        ps = st.ps("ps", [P, 4, 512])
        w_loaded = [st.sem(f"w_loaded{i}") for i in range(4)]
        squares = st.sem("squares")
        sums = st.sem("sums")
        ln_done = st.sem("ln_done")
        rstd_ready = st.sem("rstd_ready")
        normed = st.sem("normed")
        mm_done = st.sem("mm_done")
        added = st.sem("added")
        with nc.Block() as block:

            @block.sync
            def _(sp):
                for i in range(4):
                    sp.dma_start(w[:, 2 * i:2 * i + 2], wo_dram[bass.ds(L, 1), :, 2 * i * DT * P:(2 * i + 2) * DT * P]
                                 .rearrange("a p (m k c) -> (a p) m k c", m=2, k=DT)).then_inc(w_loaded[i], 16)

            @block.vector
            def _(dve):
                dve.tensor_tensor(sq[:], y[:], y[:], ALU.mult).then_inc(squares, 1)
                dve.wait_ge(rstd_ready, 1)
                g0 = V1["mix_norm"][0]
                for t in range(DT):
                    dve.scalar_tensor_tensor(yn[:, t], y[:, t], vecs[:, g0 + t:g0 + t + 1], rstd[:, t // 2],
                                             ALU.mult, ALU.mult).then_inc(normed, 1)
                for m in range(4):
                    dve.wait_ge(mm_done, m + 1)
                    xm = k.x[:, 2 * m:2 * m + 2].rearrange("p a s -> p (a s)")
                    dve.tensor_tensor(xm, xm, ps[:, m], ALU.add).then_inc(added, 1)

            @block.scalar
            def _(act):
                act.wait_ge(sums, 1)
                act.activation(lnv[:].rearrange("p g s -> p (g s)"), psG[:].rearrange("p b n -> p (b n)"), ACT.Ln,
                               bias=k.eps[RMS_EPS], scale=1.0 / 256).then_inc(ln_done, 1)
                act.wait_ge(ln_done, 1)
                act.activation(rstd[:], lnv[:], ACT.Exp, scale=-0.5).then_inc(rstd_ready, 1)

            @block.tensor
            def _(pe):
                pe.wait_ge(squares, 1)
                for g in range(4):
                    for t in range(2):
                        ins = pe.matmul(psG[:, g // 2, (g % 2) * S:(g % 2 + 1) * S], k.c("ones"), sq[:, 2 * g + t],
                                        start=t == 0, stop=t == 1)
                ins.then_inc(sums, 1)
                pe.wait_ge(normed, DT)
                for m in range(DT):
                    if m % 2 == 0:
                        pe.wait_ge(w_loaded[m // 2], 16)
                    for kk in range(DT):
                        ins = pe.matmul(ps[:, m // 2, (m % 2) * S:(m % 2 + 1) * S], w[:, m, kk], yn[:, kk],
                                        start=kk == 0, stop=kk == DT - 1)
                    if m % 2:
                        ins.then_inc(mm_done, 1)


FFN_RING = 6


def stage_ffn1(nc, k, L, vecs, wgu_dram, wd_dram):
    with Stage(nc, "ffn1") as st:
        h = st.sb("h", [P, DT, S])
        ring = st.sb("ring", [P, FFN_RING, 2, DT, P])
        ringd = st.sb("ringd", [P, 3, FT, P])
        act_sb = st.sb("act_sb", [P, FT, S])
        sig = st.sb("sig", [P, 2, S])
        ps = st.ps("ps", [P, 4, 512])
        up_loaded = [st.sem(f"up_loaded{i}") for i in range(FFN_RING)]
        down_loaded = [st.sem(f"down_loaded{i}") for i in range(3)]
        mm_done = st.sem("mm_done")
        sig_ready = st.sem("sig_ready")
        act_ready = st.sem("act_ready")
        added = st.sem("added")
        dve_step = st.sem("dve_step")
        n_vec, n_act, n_pe, normed = norm_engines(k, st, k.x, h, vecs[:, V1["ffn_norm"][0]:], RMS_EPS)
        with nc.Block() as block:

            @block.sync
            def _(sp):
                for j in range(FT):
                    if j >= FFN_RING:
                        sp.wait_ge(mm_done, j - FFN_RING + 1)
                    sp.dma_start(ring[:, j % FFN_RING], wgu_dram[bass.ds(L, 1), j]
                                 .rearrange("a p (g k c) -> (a p) g k c", g=2, k=DT)).then_inc(up_loaded[j % FFN_RING], 16)
                for m in range(DT):
                    if m >= 3:
                        sp.wait_ge(mm_done, FT + m - 2)
                    sp.dma_start(ringd[:, m % 3], wd_dram[bass.ds(L, 1), m].rearrange("a p (k c) -> (a p) k c", k=FT))\
                        .then_inc(down_loaded[m % 3], 16)

            @block.vector
            def _(dve):
                ch = Chain(dve, dve_step)
                n_vec(dve, ch)
                for j in range(FT):
                    dve.wait_ge(sig_ready, j + 1)
                    ch.link(dve.tensor_tensor(sig[:, j % 2], sig[:, j % 2], ps[:, j % 4, 0:S], ALU.mult))
                    dve.tensor_tensor(act_sb[:, j], sig[:, j % 2], ps[:, j % 4, S:2 * S], ALU.mult).then_inc(act_ready, 1)
                for m in range(DT):
                    dve.wait_ge(mm_done, FT + m + 1)
                    dve.tensor_tensor(k.x[:, m], k.x[:, m], ps[:, (FT + m) % 4, 0:S], ALU.add).then_inc(added, 1)

            @block.scalar
            def _(act):
                n_act(act)
                for j in range(FT):
                    act.wait_ge(mm_done, j + 1)
                    if j >= 2:
                        act.wait_ge(act_ready, j - 1)
                    act.activation(sig[:, j % 2], ps[:, j % 4, 0:S], ACT.Sigmoid).then_inc(sig_ready, 1)

            @block.tensor
            def _(pe):
                n_pe(pe)
                pe.wait_ge(normed, DT)
                for j in range(FT):
                    pe.wait_ge(up_loaded[j % FFN_RING], 16 * (j // FFN_RING + 1))
                    if j >= 4:
                        pe.wait_ge(act_ready, j - 3)
                    for g in range(2):
                        for kk in range(DT):
                            ins = pe.matmul(ps[:, j % 4, g * S:(g + 1) * S], ring[:, j % FFN_RING, g, kk], h[:, kk],
                                            start=kk == 0, stop=kk == DT - 1)
                    ins.then_inc(mm_done, 1)
                pe.wait_ge(act_ready, FT)
                for m in range(DT):
                    pe.wait_ge(down_loaded[m % 3], 16 * (m // 3 + 1))
                    if m >= 4:
                        pe.wait_ge(added, m - 3)
                    for j in range(FT):
                        ins = pe.matmul(ps[:, (FT + m) % 4, 0:S], ringd[:, m % 3, j], act_sb[:, j],
                                        start=j == 0, stop=j == FT - 1)
                    ins.then_inc(mm_done, 1)


def stage_norm(nc, k, name, vec_dram, col_g, col_b, n, eps):
    with Stage(nc, name) as st:
        gv = st.sb("gv", [P, n])
        tmp = st.sb("tmp", [P, DT, S])
        loaded = st.sem("loaded")
        dve_step = st.sem("dve_step")
        n_vec, n_act, n_pe, normed = norm_engines(k, st, k.x, tmp, gv[:, col_g:col_g + DT], eps,
                                                  None if col_b is None else gv[:, col_b:col_b + DT])
        with nc.Block() as block:

            @block.sync
            def _(sp):
                sp.dma_start(gv[:], vec_dram).then_inc(loaded, 16)

            @block.vector
            def _(dve):
                dve.wait_ge(loaded, 16)
                n_vec(dve, Chain(dve, dve_step))
                dve.wait_ge(normed, DT)
                dve.tensor_copy(k.x[:], tmp[:])

            @block.scalar
            def _(act):
                n_act(act)

            @block.tensor
            def _(pe):
                n_pe(pe)


def stage_store(nc, k, out):
    with Stage(nc, "store") as st:
        stored = st.sem("stored")
        with nc.Block() as block:

            @block.sync
            def _(sp):
                sp.dma_start(out.rearrange("p (t s) -> p t s", t=DT), k.x[:]).then_inc(stored, 16)
                sp.wait_ge(stored, 16)




def stage_project2(nc, k, L, w_dram, v_dram, vecs, b):
    with Stage(nc, "project2") as st:
        w = st.sb("w", [P, DT * IN2_COLS])
        ps = st.ps("ps", [P, 4, 512])
        loaded = [st.sem(f"loaded{i}") for i in range(12)]
        mm_done = st.sem("mm_done")
        copied = st.sem("copied")
        dst = [b.z[:, t] for t in range(4)] + [b.xbc[:, t, 3:] for t in range(6)] + \
              [b.rw[:, t, 1:] for t in range(7)] + [b.gl[:, t] for t in range(4)] + \
              [b.ga[0:N_GA, :], b.tokm[:, 0], b.tokm[:, 1]]
        cols = [P] * IN2_TILES + [N_GA, N_TOKM, N_TOKM]
        off = [DT * P * t for t in range(IN2_TILES)] + [DT * P * IN2_TILES] + [DT * (P * IN2_TILES + N_GA)] * 2
        n_units = len(dst)
        chunk_end = [off[2 * i] for i in range(1, 12)] + [DT * IN2_COLS]

        with nc.Block() as block:

            @block.sync
            def _(sp):
                a = 0
                for i, e in enumerate(chunk_end):
                    sp.dma_start(w[:, a:e], w_dram[bass.ds(L, 1), :, a:e].rearrange("a p n -> (a p) n"))\
                        .then_inc(loaded[i], 16)
                    a = e
                    if i == 0:
                        sp.dma_start(vecs[:], v_dram[bass.ds(L, 1)].rearrange("a p n -> (a p) n")).then_inc(copied, 16)
                sp.wait_ge(copied, 16 + n_units)

            @block.scalar
            def _(act):
                for u in range(n_units):
                    act.wait_ge(mm_done, u + 1)
                    m, n = (N_GA, S) if u == IN2_TILES else (P, N_TOKM) if u > IN2_TILES else (P, S)
                    act.activation(dst[u], ps[0:m, u % 4, 0:n], ACT.Copy).then_inc(copied, 1)

            @block.tensor
            def _(pe):
                for u in range(n_units):
                    chunk = min(i for i, e in enumerate(chunk_end) if off[u] + DT * cols[u] <= e)
                    pe.wait_ge(loaded[chunk], 16)
                    if u >= 4:
                        pe.wait_ge(copied, 16 + u - 3)
                    wt = w[:, off[u]:off[u] + DT * cols[u]].rearrange("p (k c) -> p k c", k=DT)
                    for kk in range(DT):
                        if u > IN2_TILES:
                            blk = u - IN2_TILES - 1
                            ins = pe.matmul(ps[:, u % 4, 0:N_TOKM], k.x[:, kk, blk * P:(blk + 1) * P], wt[:, kk],
                                            start=kk == 0, stop=kk == DT - 1)
                        else:
                            ins = pe.matmul(ps[0:cols[u], u % 4, 0:S], wt[:, kk], k.x[:, kk],
                                            start=kk == 0, stop=kk == DT - 1)
                    ins.then_inc(mm_done, 1)


def stage_ssd(nc, k, vecs, b, y):
    with Stage(nc, "ssd") as st:
        cx = st.sb("cx", [P, 6, S])
        sg = st.sb("sg", [P, 6, S])
        dt = st.sb("dt", [P, SB, 8])
        dta = st.sb("dta", [P, SB, 8])
        tmp = st.sb("tmp", [P, SB, 8])
        ea = st.sb("ea", [P, 8])
        G = st.sb("G", [P, SB, 8, P])
        xd = st.sb("xd", [P, SB, 8, 64])
        cb = st.sb("cb", [P, 2, 3 * P])
        E = st.sb("E", [P, 2, 3 * P])
        M = st.sb("M", [P, 2, 3 * P])
        sq = st.sb("sq", [P, 4, S])
        lnv = st.sb("lnv", [P, 2, S])
        rstd = st.sb("rstd", [P, 2, S])
        psT = st.ps("psT", [P, SB, 512])
        psC = st.ps("psC", [P, 2, 512])
        psD = st.ps("psD", [P, 2, 512])
        psY = st.ps("psY", [P, 2, 512])
        dve_step, act_step = st.sem("dve_step"), st.sem("act_step")
        conv_ready, sig_ready, x_ready = st.sem("conv_ready"), st.sem("sig_ready"), st.sem("x_ready")
        dt_pre, dt_exp, dt_ready = st.sem("dt_pre"), st.sem("dt_exp"), st.sem("dt_ready")
        xT_done, xd_ready = st.sem("xT_done"), st.sem("xd_ready")
        cb_done, G_ready = st.sem("cb_done"), st.sem("G_ready")
        decay_done, E_ready, M_ready = st.sem("decay_done"), st.sem("E_ready"), st.sem("M_ready")
        y_done, squares, sums, rstd_ready = st.sem("y_done"), st.sem("squares"), st.sem("sums"), st.sem("rstd_ready")
        z_sig = st.sem("z_sig")
        vec = lambda n, i=0: vecs[:, V2[n][0] + i:V2[n][0] + i + 1]
        vecn = lambda n: vecs[:, V2[n][0]:V2[n][0] + V2[n][1]]
        psYt = psY[:].rearrange("p b (t s) -> p (b t) s", t=2)

        with nc.Block() as block:

            @block.vector
            def _(dve):
                ch = Chain(dve, dve_step)
                ch.link(dve.tensor_tensor(dt[:], b.tokm[:, :, 0:8], bc(vecn("dt_bias"), SB, 1), ALU.add))
                ch.link(dve.tensor_scalar(tmp[:], dt[:], -1.0, None, ALU.mult))
                dve.tensor_tensor(tmp[:], tmp[:], dt[:], ALU.max).then_inc(dt_pre, 1)
                for t in range(6):
                    ch.link(dve.tensor_scalar(cx[:, t], b.xbc[:, t, 0:S], vec("conv_w", t), vec("conv_b", t),
                                              ALU.mult, ALU.add))
                    for tap in (1, 2, 3):
                        ins = dve.scalar_tensor_tensor(cx[:, t], b.xbc[:, t, tap:tap + S], vec("conv_w", 6 * tap + t),
                                                       cx[:, t], ALU.mult, ALU.add)
                        if tap < 3:
                            ch.link(ins)
                    ins.then_inc(conv_ready, 1)
                dve.wait_ge(dt_exp, 1)
                ch.link(dve.tensor_scalar(dt[:], dt[:], 0.0, None, ALU.max))
                ch.link(dve.tensor_tensor(dt[:], dt[:], tmp[:], ALU.add))
                ch.link(dve.tensor_tensor(dta[:], dt[:], bc(ea[:], SB, 1), ALU.mult))
                dve.tensor_scalar(dta[:], dta[:], -1.0, None, ALU.mult).then_inc(dt_ready, 1)
                dve.wait_ge(dt_ready, 1)
                for h in range(8):
                    for blk in range(SB):
                        dve.tensor_scalar(G[:, blk, h], k.c("gt"), dta[:, blk, h:h + 1], None, ALU.mult)\
                            .then_inc(G_ready, 1)
                dve.wait_ge(sig_ready, 1)
                dve.wait_ge(conv_ready, 6)
                dve.tensor_tensor(cx[:], cx[:], sg[:], ALU.mult).then_inc(x_ready, 1)
                dve.wait_ge(cb_done, 1)
                for g in range(2):
                    ins = dve.tensor_tensor(cb[:, g], psC[:, g, 0:3 * P], k.c("le3"), ALU.mult)
                    ch.link(ins)
                dve.wait_ge(xT_done, 1)
                for blk in range(SB):
                    dve.tensor_tensor(xd[:, blk], psT[:, blk].rearrange("p (h c) -> p h c", h=8),
                                      bc(dt[:, blk], 64, 2), ALU.mult).then_inc(xd_ready, 1)
                for h in range(8):
                    dve.wait_ge(E_ready, h + 1)
                    if h >= 2:
                        dve.wait_ge(y_done, h - 1)
                    dve.tensor_tensor(M[:, h % 2], E[:, h % 2], cb[:, h // 4], ALU.mult).then_inc(M_ready, 1)
                dve.wait_ge(y_done, 8)
                for t in range(4):
                    ins = dve.scalar_tensor_tensor(y[:, t], cx[:, t], vec("ssd_d", t), psYt[:, t], ALU.mult, ALU.add)
                    ch.link(ins)
                dve.wait_ge(z_sig, 1)
                ch.link(dve.tensor_tensor(y[:, 0:4], y[:, 0:4], b.z[:], ALU.mult))
                ch.link(dve.tensor_tensor(y[:, 0:4], y[:, 0:4], sg[:, 0:4], ALU.mult))
                dve.tensor_tensor(sq[:], y[:, 0:4], y[:, 0:4], ALU.mult).then_inc(squares, 1)
                dve.wait_ge(rstd_ready, 1)
                for t in range(4):
                    dve.scalar_tensor_tensor(y[:, t], y[:, t], vec("ssd_norm", t), rstd[:, t // 2], ALU.mult, ALU.mult)

            @block.scalar
            def _(act):
                ch = Chain(act, act_step)
                act.wait_ge(dt_pre, 1)
                ch.link(act.activation(ea[:], vecn("a_log"), ACT.Exp))
                ch.link(act.activation(tmp[:], tmp[:], ACT.Exp, scale=-1.0))
                act.activation(tmp[:], tmp[:], ACT.Ln, bias=k.eps[1.0]).then_inc(dt_exp, 1)
                act.wait_ge(conv_ready, 6)
                act.activation(sg[:], cx[:], ACT.Sigmoid).then_inc(sig_ready, 1)
                act.wait_ge(x_ready, 1)
                act.activation(sg[:, 0:4], b.z[:], ACT.Sigmoid).then_inc(z_sig, 1)
                for h in range(8):
                    act.wait_ge(decay_done, h + 1)
                    if h >= 2:
                        act.wait_ge(M_ready, h - 1)
                    act.activation(E[:, h % 2], psD[:, h % 2, 0:3 * P], ACT.Exp).then_inc(E_ready, 1)
                act.wait_ge(sums, 1)
                ch.link(act.activation(lnv[:].rearrange("p g s -> p (g s)"), psT[:, 0], ACT.Ln, bias=k.eps[RMS_EPS],
                                       scale=1.0 / 256))
                act.activation(rstd[:], lnv[:], ACT.Exp, scale=-0.5).then_inc(rstd_ready, 1)

            @block.tensor
            def _(pe):
                def decay(h):
                    pe.wait_ge(G_ready, 2 * h + 2)
                    if h >= 2:
                        pe.wait_ge(E_ready, h - 1)
                    d = psD[:, h % 2]
                    le3 = k.c("le3")
                    pe.matmul(d[:, 0:2 * P], G[:, 0, h], le3[:, 0:2 * P], start=True, stop=False)
                    pe.matmul(d[:, P:2 * P], dta[:, 1, h:h + 1].broadcast_to([P, P]), le3[:, 0:P], start=False, stop=True)
                    pe.matmul(d[:, 2 * P:3 * P], G[:, 1, h], le3[:, 0:P], start=True, stop=True).then_inc(decay_done, 1)

                decay(0)
                decay(1)
                pe.wait_ge(x_ready, 1)
                for g in range(2):
                    rows = slice(64 * g, 64 * g + 64)
                    pe.matmul(psC[:, g, 0:S], cx[rows, 4, 0:P], cx[rows, 5], start=True, stop=True)
                    ins = pe.matmul(psC[:, g, S:S + P], cx[rows, 4, P:S], cx[rows, 5, P:S], start=True, stop=True)
                ins.then_inc(cb_done, 1)
                for blk in range(SB):
                    for t in range(4):
                        ins = pe.transpose(psT[:, blk, t * P:(t + 1) * P], cx[:, t, blk * P:(blk + 1) * P], k.c("ident"))
                ins.then_inc(xT_done, 1)
                pe.wait_ge(xd_ready, 2)
                for h in range(8):
                    pe.wait_ge(M_ready, h + 1)
                    rows, t = slice(64 * (h % 2), 64 * (h % 2) + 64), h // 2
                    pe.matmul(psYt[rows, t], xd[:, 0, h], M[:, h % 2, 0:S], start=True, stop=False)
                    pe.matmul(psYt[rows, t, P:S], xd[:, 1, h], M[:, h % 2, S:S + P], start=False, stop=True)\
                        .then_inc(y_done, 1)
                    if h + 2 < 8:
                        decay(h + 2)
                pe.wait_ge(squares, 1)
                for g in range(2):
                    for t in range(2):
                        ins = pe.matmul(psT[:, 0, g * S:(g + 1) * S], k.c("ones"), sq[:, 2 * g + t],
                                        start=t == 0, stop=t == 1)
                ins.then_inc(sums, 1)


def stage_rwkv(nc, k, vecs, b, lr_dram, L, y):
    with Stage(nc, "rwkv") as st:
        lrw = st.sb("lrw", [P, 256])
        ps_ = st.sb("shifted", [P, 7, S])
        lact = st.sb("lact", [P, S])
        wa = st.sb("wa", [P, 4, S])
        gg = st.sb("gg", [P, 2, S])
        cum = st.sb("cum", [P, 2, S])
        ex = st.sb("ex", [P, 3, 2, S])
        kk = st.sb("kk", [P, 2, S])
        t1 = st.sb("t1", [P, 2, S])
        t2 = st.sb("t2", [P, 2, S])
        F = st.sb("F", [P, 4, 2, S])
        A_, B_, K_, R_ = range(4)
        tok = st.sb("tok", [P, 4, SB, 256])
        U = HEADS * SB
        mN = st.sb("mN", [P, 2, U, P])
        mX = st.sb("mX", [P, U, P])
        mM = st.sb("mM", [P, 3, U, P])
        W = st.sb("W", [P, 3, SB, HEADS, 64])
        QT = st.sb("QT", [P, CPB, SB * 2, P])
        EE = st.sb("EE", [P, CPB, SB * 2, P])
        St = st.sb("St", [P, NCH, 2, P])
        Rp = st.sb("Rp", [P, 2, S])
        yy = st.sb("yy", [P, 2, S])
        lnv = st.sb("lnv", [P, 2, S])
        rstd = st.sb("rstd", [P, 2, S])
        ps = st.ps("ps", [P, 8, 512])
        lr_loaded = st.sem("lr_loaded")
        dve_step, act_step = st.sem("dve_step"), st.sem("act_step")
        (low_ready, lact_ready, kksq_ready, low_done, logits_ready, kknorm_ready, sig_ready, gate_copied, sums_ready,
         exps_ready, F_ready, masked_done, masked, tok_done, tok_copied, power_done, power_copied, inv_done,
         inv_updated, mv_done, mv_copied, w_done, w_copied, q_done, e_done, q_ready, e_ready, state_done,
         state_ready, rp_done, rp_ready, intra_done, intra_copied, inter_done, yy_ready, bonus_ready, mean_done,
         bonus_done, sq_ready, var_done, rstd_ready) = [st.sem(n) for n in (
             "low_ready lact_ready kksq_ready low_done logits_ready kknorm_ready sig_ready gate_copied sums_ready "
             "exps_ready F_ready masked_done masked tok_done tok_copied power_done power_copied inv_done "
             "inv_updated mv_done mv_copied w_done w_copied q_done e_done q_ready e_ready state_done "
             "state_ready rp_done rp_ready intra_done intra_copied inter_done yy_ready bonus_ready mean_done "
             "bonus_done sq_ready var_done rstd_ready").split()]
        vec = lambda n, i=0: vecs[:, V2[n][0] + i:V2[n][0] + i + 1]
        flat = lambda a: a.rearrange("p a s -> p (a s)")
        unit = lambda h, blk: ((h % 2) * SB + blk) * 2 + h // 2
        ones64 = k.c("ones64")
        bank2 = lambda i: ps[:, i:i + 2].rearrange("p b (u n) -> p (b u) n", u=4)
        r_, k_, v_ = ps_[:, 0:2], ps_[:, 2:4], ps_[:, 4:6]

        with nc.Block() as block:

            @block.sync
            def _(sp):
                sp.dma_start(lrw[:], lr_dram[bass.ds(L, 1)].rearrange("a p n -> (a p) n")).then_inc(lr_loaded, 16)

            @block.vector
            def _(dve):
                ch = Chain(dve, dve_step)
                ch.link(dve.tensor_tensor(ps_[:], b.rw[:, :, 0:S], b.rw[:, :, 1:], ALU.subtract))
                dve.scalar_tensor_tensor(ps_[:, 6], ps_[:, 6], vec("mu", 6), b.rw[:, 6, 1:], ALU.mult, ALU.add)\
                    .then_inc(low_ready, 1)
                for t in (2, 3, 0, 1, 4, 5):
                    ins = dve.scalar_tensor_tensor(ps_[:, t], ps_[:, t], vec("mu", t), b.rw[:, t, 1:], ALU.mult, ALU.add)
                ch.link(ins)
                for t in range(2):
                    ins = dve.tensor_scalar(kk[:, t], k_[:, t], vec("k_k", t), None, ALU.mult)
                ch.link(ins)
                dve.tensor_tensor(t1[:], kk[:], kk[:], ALU.mult).then_inc(kksq_ready, 1)
                dve.wait_ge(low_done, 1)
                for t in range(4):
                    ins = dve.tensor_scalar(wa[:, t], ps[:, t // 2, (t % 2) * S:(t % 2 + 1) * S],
                                            vec("w0" if t < 2 else "a0", t % 2), None, ALU.add)
                ins.then_inc(logits_ready, 1)
                dve.wait_ge(kknorm_ready, 1)
                ch.link(dve.tensor_tensor(kk[:], kk[:], rstd[:], ALU.mult))
                dve.wait_ge(sig_ready, 1)
                ch.link(dve.tensor_scalar(wa[:, 0:2], wa[:, 0:2], -float(np.exp(-0.5)), None, ALU.mult))
                ch.link(dve.tensor_tensor_scan(flat(cum[:]), k.c("keep"), flat(wa[:, 0:2]), 0.0, ALU.mult, ALU.add))
                dve.tensor_tensor(t2[:], cum[:], wa[:, 0:2], ALU.subtract).then_inc(sums_ready, 1)
                for t in range(2):
                    ins = dve.tensor_scalar(t1[:, t], wa[:, 2 + t], 1.0, vec("k_a", t), ALU.subtract, ALU.mult)
                ch.link(ins)
                ch.link(dve.scalar_tensor_tensor(k_, t1[:], 1.0, k_, ALU.add, ALU.mult))
                ch.link(dve.tensor_tensor(t1[:], kk[:], wa[:, 2:4], ALU.mult))
                dve.wait_ge(exps_ready, 1)
                dve.scalar_tensor_tensor(F[:, A_], kk[:], -1.0, ex[:, 2], ALU.mult, ALU.mult)
                dve.tensor_tensor(F[:, B_], t1[:], ex[:, 1], ALU.mult)
                dve.tensor_tensor(F[:, K_], k_, ex[:, 1], ALU.mult)
                dve.tensor_tensor(F[:, R_], r_, ex[:, 0], ALU.mult).then_inc(F_ready, 1)
                for i, m in enumerate(("cl_strict", "cu_strict", "cu_strict", "cu_incl", "cu_incl")):
                    dst = mN[:, i] if i < 2 else mM[:, i - 2]
                    dve.wait_ge(masked_done, i + 1)
                    dve.tensor_tensor(dst, bank2(2 * (i % 3)), bc(k.c(m), U, 1), ALU.mult).then_inc(masked, 1)
                    if i == 1:
                        dve.wait_ge(masked, 2)
                        ch.link(dve.tensor_tensor(mX[:], mN[:, 1], bc(k.c("ident"), U, 1), ALU.add))
                for j in range(4):
                    dve.wait_ge(inv_done, j + 1)
                    dve.tensor_tensor(mX[:], mX[:], bank2(4), ALU.add).then_inc(inv_updated, 1)
                    dve.wait_ge(inv_updated, j + 1)
                dve.wait_ge(w_done, 1)
                dve.tensor_copy(W[:, 2].rearrange("p b h c -> p (b h c)"), ps[:, 7]).then_inc(w_copied, 1)
                dve.wait_ge(q_done, 1)
                psQ = ps[:, 0:4].rearrange("p j (n c) -> p (j n) c", n=4)
                qt = QT[:].rearrange("p j n c -> p (j n) c")
                ch.link(dve.tensor_tensor(qt, psQ, bc(ones64, 16, 1), ALU.mult))
                dve.tensor_tensor(qt, qt, bc(k.c("ident"), 16, 1), ALU.add).then_inc(q_ready, 1)
                dve.wait_ge(e_done, 1)
                for c in range(NCH):
                    for pr in range(2):
                        j, n = c % CPB, (c // CPB) * 2 + pr
                        ins = dve.scalar_tensor_tensor(EE[:, j, n], ps[:, 4 + j, n * P:(n + 1) * P],
                                                       ex[:, 0, pr, C * c + C - 1:C * c + C], ones64, ALU.mult, ALU.mult)
                ins.then_inc(e_ready, 1)
                dve.wait_ge(e_ready, 1)
                dve.tensor_copy(St[:, 1], EE[:, 0, 0:2]).then_inc(state_ready, 1)
                dve.wait_ge(rp_done, 1)
                dve.tensor_tensor(flat(Rp[:]), flat(F[:, R_]), ps[:, 2], ALU.add).then_inc(rp_ready, 1)
                for c in range(1, NCH - 1):
                    dve.wait_ge(state_done, c)
                    for pr in range(2):
                        ins = dve.scalar_tensor_tensor(St[:, c + 1, pr], ps[:, pr, (c % 4) * P:(c % 4 + 1) * P],
                                                       ex[:, 0, pr, C * c + C - 1:C * c + C],
                                                       EE[:, c % CPB, (c // CPB) * 2 + pr], ALU.mult, ALU.add)
                    ins.then_inc(state_ready, 1)
                for t in range(2):
                    ins = dve.scalar_tensor_tensor(t1[:, t], r_[:, t], vec("r_k", t), k_[:, t], ALU.mult, ALU.mult)
                ins.then_inc(bonus_ready, 1)
                dve.wait_ge(intra_copied, 1)
                dve.wait_ge(inter_done, 1)
                psI = ps[:, 4].rearrange("p (a s) -> p a s", a=2)
                dve.tensor_tensor(yy[:, :, C:], yy[:, :, C:], psI[:, :, C:], ALU.add).then_inc(yy_ready, 1)
                dve.wait_ge(mean_done, 1)
                ch.link(dve.scalar_tensor_tensor(flat(yy[:]), ps[:, 5], -1.0 / 64, flat(yy[:]), ALU.mult, ALU.add))
                dve.tensor_tensor(t2[:], yy[:], yy[:], ALU.mult).then_inc(sq_ready, 1)
                dve.wait_ge(bonus_done, 1)
                ch.link(dve.tensor_tensor(flat(v_), ps[:, 6], flat(v_), ALU.mult))
                dve.wait_ge(rstd_ready, 1)
                for t in range(2):
                    ins = dve.scalar_tensor_tensor(yy[:, t], yy[:, t], vec("ln_g", t), rstd[:, t], ALU.mult, ALU.mult)
                ch.link(ins)
                for t in range(2):
                    ins = dve.scalar_tensor_tensor(yy[:, t], yy[:, t], vec("ln_b", t), v_[:, t], ALU.add, ALU.add)
                ch.link(ins)
                dve.wait_ge(gate_copied, 1)
                dve.tensor_tensor(y[:, 4:6], yy[:], gg[:], ALU.mult)

            @block.scalar
            def _(act):
                ch = Chain(act, act_step)
                act.wait_ge(low_ready, 1)
                act.activation(lact[0:32, :], ps_[0:32, 6], ACT.Tanh)
                act.activation(lact[32:64, :], ps_[32:64, 6], ACT.Copy)
                act.activation(lact[64:128, :], ps_[64:128, 6], ACT.Sigmoid).then_inc(lact_ready, 1)
                act.wait_ge(low_done, 1)
                act.activation(flat(gg[:]), ps[:, 2], ACT.Copy).then_inc(gate_copied, 1)
                ch.link(act.activation(flat(lnv[:]), ps[:, 3], ACT.Ln, bias=k.eps[1e-12]))
                act.activation(rstd[:], lnv[:], ACT.Exp, scale=-0.5).then_inc(kknorm_ready, 1)
                act.wait_ge(logits_ready, 1)
                act.activation(wa[:], wa[:], ACT.Sigmoid).then_inc(sig_ready, 1)
                act.wait_ge(sums_ready, 1)
                act.activation(ex[:, 0], cum[:], ACT.Exp)
                act.activation(ex[:, 1], cum[:], ACT.Exp, scale=-1.0)
                act.activation(ex[:, 2], t2[:], ACT.Exp).then_inc(exps_ready, 1)
                for i in range(2):
                    act.wait_ge(tok_done, i + 1)
                    act.activation(tok[:, 2 * i].rearrange("p b f -> p (b f)"), ps[:, 6], ACT.Copy)
                    act.activation(tok[:, 2 * i + 1].rearrange("p b f -> p (b f)"), ps[:, 7], ACT.Copy)\
                        .then_inc(tok_copied, 1)
                act.wait_ge(mv_done, 1)
                act.activation(W[:, 0].rearrange("p b h c -> p (b h c)"), ps[:, 6], ACT.Copy).then_inc(mv_copied, 1)
                for j in range(4):
                    act.wait_ge(power_done, j + 1)
                    ins = act.activation(mN[:, 0], bank2(0), ACT.Copy)
                    if j < 3:
                        ins = act.activation(mN[:, 1], bank2(2), ACT.Copy)
                    ins.then_inc(power_copied, 1)
                act.wait_ge(w_done, 1)
                act.activation(W[:, 1].rearrange("p b h c -> p (b h c)"), ps[:, 6], ACT.Copy).then_inc(w_copied, 1)
                act.wait_ge(intra_done, 1)
                act.activation(flat(yy[:]), ps[:, 3], ACT.Copy).then_inc(intra_copied, 1)
                act.wait_ge(var_done, 1)
                ch.link(act.activation(flat(lnv[:]), ps[:, 7], ACT.Ln, bias=k.eps[64e-5], scale=1.0 / 64))
                act.activation(rstd[:], lnv[:], ACT.Exp, scale=-0.5).then_inc(rstd_ready, 1)

            @block.tensor
            def _(pe):
                def heads64(bank, src):
                    for t in range(2):
                        ins = pe.matmul(ps[:, bank, t * S:(t + 1) * S], ones64, src[:, t], start=True, stop=True)
                    return ins

                pe.wait_ge(lr_loaded, 16)
                pe.wait_ge(lact_ready, 1)
                for bank, rows in ((0, slice(0, 32)), (1, slice(32, 64)), (2, slice(64, 128))):
                    for t in range(2):
                        pe.matmul(ps[:, bank, t * S:(t + 1) * S], lrw[rows, t * P:(t + 1) * P], lact[rows, :],
                                  start=True, stop=True)
                pe.wait_ge(kksq_ready, 1)
                heads64(3, t1).then_inc(low_done, 1)
                pe.wait_ge(F_ready, 1)
                pe.wait_ge(gate_copied, 1)

                def transposes(srcs):
                    for bank, src in srcs:
                        for blk in range(SB):
                            for t in range(2):
                                ins = pe.transpose(ps[:, bank, (blk * 2 + t) * P:(blk * 2 + t + 1) * P],
                                                   src[:, t, blk * P:(blk + 1) * P], k.c("ident"))
                    ins.then_inc(tok_done, 1)

                for i, (a, c) in enumerate(((A_, B_), (B_, A_), (K_, A_), (B_, R_), (K_, R_))):
                    if i >= 3:
                        pe.wait_ge(masked, i - 2)
                    for h in range(HEADS):
                        rows = slice(64 * (h % 2), 64 * (h % 2) + 64)
                        for blk in range(SB):
                            cols = slice(blk * P, (blk + 1) * P)
                            ins = pe.matmul(bank2(2 * (i % 3))[:, unit(h, blk)], F[rows, a, h // 2, cols],
                                            F[rows, c, h // 2, cols], start=True, stop=True)
                    ins.then_inc(masked_done, 1)
                    if i == 1:
                        transposes(((6, F[:, A_]), (7, F[:, B_])))
                pe.wait_ge(tok_copied, 1)
                transposes(((6, F[:, K_]), (7, v_)))

                def squares(j):
                    for u in range(U):
                        ins = pe.matmul(bank2(0)[:, u], mN[:, 1, u], mN[:, 0, u], start=True, stop=True)
                    if j < 3:
                        for u in range(U):
                            ins = pe.matmul(bank2(2)[:, u], mN[:, 0, u], mN[:, 1, u], start=True, stop=True)
                    ins.then_inc(power_done, 1)

                pe.wait_ge(masked, 5)
                squares(0)
                pe.wait_ge(tok_copied, 2)
                for blk in range(SB):
                    for h in range(HEADS):
                        ins = pe.matmul(ps[:, 6, (blk * HEADS + h) * 64:(blk * HEADS + h + 1) * 64],
                                        mM[:, 0, unit(h, blk)], tok[:, 3, blk, h * 64:(h + 1) * 64], start=True, stop=True)
                ins.then_inc(mv_done, 1)
                for j in range(4):
                    pe.wait_ge(power_copied, j + 1)
                    if j >= 1:
                        pe.wait_ge(inv_updated, j)
                    for u in range(U):
                        ins = pe.matmul(bank2(4)[:, u], mN[:, 0, u], mX[:, u], start=True, stop=True)
                    ins.then_inc(inv_done, 1)
                    if j < 3:
                        squares(j + 1)
                pe.wait_ge(inv_updated, 4)
                pe.wait_ge(mv_copied, 1)
                for blk in range(SB):
                    for h in range(HEADS):
                        at = (blk * HEADS + h) * 64
                        pe.matmul(ps[:, 6, at:at + 64], mX[:, unit(h, blk)], W[:, 0, blk, h], start=True, stop=True)
                        ins = pe.matmul(ps[:, 7, at:at + 64], mX[:, unit(h, blk)], tok[:, A_, blk, h * 64:(h + 1) * 64],
                                        start=True, stop=True)
                ins.then_inc(w_done, 1)
                pe.wait_ge(w_copied, 2)
                Wp = W[:].rearrange("p w b h c -> p w b (h c)")
                for what, done in ((0, q_done), (1, e_done)):
                    for blk in range(SB):
                        for pr in range(2):
                            cols, n = slice(pr * P, (pr + 1) * P), blk * 2 + pr
                            for j in range(CPB):
                                rows = slice(C * j, C * j + C)
                                if what == 0:
                                    ins = pe.matmul(ps[:, j, n * P:(n + 1) * P], Wp[rows, 2, blk, cols],
                                                    tok[rows, B_, blk, cols], start=True, stop=True)
                                else:
                                    pe.matmul(ps[:, 4 + j, n * P:(n + 1) * P], tok[rows, B_, blk, cols],
                                              Wp[rows, 1, blk, cols], start=True, stop=False)
                                    ins = pe.matmul(ps[:, 4 + j, n * P:(n + 1) * P], tok[rows, K_, blk, cols],
                                                    tok[rows, 3, blk, cols], start=False, stop=True)
                    ins.then_inc(done, 1)
                pe.wait_ge(q_ready, 1)
                for h in range(HEADS):
                    rows = slice(64 * (h % 2), 64 * (h % 2) + 64)
                    for blk in range(SB):
                        at = (h // 2) * S + blk * P
                        ins = pe.matmul(ps[rows, 2, at:at + P], W[:, 2, blk, h], mM[:, 1, unit(h, blk)],
                                        start=True, stop=True)
                ins.then_inc(rp_done, 1)
                for h in range(HEADS):
                    rows = slice(64 * (h % 2), 64 * (h % 2) + 64)
                    for blk in range(SB):
                        at = (h // 2) * S + blk * P
                        pe.matmul(ps[rows, 3, at:at + P], W[:, 1, blk, h], mM[:, 1, unit(h, blk)], start=True, stop=False)
                        ins = pe.matmul(ps[rows, 3, at:at + P], tok[:, 3, blk, h * 64:(h + 1) * 64],
                                        mM[:, 2, unit(h, blk)], start=False, stop=True)
                ins.then_inc(intra_done, 1)
                pe.wait_ge(e_ready, 1)
                pe.wait_ge(rp_ready, 1)
                for c in range(1, NCH):
                    pe.wait_ge(state_ready, c)
                    if c < NCH - 1:
                        for pr in range(2):
                            ins = pe.matmul(ps[:, pr, (c % 4) * P:(c % 4 + 1) * P], QT[:, c % CPB, (c // CPB) * 2 + pr],
                                            St[:, c, pr], start=True, stop=True)
                        ins.then_inc(state_done, 1)
                    for pr in range(2):
                        ins = pe.matmul(ps[:, 4, pr * S + C * c:pr * S + C * (c + 1)], St[:, c, pr],
                                        Rp[:, pr, C * c:C * (c + 1)], start=True, stop=True)
                ins.then_inc(inter_done, 1)
                pe.wait_ge(bonus_ready, 1)
                heads64(6, t1).then_inc(bonus_done, 1)
                pe.wait_ge(yy_ready, 1)
                heads64(5, yy).then_inc(mean_done, 1)
                pe.wait_ge(sq_ready, 1)
                heads64(7, t2).then_inc(var_done, 1)


def stage_gla(nc, k, vecs, b, wa2_dram, L, y):
    with Stage(nc, "gla") as st:
        wa2 = st.sb("wa2", [N_GA, P])
        x1 = st.sb("x1", [P, S])
        x2 = st.sb("x2", [P, S])
        cum = st.sb("cum", [P, S])
        qt = st.sb("qt", [P, S])
        kt = st.sb("kt", [P, S])
        el = st.sb("el", [P, S])
        en = st.sb("en", [P, S])
        ktok = st.sb("ktok", [P, SB, P])
        sT = st.sb("sT", [P, HEADS, SB, P])
        EE = st.sb("EE", [P, CPB, SB, 256])
        St = st.sb("St", [P, NCH, 256])
        o = st.sb("o", [P, 2, S])
        sg = st.sb("sg", [P, 2, S])
        sq = st.sb("sq", [P, 2, S])
        lnv = st.sb("lnv", [P, 2, S])
        rstd = st.sb("rstd", [P, 2, S])
        ps = st.ps("ps", [P, 8, 512])
        (wa_loaded, dve_step, act_step, gate_done, abs_ready, ln_ready, sums_ready, exps_ready, qk_ready, k_done,
         k_copied, score_done, score_masked, intra_done, o_copied, e_done, states_ready, inter_done, sq_ready, sum_done,
         rstd_ready, sig_ready) = [st.sem(n) for n in (
             "wa_loaded dve_step act_step gate_done abs_ready ln_ready sums_ready exps_ready qk_ready k_done "
             "k_copied score_done score_masked intra_done o_copied e_done states_ready inter_done sq_ready sum_done "
             "rstd_ready sig_ready").split()]
        vec = lambda n, i=0: vecs[:, V2[n][0] + i:V2[n][0] + i + 1]
        vtok = b.tokm[:, :, 8:8 + 256]
        flat = lambda a: a.rearrange("p a s -> p (a s)")

        with nc.Block() as block:

            @block.sync
            def _(sp):
                sp.dma_start(wa2[:], wa2_dram[bass.ds(L, 1)].rearrange("a p n -> (a p) n")).then_inc(wa_loaded, 16)

            @block.vector
            def _(dve):
                ch = Chain(dve, dve_step)
                dve.wait_ge(gate_done, 1)
                ch.link(dve.tensor_scalar(x1[:], ps[:, 0, 0:S], vec("b_a"), None, ALU.add))
                ch.link(dve.tensor_scalar(x2[:], x1[:], -1.0, None, ALU.mult))
                dve.tensor_tensor(x2[:], x2[:], x1[:], ALU.max).then_inc(abs_ready, 1)
                ch.link(dve.tensor_scalar(x1[:], x1[:], 0.0, None, ALU.min))
                dve.wait_ge(ln_ready, 1)
                ch.link(dve.tensor_tensor(x1[:], x1[:], x2[:], ALU.subtract))
                ch.link(dve.tensor_scalar(x1[:], x1[:], 1.0 / 16, None, ALU.mult))
                dve.tensor_tensor_scan(cum[:], k.c("keep")[:, 0:S], x1[:], 0.0, ALU.mult, ALU.add).then_inc(sums_ready, 1)
                dve.wait_ge(exps_ready, 1)
                dve.scalar_tensor_tensor(qt[:], b.gl[:, 0], float(32 ** -0.5), el[:], ALU.mult, ALU.mult)
                dve.tensor_tensor(kt[:], b.gl[:, 1], en[:], ALU.mult).then_inc(qk_ready, 1)
                dve.wait_ge(score_done, 1)
                dve.tensor_tensor(sT[:], ps[:, 0:4, 0:SB * P].rearrange("p h (b c) -> p h b c", b=SB),
                                  bc(bc(k.c("cu_incl"), SB, 1), HEADS, 1), ALU.mult).then_inc(score_masked, 1)
                dve.wait_ge(e_done, 1)
                for c in range(NCH - 1):
                    j, blk = c % CPB, c // CPB
                    dst = St[:, 1] if c == 0 else EE[:, j, blk]
                    ins = dve.scalar_tensor_tensor(dst, ps[:, 4 + j, blk * 256:(blk + 1) * 256],
                                                   el[:, C * c + C - 1:C * c + C], k.c("gla_heads"), ALU.mult, ALU.mult)
                ch.link(ins)
                for c in range(1, NCH - 1):
                    ins = dve.scalar_tensor_tensor(St[:, c + 1], St[:, c], el[:, C * c + C - 1:C * c + C],
                                                   EE[:, c % CPB, c // CPB], ALU.mult, ALU.add)
                    ch.link(ins)
                dve.tensor_copy(St[:, 0, 0:1], St[:, NCH - 1, 0:1]).then_inc(states_ready, 1)
                dve.wait_ge(o_copied, 1)
                dve.wait_ge(inter_done, 1)
                psI = ps[:, 6].rearrange("p (a s) -> p a s", a=2)
                ch.link(dve.tensor_tensor(o[:, :, C:], o[:, :, C:], psI[:, :, C:], ALU.add))
                dve.tensor_tensor(sq[:], o[:], o[:], ALU.mult).then_inc(sq_ready, 1)
                dve.wait_ge(sig_ready, 1)
                ch.link(dve.tensor_tensor(sg[:], sg[:], b.gl[:, 2:4], ALU.mult))
                dve.wait_ge(rstd_ready, 1)
                for t in range(2):
                    ins = dve.scalar_tensor_tensor(o[:, t], o[:, t], vec("gla_norm", t), rstd[:, t], ALU.mult, ALU.mult)
                ch.link(ins)
                dve.tensor_tensor(y[:, 6:8], o[:], sg[:], ALU.mult)

            @block.scalar
            def _(act):
                ch = Chain(act, act_step)
                act.activation(sg[:], b.gl[:, 2:4], ACT.Sigmoid).then_inc(sig_ready, 1)
                act.wait_ge(abs_ready, 1)
                ch.link(act.activation(x2[:], x2[:], ACT.Exp, scale=-1.0))
                act.activation(x2[:], x2[:], ACT.Ln, bias=k.eps[1.0]).then_inc(ln_ready, 1)
                act.wait_ge(sums_ready, 1)
                act.activation(el[:], cum[:], ACT.Exp)
                act.activation(en[:], cum[:], ACT.Exp, scale=-1.0).then_inc(exps_ready, 1)
                act.wait_ge(k_done, 1)
                act.activation(flat(ktok[:]), ps[:, 7, 0:SB * P], ACT.Copy).then_inc(k_copied, 1)
                act.wait_ge(intra_done, 1)
                act.activation(flat(o[:]), ps[:, 0], ACT.Copy).then_inc(o_copied, 1)
                act.wait_ge(sum_done, 1)
                ch.link(act.activation(flat(lnv[:]), ps[:, 1], ACT.Ln, bias=k.eps[RMS_EPS], scale=1.0 / 64))
                act.activation(rstd[:], lnv[:], ACT.Exp, scale=-0.5).then_inc(rstd_ready, 1)

            @block.tensor
            def _(pe):
                pe.wait_ge(wa_loaded, 16)
                pe.matmul(ps[:, 0, 0:S], wa2[:], b.ga[0:N_GA, :], start=True, stop=True).then_inc(gate_done, 1)
                pe.wait_ge(qk_ready, 1)
                for blk in range(SB):
                    ins = pe.transpose(ps[:, 7, blk * P:(blk + 1) * P], kt[:, blk * P:(blk + 1) * P], k.c("ident"))
                ins.then_inc(k_done, 1)
                for blk in range(SB):
                    cols = slice(blk * P, (blk + 1) * P)
                    for h in range(HEADS):
                        rows = slice(32 * h, 32 * h + 32)
                        ins = pe.matmul(ps[:, h, cols], kt[rows, cols], qt[rows, cols], start=True, stop=True,
                                        tile_position=(32 * h, 0) if h == 3 else None)
                ins.then_inc(score_done, 1)
                pe.wait_ge(k_copied, 1)
                for blk in range(SB):
                    for j in range(CPB):
                        rows = slice(C * j, C * j + C)
                        ins = pe.matmul(ps[:, 4 + j, blk * 256:(blk + 1) * 256], ktok[rows, blk], vtok[rows, blk],
                                        start=True, stop=True, tile_position=(32 * j, 0) if j == 3 else None)
                ins.then_inc(e_done, 1)
                pe.wait_ge(score_masked, 1)
                for h in range(HEADS):
                    rows = slice(64 * (h % 2), 64 * (h % 2) + 64)
                    for blk in range(SB):
                        at = (h // 2) * S + blk * P
                        ins = pe.matmul(ps[rows, 0, at:at + P], vtok[:, blk, h * 64:(h + 1) * 64], sT[:, h, blk],
                                        start=True, stop=True)
                ins.then_inc(intra_done, 1)
                pe.wait_ge(states_ready, 1)
                for c in range(1, NCH):
                    for pr in range(2):
                        ins = pe.matmul(ps[:, 6, pr * S + C * c:pr * S + C * (c + 1)], St[:, c, pr * P:(pr + 1) * P],
                                        qt[:, C * c:C * (c + 1)], start=True, stop=True)
                ins.then_inc(inter_done, 1)
                pe.wait_ge(sq_ready, 1)
                for t in range(2):
                    ins = pe.matmul(ps[:, 1, t * S:(t + 1) * S], k.c("ones64"), sq[:, t], start=True, stop=True)
                ins.then_inc(sum_done, 1)


def stage_output2(nc, k, L, vecs, y, w_dram):
    with Stage(nc, "output2") as st:
        w = st.sb("w", [P, DT, DT, P])
        xr = st.sb("xr", [P, DT, S])
        ps = st.ps("ps", [P, 4, 512])
        w_loaded = [st.sem(f"w_loaded{i}") for i in range(4)]
        mm_done, added, dve_step = st.sem("mm_done"), st.sem("added"), st.sem("dve_step")
        g, bb = V2["ln1_g"][0], V2["ln1_b"][0]
        n_vec, n_act, n_pe, normed = norm_engines(k, st, xr, k.x, vecs[:, g:g + DT], LN_EPS, vecs[:, bb:bb + DT])
        with nc.Block() as block:

            @block.sync
            def _(sp):
                for i in range(4):
                    sp.dma_start(w[:, 2 * i:2 * i + 2], w_dram[bass.ds(L, 1), :, 2 * i * DT * P:(2 * i + 2) * DT * P]
                                 .rearrange("a p (m k c) -> (a p) m k c", m=2, k=DT)).then_inc(w_loaded[i], 16)

            @block.vector
            def _(dve):
                for m in range(4):
                    dve.wait_ge(mm_done, m + 1)
                    xm = lambda a: a[:, 2 * m:2 * m + 2].rearrange("p a s -> p (a s)")
                    dve.scalar_tensor_tensor(xm(xr), xm(k.x), ALPHA, ps[:, m], ALU.mult, ALU.add).then_inc(added, 1)
                dve.wait_ge(added, 4)
                n_vec(dve, Chain(dve, dve_step))

            @block.scalar
            def _(act):
                n_act(act)

            @block.tensor
            def _(pe):
                for m in range(DT):
                    if m % 2 == 0:
                        pe.wait_ge(w_loaded[m // 2], 16)
                    for kk in range(DT):
                        ins = pe.matmul(ps[:, m // 2, (m % 2) * S:(m % 2 + 1) * S], w[:, m, kk], y[:, kk],
                                        start=kk == 0, stop=kk == DT - 1)
                    if m % 2:
                        ins.then_inc(mm_done, 1)
                pe.wait_ge(added, 4)
                n_pe(pe)


class Buffers:
    pass


def make_buffers(nc, ctx):
    b = Buffers()

    def sb(name, shape):
        return ctx.enter_context(nc.sbuf_tensor(name, shape, F32))

    b.vecs = sb("vecs2", [P, N_V2])
    b.y = sb("y2", [P, DT, S])
    b.z = sb("z2", [P, 4, S])
    b.xbc = sb("xbc2", [P, 6, S + 3])
    b.rw = sb("rw2", [P, 7, S + 1])
    b.gl = sb("gl2", [P, 4, S])
    b.ga = sb("ga2", [P, S])
    b.tokm = sb("tokm2", [P, SB, N_TOKM])
    with Stage(nc, "pads") as st:
        padded = st.sem("padded")
        with nc.Block() as block:

            @block.vector
            def _(dve):
                dve.memset(b.xbc[:, :, 0:3], 0.0).then_inc(padded, 1)
                dve.memset(b.rw[:, :, 0:1], 0.0).then_inc(padded, 1)
                dve.wait_ge(padded, 2)
    return b


class Routes:
    pass


def make_routes(nc, ctx):
    m = Routes()

    def sb(name, shape, dt=F32):
        return ctx.enter_context(nc.sbuf_tensor(name, shape, dt))

    m.parts = sb("parts", [P, 3, SB, D], BF16)
    m.slot = sb("slot", [P, SB, N_PASS])
    m.gate = sb("gate", [P, SB, N_PASS])
    m.over_expert = sb("over_expert", [P, N_OVER], I32)
    m.n_over = sb("n_over", [P, 1], I32)
    return m


def stage_route(nc, k, L, vecs, w_dram, m):
    with Stage(nc, "route") as st:
        w = st.sb("w", [P, DT, N_ROUTE])
        lg = st.sb("lg", [P, SB, N_ROUTE])
        r1 = st.sb("r1", [P, SB, D])
        one = st.sb("one", [P, 12, SB])
        grp = st.sb("grp", [P, 4, SB, N_GROUPS])
        sel = st.sb("sel", [P, SB, EPG, N_GROUPS])
        e8 = st.sb("e8", [P, 8, SB, EPG])
        A = st.sb("A", [P, SB, N_EXP])
        row = st.sb("row", [P, 5, N_EXP])
        big = st.sb("big", [P, 4, N_OVER, N_EXP])
        bigt = st.sb("bigt", [P, SB, N_OVER, N_EXP])
        onef = st.sb("onef", [P, 3, N_OVER])
        ps = st.ps("ps", [P, 4, 512])
        psl = st.ps("psl", [P, 512])
        psr = st.ps("psr", [P, 512])
        (w_loaded, dve_step, xT_done, logits_done, hi_ready, mid_ready, rest_ready, parts_ready, gexp_pre, gexp_ready,
         eexp_pre, eexp_ready, assigned, ranked) = [st.sem(n) for n in (
             "w_loaded dve_step xT_done logits_done hi_ready mid_ready rest_ready parts_ready gexp_pre gexp_ready "
             "eexp_pre eexp_ready assigned ranked").split()]
        b0 = V2["b_route"][0]
        G4, OH, GX, GE = range(4)

        with nc.Block() as block:

            @block.sync
            def _(sp):
                sp.dma_start(w[:], w_dram[bass.ds(L, 1)].rearrange("a p (k c) -> (a p) k c", k=DT)).then_inc(w_loaded, 16)

            @block.vector
            def _(dve):
                ch = Chain(dve, dve_step)
                link = ch.link

                def one_hot(dst, key, x, mx, n):
                    link(dve.tensor_tensor(key, x, bc(mx, n, 2), ALU.is_equal))
                    link(dve.tensor_tensor(key, key, bc(k.c("rank")[:, 0:n], SB, 1), ALU.mult))
                    link(dve.reduce_max(one[:, 11], key, AX.X))
                    link(dve.tensor_tensor(dst, key, bc(one[:, 11], n, 2), ALU.is_equal))

                dve.wait_ge(logits_done, 1)
                link(dve.tensor_tensor(lg[:], psl[:, 0:SB * N_ROUTE].rearrange("p (b c) -> p b c", b=SB),
                                       bc(vecs[:, b0:b0 + N_ROUTE], SB, 1), ALU.add))
                gl = lg[:, :, 0:N_GROUPS]
                link(dve.reduce_max(one[:, 0], gl, AX.X))
                one_hot(grp[:, OH], grp[:, G4], gl, one[:, 0], N_GROUPS)
                dve.tensor_tensor(grp[:, GX], gl, bc(one[:, 0], N_GROUPS, 2), ALU.subtract).then_inc(gexp_pre, 1)
                link(dve.tensor_tensor(sel[:].rearrange("p b e g -> p b g e"),
                                       lg[:, :, N_GROUPS:].rearrange("p b (g e) -> p b g e", g=N_GROUPS),
                                       bc(grp[:, OH], EPG, 3), ALU.mult))
                link(dve.tensor_reduce(e8[:, 0], sel[:], AX.X, ALU.add))
                link(dve.reduce_max(one[:, 1], e8[:, 0], AX.X))
                one_hot(e8[:, 1], e8[:, 3], e8[:, 0], one[:, 1], EPG)
                link(dve.scalar_tensor_tensor(e8[:, 4], e8[:, 1], NEG, e8[:, 0], ALU.mult, ALU.add))
                link(dve.reduce_max(one[:, 2], e8[:, 4], AX.X))
                one_hot(e8[:, 2], e8[:, 3], e8[:, 4], one[:, 2], EPG)
                dve.tensor_tensor(one[:, 3], one[:, 2], one[:, 1], ALU.subtract).then_inc(eexp_pre, 1)
                dve.wait_ge(gexp_ready, 1)
                link(dve.tensor_reduce(one[:, 4], grp[:, GE], AX.X, ALU.add))
                link(dve.reciprocal(one[:, 5], one[:, 4]))
                dve.wait_ge(eexp_ready, 1)
                link(dve.tensor_scalar(one[:, 7], one[:, 6], 1.0, None, ALU.add))
                link(dve.reciprocal(one[:, 8], one[:, 7]))
                link(dve.tensor_tensor(one[:, 9], one[:, 8], one[:, 5], ALU.mult))
                link(dve.tensor_tensor(one[:, 10], one[:, 9], one[:, 6], ALU.mult))
                link(dve.tensor_tensor(e8[:, 5], e8[:, 1], e8[:, 2], ALU.add))
                link(dve.tensor_tensor(e8[:, 6], e8[:, 1], bc(one[:, 9], EPG, 2), ALU.mult))
                link(dve.tensor_tensor(e8[:, 7], e8[:, 2], bc(one[:, 10], EPG, 2), ALU.mult))
                link(dve.tensor_tensor(e8[:, 6], e8[:, 6], e8[:, 7], ALU.add))
                for blk in range(SB):
                    grid = lambda a: a[:, blk].rearrange("p (g e) -> p g e", g=N_GROUPS)
                    ins = dve.tensor_tensor(grid(A), bc(e8[:, 5, blk], N_GROUPS, 1), bc(grp[:, OH, blk], EPG, 2), ALU.mult)
                    link(dve.tensor_tensor(m.gate[:, blk, 0:N_EXP].rearrange("p (g e) -> p g e", g=N_GROUPS),
                                           bc(e8[:, 6, blk], N_GROUPS, 1), bc(grp[:, OH, blk], EPG, 2), ALU.mult))
                dve.tensor_copy(row[:, 0], A[:, 1]).then_inc(assigned, 1)
                dve.wait_ge(hi_ready, 1)
                x4 = ps[:].rearrange("p (b q) n -> p b (q n)", b=SB)
                dve.tensor_tensor(r1[:], x4, m.parts[:, 0], ALU.subtract).then_inc(rest_ready, 1)
                dve.wait_ge(ranked, 1)
                rank = psr[:, 0:SB * N_EXP].rearrange("p (b e) -> p b e", b=SB)
                slot = m.slot[:, :, 0:N_EXP]
                link(dve.scalar_tensor_tensor(slot, rank, 1.0, A[:], ALU.add, ALU.mult))
                link(dve.tensor_scalar(slot, slot, -1.0, None, ALU.add))
                cnt = psr[:, SB * N_EXP:(SB + 1) * N_EXP]
                link(dve.tensor_scalar(row[:, 1], cnt, float(SLOTS), None, ALU.is_gt))
                for n in (2, 3):
                    link(dve.tensor_scalar(row[:, 2], cnt, float(n * SLOTS), None, ALU.is_gt))
                    link(dve.tensor_tensor(row[:, 1], row[:, 1], row[:, 2], ALU.add))
                link(dve.tensor_tensor_scan(row[:, 3], k.c("ones")[:, 0:N_EXP], row[:, 1], 0.0, ALU.mult, ALU.add))
                link(dve.tensor_tensor(row[:, 4], row[:, 3], row[:, 1], ALU.subtract))
                link(dve.tensor_copy(m.n_over[:], row[:, 3, N_EXP - 1:N_EXP]))
                grid = lambda n: k.c(n).rearrange("p (s e) -> p s e", s=N_OVER)
                link(dve.tensor_tensor(big[:, 0], bc(row[:, 3], N_OVER, 1), grid("steps"), ALU.is_gt))
                link(dve.tensor_tensor(big[:, 1], bc(row[:, 4], N_OVER, 1), grid("steps"), ALU.is_le))
                link(dve.tensor_tensor(big[:, 0], big[:, 0], big[:, 1], ALU.mult))
                link(dve.tensor_tensor(big[:, 1], big[:, 0], grid("experts"), ALU.mult))
                link(dve.tensor_reduce(onef[:, 0], big[:, 1], AX.X, ALU.add))
                link(dve.tensor_copy(m.over_expert[:], onef[:, 0]))
                link(dve.tensor_tensor(big[:, 2], grid("steps"), bc(row[:, 4], N_OVER, 1), ALU.subtract))
                link(dve.scalar_tensor_tensor(big[:, 2], big[:, 2], 1.0, big[:, 0], ALU.add, ALU.mult))
                link(dve.tensor_reduce(onef[:, 1], big[:, 2], AX.X, ALU.add))
                link(dve.tensor_scalar(onef[:, 2], onef[:, 1], float(SLOTS), 1.0, ALU.mult, ALU.add))
                for blk in range(SB):
                    link(dve.scalar_tensor_tensor(bigt[:, blk], bc(m.slot[:, blk, 0:N_EXP], N_OVER, 1), 1.0, big[:, 0],
                                                  ALU.add, ALU.mult))
                    link(dve.tensor_reduce(m.slot[:, blk, N_EXP:], bigt[:, blk], AX.X, ALU.add))
                    link(dve.tensor_tensor(m.slot[:, blk, N_EXP:], m.slot[:, blk, N_EXP:], onef[:, 2], ALU.subtract))
                    link(dve.tensor_tensor(bigt[:, blk], bc(m.gate[:, blk, 0:N_EXP], N_OVER, 1), big[:, 0], ALU.mult))
                    link(dve.tensor_reduce(m.gate[:, blk, N_EXP:], bigt[:, blk], AX.X, ALU.add))
                dve.wait_ge(mid_ready, 1)
                dve.tensor_tensor(r1[:], r1[:], m.parts[:, 1], ALU.subtract).then_inc(rest_ready, 1)

            @block.scalar
            def _(act):
                act.wait_ge(gexp_pre, 1)
                act.activation(grp[:, GE], grp[:, GX], ACT.Exp).then_inc(gexp_ready, 1)
                act.wait_ge(xT_done, 1)
                x4 = ps[:].rearrange("p (b q) n -> p b (q n)", b=SB)
                act.activation(m.parts[:, 0], x4, ACT.Copy).then_inc(hi_ready, 1)
                act.wait_ge(eexp_pre, 1)
                act.activation(one[:, 6], one[:, 3], ACT.Exp).then_inc(eexp_ready, 1)
                act.wait_ge(rest_ready, 1)
                act.activation(m.parts[:, 1], r1[:], ACT.Copy).then_inc(mid_ready, 1)
                act.wait_ge(rest_ready, 2)
                act.activation(m.parts[:, 2], r1[:], ACT.Copy).then_inc(parts_ready, 1)

            @block.tensor
            def _(pe):
                pe.wait_ge(w_loaded, 16)
                for blk in range(SB):
                    for kk in range(DT):
                        ins = pe.matmul(psl[:, blk * N_ROUTE:(blk + 1) * N_ROUTE], k.x[:, kk, blk * P:(blk + 1) * P],
                                        w[:, kk], start=kk == 0, stop=kk == DT - 1)
                ins.then_inc(logits_done, 1)
                for blk in range(SB):
                    for t in range(DT):
                        at = blk * D + t * P
                        ins = pe.transpose(ps[:, at // 512, at % 512:at % 512 + P], k.x[:, t, blk * P:(blk + 1) * P],
                                           k.c("ident"))
                ins.then_inc(xT_done, 1)
                pe.wait_ge(assigned, 1)
                pe.matmul(psr[:, 0:N_EXP], k.c("lt"), A[:, 0], start=True, stop=True)
                pe.matmul(psr[:, N_EXP:2 * N_EXP], k.c("lt"), A[:, 1], start=True, stop=False)
                pe.matmul(psr[:, N_EXP:2 * N_EXP], k.c("ones"), A[:, 0], start=False, stop=True)
                pe.matmul(psr[:, 2 * N_EXP:3 * N_EXP], k.c("ones"), A[:, 0], start=True, stop=False)
                pe.matmul(psr[:, 2 * N_EXP:3 * N_EXP], k.c("ones"), A[:, 1], start=False, stop=True).then_inc(ranked, 1)


def stage_experts(nc, k, L, m, wg_dram, wu_dram, wd_dram, first, n, name, base_scale):
    with Stage(nc, name) as st:
        wgu = st.sb("wgu", [P, 2, 2, DT, EFF])
        wd = st.sb("wd", [P, 2, 4, D])
        selg = st.sb("selg", [P, 2, SB, P])
        selb = st.sb("selb", [P, 2, SB, SLOTS], BF16)
        selT = st.sb("selT", [P, 2, S])
        xc = st.sb("xc", [P, DT, SLOTS])
        sig = st.sb("sig", [P, S])
        hh = st.sb("hh", [P, S])
        hT = st.sb("hT", [P, 2, P])
        yc = st.sb("yc", [P, 512])
        zero = st.sb("zero", [P, 512])
        psG = st.ps("psG", [P, 512])
        psX = st.ps("psX", [P, 512])
        psS = st.ps("psS", [P, 512])
        psD = st.ps("psD", [P, 512])
        psY = st.ps("psY", [P, 4, 512])
        gu_loaded = [st.sem("gu_loaded0"), st.sem("gu_loaded1")]
        d_loaded = [st.sem("d_loaded0"), st.sem("d_loaded1")]
        (dve_step, zero_ready, sel_ready, gathered, xc_ready, gu_done, sig_ready, h_ready, selT_done, selT_ready,
         hT_done, hT_ready, down_done, yc_ready, scattered, y_done) = [st.sem(s) for s in (
             "dve_step zero_ready sel_ready gathered xc_ready gu_done sig_ready h_ready selT_done selT_ready "
             "hT_done hT_ready down_done yc_ready scattered y_done").split()]
        main = first == 0

        def passes(eng, body):
            body(0, 0, True, False)
            body(1, 1, False, False)
            with eng.Fori(1, n // 2 - 1) as it:
                body(2 * it, 0, False, False)
                body(2 * it + 1, 1, False, False)
            body(n - 2, 0, False, False)
            body(n - 1, 1, False, True)

        with nc.Block() as block:

            @block.sync
            def _(sp):
                def load(e, par, is_first, is_last):
                    if main:
                        at = L * N_EXP + e
                    else:
                        at = L * N_EXP + sp.value_load(m.over_expert[0:1, bass.ds(e, 1)], min_val=0, max_val=N_EXP - 1)
                    if not (isinstance(e, int) and e < 2):
                        sp.wait_ge(gu_done, e - 1)
                    for i, w in enumerate((wg_dram, wu_dram)):
                        sp.dma_start(wgu[:, par, i], w[bass.ds(at, 1)].rearrange("a (k p) n -> (a p) k n", p=P))\
                            .then_inc(gu_loaded[par], 16)
                    if not (isinstance(e, int) and e < 2):
                        sp.wait_ge(down_done, e - 1)
                    sp.dma_start(wd[:, par], wd_dram[bass.ds(at, 1)].rearrange("a (t p) n -> (a p) t n", p=P))\
                        .then_inc(d_loaded[par], 16)

                passes(sp, load)

            @block.vector
            def _(dve):
                ch = Chain(dve, dve_step)

                def select(e, par):
                    if not (isinstance(e, int) and e < 2):
                        dve.wait_ge(selT_done, e - 1)
                    for blk in range(SB):
                        col = m.slot[:, blk, bass.ds(first + e, 1)]
                        dve.tensor_scalar(selb[:, par, blk], k.c("slots")[:, 0:SLOTS], col, None, ALU.is_equal)
                        ins = dve.tensor_scalar(selg[:, par, blk], k.c("slots"), col, m.gate[:, blk, bass.ds(first + e, 1)],
                                                ALU.is_equal, ALU.mult)
                    ins.then_inc(sel_ready, 1)

                def step(e, par, is_first, is_last):
                    if not is_last:
                        select(e + 1, 1 - par)
                    dve.wait_ge(sig_ready, e + 1)
                    dve.tensor_tensor(sig[:], sig[:], psG[:, 0:S], ALU.mult).then_inc(dve_step, 1)
                    dve.wait_ge(dve_step, e + 1)
                    dve.tensor_tensor(hh[:], sig[:], psG[:, S:2 * S], ALU.mult).then_inc(h_ready, 1)

                dve.memset(zero[:], 0.0).then_inc(zero_ready, 1)
                select(0, 0)
                passes(dve, step)
                dve.wait_ge(y_done, 1)
                xf = k.x[:].rearrange("p (b t) s -> p b (t s)", b=4)
                dve.scalar_tensor_tensor(xf, xf, base_scale, psY[:], ALU.mult, ALU.add)

            @block.scalar
            def _(act):
                def take(e):
                    act.wait_ge(gathered, e + 1)
                    act.activation(xc[:].rearrange("p t c -> p (t c)"), psX[:], ACT.Copy).then_inc(xc_ready, 1)

                def step(e, par, is_first, is_last):
                    act.wait_ge(gu_done, e + 1)
                    if not is_first:
                        act.wait_ge(h_ready, e)
                    act.activation(sig[:], psG[:, 0:S], ACT.Sigmoid).then_inc(sig_ready, 1)
                    act.wait_ge(selT_done, e + 1)
                    if not (isinstance(e, int) and e < 2):
                        act.wait_ge(scattered, e - 1)
                    act.activation(selT[:, par], psS[:, 0:S], ACT.Copy).then_inc(selT_ready, 1)
                    if not is_last:
                        take(e + 1)
                    act.wait_ge(hT_done, e + 1)
                    act.activation(hT[:].rearrange("p c n -> p (c n)"), psS[:, S:2 * S], ACT.Copy).then_inc(hT_ready, 1)
                    act.wait_ge(down_done, e + 1)
                    act.activation(yc[:], psD[:], ACT.Copy).then_inc(yc_ready, 1)

                take(0)
                passes(act, step)

            @block.tensor
            def _(pe):
                def gather(e, par):
                    pe.wait_ge(sel_ready, e + 1)
                    for t in range(DT):
                        for i in range(3):
                            for blk in range(SB):
                                ins = pe.matmul(psX[:, t * SLOTS:(t + 1) * SLOTS], m.parts[:, i, blk, t * P:(t + 1) * P],
                                                selb[:, par, blk], start=i == 0 and blk == 0, stop=i == 2 and blk == SB - 1)
                    ins.then_inc(gathered, 1)

                def scatter(par, e):
                    pe.wait_ge(yc_ready, e + 1)
                    for t in range(4):
                        for i in range(2):
                            rows = slice(SLOTS * i, SLOTS * i + SLOTS)
                            ins = pe.matmul(psY[:, 2 * i + t // 2, (t % 2) * S:(t % 2 + 1) * S],
                                            yc[rows, t * P:(t + 1) * P], selT[rows, par], start=False, stop=False)
                    ins.then_inc(scattered, 1)

                def step(e, par, is_first, is_last):
                    pe.wait_ge(gu_loaded[par], (e + (2 - par)) * 16)
                    pe.wait_ge(xc_ready, e + 1)
                    if not is_first:
                        pe.wait_ge(h_ready, e)
                    for kk in range(DT):
                        for j in range(2):
                            out = psG[SLOTS * j:SLOTS * (j + 1), :].rearrange("p (g c) -> p g c", g=2)
                            ins = pe.matmul(out, xc[:, kk], wgu[:, par, :, kk, j * S:(j + 1) * S],
                                            start=kk == 0, stop=kk == DT - 1)
                    ins.then_inc(gu_done, 1)
                    if not is_first:
                        pe.wait_ge(hT_ready, e)
                    for blk in range(SB):
                        ins = pe.transpose(psS[:, blk * P:(blk + 1) * P], selg[:, par, blk], k.c("ident"))
                    ins.then_inc(selT_done, 1)
                    if not is_last:
                        gather(e + 1, 1 - par)
                    pe.wait_ge(h_ready, e + 1)
                    pe.wait_ge(selT_ready, e + 1)
                    for c in range(2):
                        ins = pe.transpose(psS[:, S + c * P:S + (c + 1) * P], hh[:, c * P:(c + 1) * P], k.c("ident"))
                    ins.then_inc(hT_done, 1)
                    if not is_first:
                        scatter(1 - par, e - 1)
                    pe.wait_ge(d_loaded[par], half_count(e, par))
                    pe.wait_ge(hT_ready, e + 1)
                    for j in range(2):
                        for c in range(2):
                            for i in range(2):
                                rows = slice(SLOTS * i, SLOTS * i + SLOTS)
                                ins = pe.matmul(psD[rows, :], hT[:, c, j * SLOTS:(j + 1) * SLOTS],
                                                wd[:, par, 2 * j + c, i * 512:(i + 1) * 512],
                                                start=j == 0 and c == 0, stop=j == 1 and c == 1)
                    ins.then_inc(down_done, 1)

                def half_count(e, par):
                    return (e + (2 - par)) * 8

                pe.wait_ge(zero_ready, 1)
                for i in range(4):
                    pe.matmul(psY[:, i], k.c("ident"), zero[:], start=True, stop=False)
                gather(0, 0)
                passes(pe, step)
                scatter((n - 1) % 2, n - 1)
                for i in range(4):
                    ins = pe.matmul(psY[:, i], k.c("ident"), zero[:], start=False, stop=True)
                ins.then_inc(y_done, 1)


def stage_norm2(nc, k, vecs):
    with Stage(nc, "norm2") as st:
        tmp = st.sb("tmp", [P, DT, S])
        dve_step = st.sem("dve_step")
        g, b = V2["ln2_g"][0], V2["ln2_b"][0]
        n_vec, n_act, n_pe, normed = norm_engines(k, st, k.x, tmp, vecs[:, g:g + DT], LN_EPS, vecs[:, b:b + DT])
        with nc.Block() as block:

            @block.vector
            def _(dve):
                n_vec(dve, Chain(dve, dve_step))
                dve.wait_ge(normed, DT)
                dve.tensor_copy(k.x[:], tmp[:])

            @block.scalar
            def _(act):
                n_act(act)

            @block.tensor
            def _(pe):
                n_pe(pe)


def program(nc, a, out):
    with ExitStack() as whole:
        k = Kit(nc, whole)
        stage_load(nc, k, a["x_t"], a["const"])

        with ExitStack() as first:
            def sb(name, shape):
                return first.enter_context(nc.sbuf_tensor(name, shape, F32))

            vecs, proj = sb("vecs1", [P, N_V1]), sb("proj1", [P, N_IN1_TILES, S])
            vtok, y = sb("vtok1", [P, SB, P]), sb("y1", [P, DT, S])
            with nc.Fori(0, DEPTH) as L:
                stage_project1(nc, k, L, a["w_in1"], a["vec1"], vecs, proj, vtok)
                stage_mixers1(nc, k, L, proj, vtok, vecs, a["w_uq"], a["w_ukv"], a["pool_w"], y)
                stage_output1(nc, k, L, vecs, y, a["w_o"])
                stage_ffn1(nc, k, L, vecs, a["w_gu"], a["w_dn"])
            stage_norm(nc, k, "final_norm", a["fin_g"], 0, None, DT, RMS_EPS)

        stage_norm(nc, k, "ln_in", a["ln_in"], 0, DT, 2 * DT, LN_EPS)
        b, m = make_buffers(nc, whole), make_routes(nc, whole)
        experts = a["moe_gate"], a["moe_up"], a["moe_down"]
        with nc.Fori(0, DEPTH) as L:
            stage_project2(nc, k, L, a["w_in2"], a["vec2"], b.vecs, b)
            stage_ssd(nc, k, b.vecs, b, b.y)
            stage_rwkv(nc, k, b.vecs, b, a["lr2"], L, b.y)
            stage_gla(nc, k, b.vecs, b, a["wa2"], L, b.y)
            stage_output2(nc, k, L, b.vecs, b.y, a["w_out"])
            stage_route(nc, k, L, b.vecs, a["w_route"], m)
            stage_experts(nc, k, L, m, *experts, 0, N_EXP, "experts", ALPHA)
            n_over = nc.values_load(m.n_over[0:1, 0:1], min_val=0, max_val=N_OVER)
            with nc.If(n_over > 0):
                stage_experts(nc, k, L, m, *experts, N_EXP, N_OVER, "further", 1.0)
            with nc.Else():
                nc.all_engine_barrier()
            stage_norm2(nc, k, b.vecs)
        stage_store(nc, k, out)


def feat_cols(a):
    return np.swapaxes(a.reshape(*a.shape[:-1], -1, P), -1, -2)


def rows_to_all(a):
    return np.broadcast_to(a[:, None, :], (a.shape[0], P, a.shape[1]))


def tiles_kc(w, cols):
    L, K, _ = w.shape
    parts = [np.transpose(w[:, :, c].reshape(L, K // P, P, len(c)), (0, 2, 1, 3)).reshape(L, P, -1) for c in cols]
    return np.ascontiguousarray(np.concatenate(parts, 2))


def lay_out1(i):
    r = np.arange
    kr = list(r(384, 400)) + list(r(400, 416))
    kr_swapped = list(r(400, 416)) + list(r(384, 400))
    conv, pool, qs = 416, 416 + 768, 416 + 768 + 256
    head = lambda h: list(r(qs + 64 * h, qs + 64 * h + 64))
    cols = [list(r(0, 128)), list(r(128, 256)), list(r(256, 384)), kr + kr_swapped]
    cols += [list(r(conv + 128 * t, conv + 128 * t + 128)) for t in range(6)]
    cols += [list(r(pool + 128 * t, pool + 128 * t + 128)) for t in range(2)]
    cols += [head(0) + head(2), head(1) + head(3), list(r(qs + 256, qs + 384)), list(r(qs + 384, qs + 512))]
    uq = [96 * h + c for h in range(HEADS) for c in list(r(96)) + list(r(80, 96)) + list(r(64, 80))]
    L = DEPTH
    w_uq = np.transpose(i["w_uq"][:, :, uq].reshape(L, 2, P, 512), (0, 2, 1, 3)).reshape(L, P, -1)
    ukv = [128 * h + c for h in range(HEADS) for c in r(64)] + [128 * h + 64 + c for h in range(HEADS) for c in r(64)]
    pool_w = np.transpose(i["pool_w"].reshape(L, 2, P, 64), (0, 2, 1, 3)).reshape(L, P, -1)
    gate, up = i["w_gate_up"][:, :, :D_FF], i["w_gate_up"][:, :, D_FF:]
    gu = np.stack([gate.reshape(L, DT, P, FT, P), up.reshape(L, DT, P, FT, P)], 0)
    gu = np.transpose(gu, (1, 4, 3, 0, 2, 5)).reshape(L, FT, P, -1)
    down = np.transpose(i["w_down"].reshape(L, FT, P, DT, P), (0, 3, 2, 1, 4)).reshape(L, DT, P, -1)
    vec = [feat_cols(i["attn_norm"]), feat_cols(i["mla_q_norm"]), feat_cols(i["mla_kv_norm"]),
           *[feat_cols(i["conv_w"][:, t]) for t in range(3)], feat_cols(i["pool_scale"]), feat_cols(i["mix_norm"]),
           feat_cols(i["ffn_norm"]), rows_to_all(i["swa_sinks"])]
    c = np.ascontiguousarray
    return {
        "x_t": c(feat_cols(np.transpose(i["x"][0])[None].reshape(D, S).T).transpose(1, 2, 0).reshape(P, DT * S)),
        "w_in1": tiles_kc(i["w_in"], cols),
        "vec1": c(np.concatenate(vec, 2)),
        "w_uq": c(w_uq),
        "w_ukv": c(i["w_ukv"][:, :, ukv]),
        "pool_w": c(pool_w),
        "w_o": tiles_kc(i["w_o"], [list(r(128 * m, 128 * m + 128)) for m in range(DT)]),
        "w_gu": c(gu),
        "w_dn": c(down),
        "fin_g": c(feat_cols(i["final_norm"])),
    }


def lay_out2(i):
    r = lambda a, b: list(range(a, b))
    tiles = [r(P * t, P * t + P) for t in range(10)] + [r(1288 + P * t, 1288 + P * t + P) for t in range(7)]
    tiles += [r(2184, 2312), r(2312, 2440), r(2696, 2824), r(2824, 2952), r(2952, 2968), r(1280, 1288) + r(2440, 2696)]
    L = DEPTH
    c = np.ascontiguousarray
    vec = [*[feat_cols(i["ssd_conv_w"][:, t]) for t in range(4)], feat_cols(i["ssd_conv_b"]),
           rows_to_all(i["ssd_dt_bias"]), rows_to_all(i["ssd_a_log"]), feat_cols(np.repeat(i["ssd_d"], 64, 1)),
           feat_cols(i["ssd_norm_g"]), feat_cols(i["rwkv_mu"]), feat_cols(i["rwkv_w0"]), feat_cols(i["rwkv_a0"]),
           feat_cols(i["rwkv_k_k"]), feat_cols(i["rwkv_k_a"]), feat_cols(i["rwkv_r_k"].reshape(L, 256)),
           feat_cols(i["rwkv_ln_g"]), feat_cols(i["rwkv_ln_b"]), feat_cols(i["gla_b_a"]), feat_cols(i["gla_norm_g"]),
           feat_cols(i["ln1_g"]), feat_cols(i["ln1_b"]), feat_cols(i["ln2_g"]), feat_cols(i["ln2_b"]),
           rows_to_all(i["moe_b_rg"]), rows_to_all(i["moe_b_re"])]
    route = np.concatenate([i["moe_w_rg"], i["moe_w_re"]], 2)
    return {
        "w_in2": tiles_kc(i["w_in"], tiles),
        "vec2": c(np.concatenate(vec, 2)),
        "lr2": c(np.concatenate([i["rwkv_w2"], i["rwkv_a2"], i["rwkv_g2"]], 1)),
        "wa2": c(i["gla_w_a2"]),
        "w_out": tiles_kc(i["w_out"], [r(P * m, P * m + P) for m in range(DT)]),
        "w_route": tiles_kc(route, [r(0, N_ROUTE)]),
        "ln_in": c(np.concatenate([feat_cols(i["ln_in_g"]), feat_cols(i["ln_in_b"])], 1)),
    }


def kernel(**inputs):
    import numpy as _np
    import concourse.bacc as _bacc
    from concourse import mybir as _mybir
    from concourse.bass_utils import run_bass_kernel_spmd as _run

    given = {n: _np.asarray(v) for n, v in inputs.items()}
    second = {n[:-2]: v for n, v in given.items() if n.endswith("_2")}
    arrays = {**lay_out1(given), **lay_out2(second), "const": CONST_ARRAY}
    for n in ("gate", "up", "down"):
        w = second["moe_w_" + n]
        arrays["moe_" + n] = w.reshape((-1,) + w.shape[2:])
    nc = _bacc.Bacc("TRN2", target_bir_lowering=False, num_devices=1)
    aps = {n: nc.dram_tensor(f"in_{n}", v.shape, _mybir.dt.from_np(v.dtype), kind="ExternalInput").ap()
           for n, v in arrays.items()}
    out = nc.dram_tensor("out_t", (P, DT * S), _mybir.dt.float32, kind="ExternalOutput").ap()
    program(nc, aps, out)
    r = _run(nc, [{f"in_{n}": v for n, v in arrays.items()}], core_ids=[0])
    y = r.results[0]["out_t"].reshape(P, DT, S)
    return _np.ascontiguousarray(_np.transpose(y, (2, 1, 0)).reshape(1, S, D))
```

```python
from contextlib import ExitStack

import numpy as np

import concourse.bass as bass
from concourse import mybir

F32 = mybir.dt.float32
F32R = mybir.dt.float32r
BF16 = mybir.dt.bfloat16
ALU = mybir.AluOpType
ACT = mybir.ActivationFunctionType
AX = mybir.AxisListType

P = 128
D = 1024
S = 256
DT = D // P
SB = S // P
DEPTH = 2
RMS_EPS = 1e-6
LN_EPS = 1e-5
NEG = -1.0e30

HEADS = 4
NOPE, ROPE, HD = 64, 32, 64
MLA_SCALE = float(1.0 / np.sqrt(NOPE + ROPE))
SWA_SCALE = float(1.0 / np.sqrt(HD))
SWA_WINDOW = 128
D_FF = 2816
FT = D_FF // P
IN1_WIDTHS = [128] * 16
IN1_OFF = [sum(IN1_WIDTHS[:i]) for i in range(len(IN1_WIDTHS))]
IN1_COLS = sum(IN1_WIDTHS)
T_CQ, T_CKV, T_KR, T_GB, T_GC, T_UC, T_UP, T_QS, T_KS = 0, 2, 3, 4, 6, 8, 10, 12, 14
N_IN1_TILES = 15

V1 = dict(attn_norm=(0, 8), q_norm=(8, 2), kv_norm=(10, 1), conv_w=(11, 6), pool_scale=(17, 2),
          mix_norm=(19, 8), ffn_norm=(27, 8), sinks=(35, 4))
N_V1 = 39

C = 32
NCH = S // C
CPB = P // C
IN2_TILES = 21
N_GA = 16
N_TOKM = 8 + 256
IN2_COLS = (IN2_TILES + 1) * P + N_TOKM
N_GROUPS, EPG, N_EXP, EFF = 4, 8, 32, 512
N_ROUTE = N_GROUPS + N_EXP
SLOTS = 64
N_OVER = 2 * S // SLOTS
N_PASS = N_EXP + N_OVER
I32 = mybir.dt.int32
ALPHA = float((2 * DEPTH) ** 0.25)
V2 = dict(conv_w=(0, 24), conv_b=(24, 6), dt_bias=(30, 8), a_log=(38, 8), ssd_d=(46, 4), ssd_norm=(50, 4),
          mu=(54, 7), w0=(61, 2), a0=(63, 2), k_k=(65, 2), k_a=(67, 2), r_k=(69, 2), ln_g=(71, 2), ln_b=(73, 2),
          b_a=(75, 1), gla_norm=(76, 2), ln1_g=(78, 8), ln1_b=(86, 8), ln2_g=(94, 8), ln2_b=(102, 8),
          b_route=(110, 36))
N_V2 = 146

CONST = {}


def const_pack():
    r, c = np.arange(P)[:, None], np.arange(P)[None, :]
    same = r // C == c // C
    inv = (1.0 / (np.float32(10000.0) ** (np.arange(0, ROPE, 2, dtype=np.float32) / np.float32(ROPE))))
    ang = np.arange(S, dtype=np.float32)[None, :] * inv.astype(np.float32)[:, None]
    cos, sin = np.cos(ang).astype(np.float32), np.sin(ang).astype(np.float32)
    rope = np.zeros((P, S), np.float32)
    rope[64:96] = np.concatenate([cos, cos])
    rope[96:128] = np.concatenate([-sin, sin])
    q, k = np.arange(P)[:, None] + P, np.arange(2 * P)[None, :]
    dist = q - k
    slopes = [2.0 ** (-8.0 * (i + 1) / HEADS) for i in range(HEADS)]
    swa = [np.where((dist >= 0) & (dist < SWA_WINDOW), -s * dist, NEG) for s in slopes]
    mla = np.where(dist >= 0, 0.0, NEG)
    t = np.arange(S) + 1
    invc = np.stack([np.concatenate([np.tile(1.0 / np.minimum(t, w), (64, 1)) for w in ws])
                     for ws in ((2, 4), (8, 16))], 1)
    gla_heads = (np.arange(P)[:, None] // 32 == np.arange(256)[None, :] // 64)
    parts = [("ident", r == c), ("ones", np.ones((P, P))), ("ones64", r // 64 == c // 64),
             ("le3", np.concatenate([r <= c, np.ones((P, P)), r <= c], 1)), ("lt", r < c), ("gt", r > c), ("cu_incl", same & (r <= c)), ("cu_strict", same & (r < c)),
             ("cl_strict", same & (r > c)), ("rope", rope), ("mla", mla), ("swa", np.concatenate(swa, 1)),
             ("invc", invc.reshape(P, 2 * S)), ("keep", np.tile((np.arange(2 * S) % C != 0), (P, 1))),
             ("gla_heads", gla_heads), ("rank", np.tile(64.0 - np.arange(64.0), (P, 1))), ("slots", np.tile(np.arange(P) % SLOTS, (P, 1))),
             ("steps", np.tile(np.repeat(np.arange(N_OVER), N_EXP), (P, 1))),
             ("experts", np.tile(np.arange(N_OVER * N_EXP) % N_EXP, (P, 1)))]
    at = 0
    for name, m in parts:
        CONST[name] = (at, m.shape[1])
        at += m.shape[1]
    return np.ascontiguousarray(np.concatenate([np.asarray(m, np.float32) for _, m in parts], 1))


CONST_ARRAY = const_pack()
N_CONST = CONST_ARRAY.shape[1]


class Chain:

    def __init__(self, eng, sem):
        self.eng, self.sem, self.n = eng, sem, 0

    def link(self, ins):
        self.n += 1
        ins.then_inc(self.sem, 1)
        self.eng.wait_ge(self.sem, self.n)


class Stage:

    def __init__(self, nc, name):
        self.nc, self.name, self.ctx, self.sems = nc, name, ExitStack(), []

    def __enter__(self):
        return self

    def __exit__(self, *a):
        for s in self.sems:
            self.nc.sync.sem_clear(s)
        self.ctx.close()

    def sem(self, name):
        s = self.ctx.enter_context(self.nc.semaphore(f"{self.name}_{name}"))
        self.sems.append(s)
        return s

    def sb(self, name, shape, dt=F32):
        return self.ctx.enter_context(self.nc.sbuf_tensor(f"{self.name}_{name}", shape, dt))

    def ps(self, name, shape, dt=F32):
        return self.ctx.enter_context(self.nc.psum_tensor(f"{self.name}_{name}", shape, dt))


def bc(ap, n, axis):
    ap = ap.unsqueeze(axis)
    return ap.broadcast_to([n if i == axis else d for i, d in enumerate(ap.shape)])


def norm_engines(k, st, x, out, gain, eps, bias=None, tag="n"):
    ln = bias is not None
    sq = st.sb(tag + "_sq", [P, DT, S]) if ln else out
    lnv = st.sb(tag + "_lnv", [P, S])
    rstd = st.sb(tag + "_rstd", [P, S])
    mean = st.sb(tag + "_mean", [P, S]) if ln else None
    psum = st.ps(tag + "_ps", [P, 2, 512])
    squares = st.sem(tag + "_squares")
    sums = st.sem(tag + "_sums")
    mean_ready = st.sem(tag + "_mean_ready")
    rstd_ready = st.sem(tag + "_rstd_ready")
    ln_done = st.sem(tag + "_ln_done")
    normed = st.sem(tag + "_normed")
    src = out if ln else x
    extra = 1 if ln else 0

    def vector(dve, ch):
        if ln:
            dve.wait_ge(sums, 1)
            ch.link(dve.tensor_scalar(mean[:], psum[:, 0, 0:S], 1.0 / D, None, ALU.mult))
            ch.link(dve.tensor_tensor(out[:], x[:], bc(mean[:], DT, 1), ALU.subtract))
        dve.tensor_tensor(sq[:], src[:], src[:], ALU.mult).then_inc(squares, 1)
        dve.wait_ge(rstd_ready, 1)
        for t in range(DT):
            ins = dve.scalar_tensor_tensor(out[:, t], src[:, t], gain[:, t:t + 1], rstd[:], ALU.mult, ALU.mult)
            if ln:
                ch.link(ins)
                ins = dve.tensor_scalar(out[:, t], out[:, t], bias[:, t:t + 1], None, ALU.add)
            ins.then_inc(normed, 1)

    def scalar(act):
        act.wait_ge(sums, 1 + extra)
        act.activation(lnv[:], psum[:, 1, 0:S], ACT.Ln, bias=k.eps[eps], scale=1.0 / D).then_inc(ln_done, 1)
        act.wait_ge(ln_done, 1)
        act.activation(rstd[:], lnv[:], ACT.Exp, scale=-0.5).then_inc(rstd_ready, 1)

    def tensor(pe):
        if ln:
            for t in range(DT):
                ins = pe.matmul(psum[:, 0, 0:S], k.c("ones"), x[:, t], start=t == 0, stop=t == DT - 1)
            ins.then_inc(sums, 1)
        pe.wait_ge(squares, 1)
        for t in range(DT):
            ins = pe.matmul(psum[:, 1, 0:S], k.c("ones"), sq[:, t], start=t == 0, stop=t == DT - 1)
        ins.then_inc(sums, 1)

    return vector, scalar, tensor, normed


class Stream:

    def __init__(self, st, tag, sizes, slots, split_slots=2):
        self.sizes, self.slots, self.n2 = sizes, slots, split_slots
        n = max(sizes)
        self.raw = st.sb(tag + "_raw", [P, slots, n])
        self.high = st.sb(tag + "_high", [P, split_slots, n], F32R)
        self.low = st.sb(tag + "_low", [P, split_slots, n], F32R)
        self.loaded = [st.sem(f"{tag}_loaded{i}") for i in range(slots)]
        self.rounded = st.sem(tag + "_rounded")
        self.split = st.sem(tag + "_split")
        self.used = st.sem(tag + "_used")

    def halves(self, i):
        h = self.sizes[i] // 2
        return ((0, h), (h, self.sizes[i]))

    def load(self, sp, i, src):
        if i >= self.slots:
            sp.wait_ge(self.split, 2 * (i - self.slots + 1))
        sp.dma_start(self.raw[:, i % self.slots, 0:self.sizes[i]], src).then_inc(self.loaded[i % self.slots], 16)

    def round(self, act, i):
        act.wait_ge(self.loaded[i % self.slots], 16 * (i // self.slots + 1))
        if i >= self.n2:
            act.wait_ge(self.used, i - self.n2 + 1)
        for a, b in self.halves(i):
            act.activation(self.high[:, i % self.n2, a:b], self.raw[:, i % self.slots, a:b], ACT.Copy)\
                .then_inc(self.rounded, 1)

    def rest(self, dve, i):
        for n, (a, b) in enumerate(self.halves(i)):
            dve.wait_ge(self.rounded, 2 * i + n + 1)
            dve.tensor_tensor(self.low[:, i % self.n2, a:b], self.raw[:, i % self.slots, a:b],
                              self.high[:, i % self.n2, a:b], ALU.subtract).then_inc(self.split, 1)

    def weights(self, i, off, n, width=P):
        return [w[:, i % self.n2, off * width:(off + n) * width].rearrange("p (k c) -> p k c", k=n)
                for w in (self.high, self.low)]

    def ready(self, pe, i):
        pe.wait_ge(self.split, 2 * (i + 1))


def product3(pe, out, stationary, moving, n):
    (sh, sl), (mh, ml) = stationary, moving
    for kk in range(n):
        pe.matmul(out, sh(kk), mh(kk), start=kk == 0, stop=False)
        pe.matmul(out, sh(kk), ml(kk), start=False, stop=False)
        ins = pe.matmul(out, sl(kk), mh(kk), start=False, stop=kk == n - 1)
    return ins


class Halves:

    def __init__(self, st, tag, n):
        self.high = st.sb(tag + "_high", [P, n, S], F32R)
        self.low = st.sb(tag + "_low", [P, n, S], F32R)
        self.rounded = st.sem(tag + "_rounded")
        self.split = st.sem(tag + "_split")
        self.n = n

    def round(self, act, src, ready=None, step=1):
        for t in range(0, self.n, step):
            if ready is not None:
                act.wait_ge(ready, t + step)
            act.activation(self.high[:, t:t + step], src[:, t:t + step], ACT.Copy).then_inc(self.rounded, step)

    def rest(self, dve, src, step=1):
        for t in range(0, self.n, step):
            dve.wait_ge(self.rounded, t + step)
            dve.tensor_tensor(self.low[:, t:t + step], src[:, t:t + step], self.high[:, t:t + step], ALU.subtract)\
                .then_inc(self.split, step)

    def tiles(self):
        return [lambda kk, w=w: w[:, kk] for w in (self.high, self.low)]

    def block(self, blk):
        return [lambda kk, w=w: w[:, kk, blk * P:(blk + 1) * P] for w in (self.high, self.low)]


def at(pair):
    return [lambda kk, w=w: w[:, kk] for w in pair]


class Kit:

    def __init__(self, nc, ctx):
        self.nc = nc
        self.x = ctx.enter_context(nc.sbuf_tensor("x_resid", [P, DT, S], F32))
        self.const = ctx.enter_context(nc.sbuf_tensor("const", [P, N_CONST], F32))
        self.eps_sb = ctx.enter_context(nc.sbuf_tensor("eps_sb", [P, 5], F32))
        self.eps = {RMS_EPS: self.eps_sb[:, 0:1], LN_EPS: self.eps_sb[:, 1:2], 64e-5: self.eps_sb[:, 2:3],
                    1e-12: self.eps_sb[:, 3:4], 1.0: self.eps_sb[:, 4:5]}

    def c(self, name):
        at, n = CONST[name]
        return self.const[:, at:at + n]


def stage_load(nc, k, x_in, const_in):
    with Stage(nc, "load") as st:
        loaded = st.sem("loaded")
        eps_set = st.sem("eps_set")
        with nc.Block() as block:

            @block.sync
            def _(sp):
                sp.dma_start(k.x[:], x_in.rearrange("p (t s) -> p t s", t=DT)).then_inc(loaded, 16)
                sp.dma_start(k.const[:], const_in).then_inc(loaded, 16)
                sp.wait_ge(loaded, 32)

            @block.vector
            def _(dve):
                for i, e in enumerate((RMS_EPS, LN_EPS, 64e-5, 1e-12, 1.0)):
                    dve.memset(k.eps_sb[:, i:i + 1], e).then_inc(eps_set, 1)
                dve.wait_ge(eps_set, 5)


def stage_project1(nc, k, L, w_dram, v_dram, vecs, proj, vtok):
    with Stage(nc, "project1") as st:
        h = st.sb("h", [P, DT, S])
        hs = Halves(st, "hs", DT)
        unit = 2 * DT * P
        w = Stream(st, "w", [unit] * 8, 4)
        ps = st.ps("ps", [P, 4, 512])
        vec_loaded = st.sem("vec_loaded")
        copied = st.sem("copied")
        dve_step = st.sem("dve_step")
        n_vec, n_act, n_pe, normed = norm_engines(k, st, k.x, h, vecs[:, V1["attn_norm"][0]:], RMS_EPS)

        with nc.Block() as block:

            @block.sync
            def _(sp):
                sp.dma_start(vecs[:], v_dram[bass.ds(L, 1)].rearrange("a p n -> (a p) n")).then_inc(vec_loaded, 16)
                for i in range(8):
                    w.load(sp, i, w_dram[bass.ds(L, 1), :, i * unit:(i + 1) * unit].rearrange("a p n -> (a p) n"))

            @block.vector
            def _(dve):
                dve.wait_ge(vec_loaded, 16)
                n_vec(dve, Chain(dve, dve_step))
                hs.rest(dve, h)
                for i in range(8):
                    w.rest(dve, i)

            @block.scalar
            def _(act):
                w.round(act, 0)
                n_act(act)
                hs.round(act, h, normed)
                w.round(act, 1)
                for i in range(8):
                    act.wait_ge(w.used, i + 1)
                    if i < 7:
                        act.activation(proj[:, 2 * i:2 * i + 2].rearrange("p a s -> p (a s)"), ps[:, i % 4], ACT.Copy)\
                            .then_inc(copied, 1)
                    else:
                        act.activation(proj[:, 14], ps[:, i % 4, 0:S], ACT.Copy)
                        act.activation(vtok[:].rearrange("p b f -> p (b f)"), ps[:, i % 4, S:2 * S], ACT.Copy)\
                            .then_inc(copied, 1)
                    if i + 2 < 8:
                        w.round(act, i + 2)

            @block.tensor
            def _(pe):
                n_pe(pe)
                pe.wait_ge(hs.split, DT)
                for i in range(8):
                    w.ready(pe, i)
                    if i >= 4:
                        pe.wait_ge(copied, i - 3)
                    ins = product3(pe, ps[:, i % 4, 0:S], at(w.weights(i, 0, DT)), hs.tiles(), DT)
                    if i < 7:
                        ins = product3(pe, ps[:, i % 4, S:2 * S], at(w.weights(i, DT, DT)), hs.tiles(), DT)
                    else:
                        for blk in range(SB):
                            ins = product3(pe, ps[:, i % 4, S + blk * P:S + (blk + 1) * P], hs.block(blk),
                                           at(w.weights(i, DT, DT)), DT)
                    ins.then_inc(w.used, 1)


def stage_mixers1(nc, k, L, proj, vtok, vecs, wuq_dram, wukv_dram, poolw_dram, y):
    with Stage(nc, "mixers1") as st:
        wuq = st.sb("wuq", [P, 2, HEADS, P])
        wukv = st.sb("wukv", [P, 2, 256])
        poolw = st.sb("poolw", [P, 2, 64])
        cn = st.sb("cn", [P, 3, S])
        sq = st.sb("sqc", [P, 3, S])
        lnv = st.sb("lnvc", [P, 2, S])
        rstd = st.sb("rstdc", [P, 2, S])
        qT = st.sb("qT", [P, HEADS, S])
        kT = st.sb("kT", [P, HEADS, S])
        rot = st.sb("rot", [P, HEADS, S])
        vm = st.sb("vm", [P, SB, 256])
        prob = st.sb("prob", [P, 2, HEADS, S])
        probT = st.sb("probT", [P, HEADS * SB, P])
        mx = st.sb("mx", [P, 2, HEADS])
        nmx = st.sb("nmx", [P, 2, HEADS])
        den = st.sb("den", [P, 2, HEADS])
        snk = st.sb("snk", [P, 2, HEADS])
        rden = st.sb("rden", [P, 2, HEADS])
        zc = st.sb("zc", [P, 2, S + 2])
        ct = st.sb("ct", [P, 2, S])
        up = st.sb("up", [P, 2, S + 16])
        s2 = st.sb("s2", [P, 2, S + 16])
        s4 = st.sb("s4", [P, 2, S + 16])
        s8 = st.sb("s8", [P, 2, S + 16])
        s16 = st.sb("s16", [P, 2, S + 16])
        pooled = st.sb("pooled", [P, 2, S])
        psA = st.ps("psA", [P, 4, 512])
        psT = st.ps("psT", [P, 2, 512])
        psY = st.ps("psY", [P, 512])
        psX = st.ps("psX", [P, 512])
        w_loaded = st.sem("w_loaded")
        squares = st.sem("squares")
        sums = st.sem("sums")
        ln_done = st.sem("ln_done")
        rstd_ready = st.sem("rstd_ready")
        latent_ready = st.sem("latent_ready")
        q_done = st.sem("q_done")
        k_done = st.sem("k_done")
        v_done = st.sem("v_done")
        kv_copied = st.sem("kv_copied")
        q_copied = st.sem("q_copied")
        rope_ready = st.sem("rope_ready")
        scores_done = st.sem("scores_done")
        scores_read = st.sem("scores_read")
        max_ready = st.sem("max_ready")
        exp_done = st.sem("exp_done")
        probs_ready = st.sem("probs_ready")
        transposed = st.sem("transposed")
        probT_ready = st.sem("probT_ready")
        attended = st.sem("attended")
        y_copied = st.sem("y_copied")
        pool_ready = st.sem("pool_ready")
        pool_mixed = st.sem("pool_mixed")
        dve_step = st.sem("dve_step")
        gp_step = st.sem("gp_step")
        units = [(1, 0), (1, 1), (0, 0), (0, 1)]
        vec = lambda n, i=0: vecs[:, V1[n][0] + i:V1[n][0] + i + 1]

        with nc.Block() as block:

            @block.sync
            def _(sp):
                sp.dma_start(wuq[:], wuq_dram[bass.ds(L, 1)].rearrange("a p (k h c) -> (a p) k h c", k=2, h=HEADS))\
                    .then_inc(w_loaded, 16)
                sp.dma_start(wukv[:], wukv_dram[bass.ds(L, 1)].rearrange("a p (k c) -> (a p) k c", k=2))\
                    .then_inc(w_loaded, 16)
                sp.dma_start(poolw[:], poolw_dram[bass.ds(L, 1)].rearrange("a p (k c) -> (a p) k c", k=2))\
                    .then_inc(w_loaded, 16)

            @block.gpsimd
            def _(gp):
                ch = Chain(gp, gp_step)
                gp.memset(zc[:, :, 0:2], 0.0)
                gp.memset(up[:, :, 0:16], 0.0)
                gp.memset(s2[:, :, 0:16], 0.0)
                gp.memset(s4[:, :, 0:16], 0.0)
                gp.memset(s8[:, :, 0:16], 0.0)
                ch.link(gp.tensor_tensor(zc[:, :, 2:], proj[:, T_GC:T_GC + 2], proj[:, T_UC:T_UC + 2], ALU.mult))
                ch.link(gp.tensor_copy(up[:, :, 16:], proj[:, T_UP:T_UP + 2]))
                for t in range(2):
                    yt = y[:, 2 + t]
                    ch.link(gp.tensor_scalar(yt, zc[:, t, 0:S], vec("conv_w", t), None, ALU.mult))
                    for tap in (1, 2):
                        ch.link(gp.tensor_scalar(ct[:, t], zc[:, t, tap:tap + S], vec("conv_w", 2 * tap + t), None,
                                                 ALU.mult))
                        ch.link(gp.tensor_tensor(yt, yt, ct[:, t], ALU.add))
                    ch.link(gp.tensor_tensor(yt, yt, proj[:, T_GB + t], ALU.mult))
                for a, b, w in ((up, s2, 1), (s2, s4, 2), (s4, s8, 4), (s8, s16, 8)):
                    ch.link(gp.tensor_tensor(b[:, :, 16:], a[:, :, 16:], a[:, :, 16 - w:S + 16 - w], ALU.add))
                invc = k.c("invc").rearrange("p (t s) -> p t s", t=2)
                for i, s in enumerate((s2, s4, s8, s16)):
                    rows, t = slice(64 * (i % 2), 64 * (i % 2) + 64), i // 2
                    ch.link(gp.tensor_tensor(pooled[rows, t], s[rows, t, 16:], invc[rows, t], ALU.mult))
                gp.tensor_tensor(pooled[:], pooled[:], up[:, :, 16:], ALU.subtract).then_inc(pool_ready, 1)

            @block.vector
            def _(dve):
                ch = Chain(dve, dve_step)
                dve.tensor_tensor(sq[:], proj[:, 0:3], proj[:, 0:3], ALU.mult).then_inc(squares, 1)
                dve.wait_ge(rstd_ready, 1)
                for t in range(3):
                    dve.scalar_tensor_tensor(cn[:, t], proj[:, t], vec("q_norm", t) if t < 2 else vec("kv_norm"),
                                             rstd[:, 0 if t < 2 else 1], ALU.mult, ALU.mult).then_inc(latent_ready, 1)
                cos, sin = k.c("rope")[64:96, :], k.c("rope")[96:128, :]
                dve.wait_ge(q_done, 1)
                psq = psA[:].rearrange("p b (h s) -> p (b h) s", h=2)
                ch.link(dve.tensor_tensor(rot[64:96], psq[96:128, 0:HEADS], bc(sin, HEADS, 1), ALU.mult))
                ch.link(dve.tensor_tensor(qT[64:96], psq[64:96, 0:HEADS], bc(cos, HEADS, 1), ALU.mult))
                dve.tensor_tensor(qT[64:96], qT[64:96], rot[64:96], ALU.add).then_inc(rope_ready, 1)
                dve.wait_ge(rope_ready, 1)
                ch.link(dve.tensor_tensor(rot[64:96, 0], proj[96:128, T_KR], sin, ALU.mult))
                ch.link(dve.tensor_tensor(rot[64:96, 1], proj[64:96, T_KR], cos, ALU.mult))
                dve.tensor_tensor(kT[64:96], bc(rot[64:96, 0], HEADS, 1), bc(rot[64:96, 1], HEADS, 1), ALU.add)\
                    .then_inc(rope_ready, 1)
                dve.wait_ge(pool_mixed, 1)
                for t in range(2):
                    dve.tensor_scalar(y[:, 4 + t], psX[:, t * S:(t + 1) * S], vec("pool_scale", t), None, ALU.mult)

                def soften(u):
                    mla, blk = units[u]
                    n, pr = P * (blk + 1), prob[:, u % 2]
                    if mla:
                        bias = bc(k.c("mla")[:, 2 * P - n:], HEADS, 1)
                    else:
                        bias = k.c("swa").rearrange("p (h c) -> p h c", h=HEADS)[:, :, 2 * P - n:]
                    dve.wait_ge(scores_done, u + 1)
                    sc = psA[:, 2 * (u % 2):2 * (u % 2) + 2].rearrange("p b (h c) -> p (b h) c", h=2)
                    if not mla:
                        pass
                    ins = dve.scalar_tensor_tensor(pr[:, :, 0:n], sc[:, :, 0:n], MLA_SCALE if mla else SWA_SCALE, bias,
                                                   ALU.mult, ALU.add)
                    ins.then_inc(scores_read, 1)
                    dve.wait_ge(scores_read, u + 1)
                    ch.link(dve.reduce_max(mx[:, u % 2], pr[:, :, 0:n], AX.X))
                    if not mla:
                        sinks = vecs[:, V1["sinks"][0]:V1["sinks"][0] + HEADS]
                        ch.link(dve.tensor_tensor(mx[:, u % 2], mx[:, u % 2], sinks, ALU.max))
                        ch.link(dve.tensor_tensor(snk[:, u % 2], sinks, mx[:, u % 2], ALU.subtract))
                    dve.tensor_scalar(nmx[:, u % 2], mx[:, u % 2], -1.0, None, ALU.mult).then_inc(max_ready, 1)

                def normalise(u):
                    mla, blk = units[u]
                    n, pr = P * (blk + 1), prob[:, u % 2]
                    dve.wait_ge(exp_done, u + 1)
                    if not mla:
                        ch.link(dve.tensor_tensor(den[:, u % 2], den[:, u % 2], snk[:, u % 2], ALU.add))
                    ch.link(dve.reciprocal(rden[:, u % 2], den[:, u % 2]))
                    dve.tensor_tensor(pr[:, :, 0:n], pr[:, :, 0:n], bc(rden[:, u % 2], n, 2), ALU.mult)\
                        .then_inc(probs_ready, 1)

                soften(0)
                for u in range(4):
                    if u < 3:
                        if u >= 1:
                            dve.wait_ge(transposed, u)
                        soften(u + 1)
                    normalise(u)

            @block.scalar
            def _(act):
                act.wait_ge(sums, 1)
                act.activation(lnv[:, 0], psX[:, 0:S], ACT.Ln, bias=k.eps[RMS_EPS], scale=1.0 / 256).then_inc(ln_done, 1)
                act.activation(lnv[:, 1], psX[:, S:2 * S], ACT.Ln, bias=k.eps[RMS_EPS], scale=1.0 / 128)\
                    .then_inc(ln_done, 1)
                act.wait_ge(ln_done, 2)
                act.activation(rstd[:], lnv[:], ACT.Exp, scale=-0.5).then_inc(rstd_ready, 1)
                act.wait_ge(q_done, 1)
                act.wait_ge(rope_ready, 1)
                psq = psA[:].rearrange("p b (h s) -> p (b h) s", h=2)
                act.activation(qT[0:64], psq[0:64, 0:HEADS], ACT.Copy).then_inc(q_copied, 1)
                act.wait_ge(k_done, 1)
                act.activation(kT[0:64], psq[0:64, HEADS:], ACT.Copy).then_inc(kv_copied, 1)
                act.wait_ge(v_done, 1)
                act.activation(vm[:].rearrange("p b f -> p (b f)"), psY[:], ACT.Copy).then_inc(kv_copied, 1)

                def exps(u):
                    mla, blk = units[u]
                    n, pr = P * (blk + 1), prob[:, u % 2]
                    act.wait_ge(max_ready, u + 1)
                    for h in range(HEADS):
                        ins = act.activation(pr[:, h, 0:n], pr[:, h, 0:n], ACT.Exp, bias=nmx[:, u % 2, h:h + 1],
                                             accum_out=den[:, u % 2, h:h + 1])
                    if not mla:
                        ins = act.activation(snk[:, u % 2], snk[:, u % 2], ACT.Exp)
                    ins.then_inc(exp_done, 1)

                exps(0)
                for u in range(4):
                    mla, blk = units[u]
                    if u < 3:
                        exps(u + 1)
                    nt = HEADS * (blk + 1)
                    act.wait_ge(transposed, u + 1)
                    act.activation(probT[:, 0:nt].rearrange("p t q -> p (t q)"),
                                   psT[:].rearrange("p b n -> p (b n)")[:, 0:nt * P], ACT.Copy).then_inc(probT_ready, 1)
                    act.wait_ge(attended, u + 1)
                    act.activation(y[:, 0 if mla else 6:2 if mla else 8, blk * P:(blk + 1) * P],
                                   psY[:].rearrange("p (t s) -> p t s", t=2)[:, :, 0:P], ACT.Copy).then_inc(y_copied, 1)

            @block.tensor
            def _(pe):
                pe.wait_ge(squares, 1)
                for t in range(2):
                    pe.matmul(psX[:, 0:S], k.c("ones"), sq[:, t], start=t == 0, stop=t == 1)
                pe.matmul(psX[:, S:2 * S], k.c("ones"), sq[:, 2], start=True, stop=True).then_inc(sums, 1)
                pe.wait_ge(w_loaded, 48)
                pe.wait_ge(latent_ready, 3)
                psq = psA[:].rearrange("p b (h s) -> p (b h) s", h=2)
                for h in range(HEADS):
                    for t in range(2):
                        ins = pe.matmul(psq[:, h], wuq[:, t, h], cn[:, t], start=t == 0, stop=t == 1)
                ins.then_inc(q_done, 1)
                for h in range(HEADS):
                    ins = pe.matmul(psq[0:64, HEADS + h], wukv[:, 0, h * 64:(h + 1) * 64], cn[:, 2], start=True, stop=True)
                ins.then_inc(k_done, 1)
                for blk in range(SB):
                    ins = pe.matmul(psY[:, blk * S:(blk + 1) * S], cn[:, 2, blk * P:(blk + 1) * P], wukv[:, 1],
                                    start=True, stop=True)
                ins.then_inc(v_done, 1)
                pe.wait_ge(ln_done, 2)
                pe.wait_ge(pool_ready, 1)
                for g in range(4):
                    rows, t = slice(64 * (g % 2), 64 * (g % 2) + 64), g // 2
                    ins = pe.matmul(psX[rows, t * S:(t + 1) * S], poolw[rows, t], pooled[rows, t], start=True, stop=True)
                ins.then_inc(pool_mixed, 1)

                def scores(u):
                    mla, blk = units[u]
                    n = P * (blk + 1)
                    qs = slice(blk * P, (blk + 1) * P)
                    sc = psA[:, 2 * (u % 2):2 * (u % 2) + 2].rearrange("p b (h c) -> p (b h) c", h=2)
                    if u >= 2:
                        pe.wait_ge(scores_read, u - 1)
                    for h in range(HEADS):
                        if mla:
                            ins = pe.matmul(sc[:, h, 0:n], qT[0:96, h, qs], kT[0:96, h, 0:n], start=True, stop=True)
                        else:
                            rows = slice(64 * (h // 2), 64 * (h // 2) + 64)
                            ins = pe.matmul(sc[:, h, 0:n], proj[rows, T_QS + h % 2, qs], proj[rows, T_KS, 0:n],
                                            start=True, stop=True)
                    ins.then_inc(scores_done, 1)

                pe.wait_ge(q_copied, 1)
                pe.wait_ge(kv_copied, 2)
                pe.wait_ge(rope_ready, 2)
                scores(0)
                scores(1)
                for u in range(4):
                    mla, blk = units[u]
                    pe.wait_ge(probs_ready, u + 1)
                    if u >= 1:
                        pe.wait_ge(probT_ready, u)
                    for h in range(HEADS):
                        for kb in range(blk + 1):
                            at = (h * (blk + 1) + kb) * P
                            ins = pe.transpose(psT[:, at // 512, at % 512:at % 512 + P],
                                               prob[:, u % 2, h, kb * P:(kb + 1) * P], k.c("ident"))
                    ins.then_inc(transposed, 1)
                    if u < 2:
                        scores(u + 2)
                    pe.wait_ge(probT_ready, u + 1)
                    if u >= 1:
                        pe.wait_ge(y_copied, u)
                    for h in range(HEADS):
                        rows = slice(64 * (h % 2), 64 * (h % 2) + 64)
                        for kb in range(blk + 1):
                            v = vm[:, kb, h * 64:(h + 1) * 64] if mla else vtok[:, kb, (h // 2) * 64:(h // 2) * 64 + 64]
                            ins = pe.matmul(psY[rows, (h // 2) * S:(h // 2) * S + P], v, probT[:, h * (blk + 1) + kb],
                                            start=kb == 0, stop=kb == blk)
                    ins.then_inc(attended, 1)


def stage_output1(nc, k, L, vecs, y, wo_dram):
    with Stage(nc, "output1") as st:
        unit = 2 * DT * P
        w = Stream(st, "w", [unit] * 4, 4)
        sq = st.sb("sq", [P, DT, S])
        lnv = st.sb("lnv", [P, 4, S])
        rstd = st.sb("rstd", [P, 4, S])
        yn = st.sb("yn", [P, DT, S])
        ys = Halves(st, "ys", DT)
        psG = st.ps("psG", [P, 2, 512])
        ps = st.ps("ps", [P, 4, 512])
        squares = st.sem("squares")
        sums = st.sem("sums")
        ln_done = st.sem("ln_done")
        rstd_ready = st.sem("rstd_ready")
        normed = st.sem("normed")
        added = st.sem("added")
        with nc.Block() as block:

            @block.sync
            def _(sp):
                for i in range(4):
                    w.load(sp, i, wo_dram[bass.ds(L, 1), :, i * unit:(i + 1) * unit].rearrange("a p n -> (a p) n"))

            @block.vector
            def _(dve):
                dve.tensor_tensor(sq[:], y[:], y[:], ALU.mult).then_inc(squares, 1)
                w.rest(dve, 0)
                dve.wait_ge(rstd_ready, 1)
                g0 = V1["mix_norm"][0]
                for t in range(DT):
                    dve.scalar_tensor_tensor(yn[:, t], y[:, t], vecs[:, g0 + t:g0 + t + 1], rstd[:, t // 2],
                                             ALU.mult, ALU.mult).then_inc(normed, 1)
                ys.rest(dve, yn)
                w.rest(dve, 1)
                for m in range(4):
                    dve.wait_ge(w.used, m + 1)
                    xm = k.x[:, 2 * m:2 * m + 2].rearrange("p a s -> p (a s)")
                    dve.tensor_tensor(xm, xm, ps[:, m], ALU.add).then_inc(added, 1)
                    if m + 2 < 4:
                        w.rest(dve, m + 2)

            @block.scalar
            def _(act):
                w.round(act, 0)
                act.wait_ge(sums, 1)
                act.activation(lnv[:].rearrange("p g s -> p (g s)"), psG[:].rearrange("p b n -> p (b n)"), ACT.Ln,
                               bias=k.eps[RMS_EPS], scale=1.0 / 256).then_inc(ln_done, 1)
                act.wait_ge(ln_done, 1)
                act.activation(rstd[:], lnv[:], ACT.Exp, scale=-0.5).then_inc(rstd_ready, 1)
                ys.round(act, yn, normed)
                for i in range(1, 4):
                    w.round(act, i)

            @block.tensor
            def _(pe):
                pe.wait_ge(squares, 1)
                for g in range(4):
                    for t in range(2):
                        ins = pe.matmul(psG[:, g // 2, (g % 2) * S:(g % 2 + 1) * S], k.c("ones"), sq[:, 2 * g + t],
                                        start=t == 0, stop=t == 1)
                ins.then_inc(sums, 1)
                pe.wait_ge(ys.split, DT)
                for i in range(4):
                    w.ready(pe, i)
                    for m in range(2):
                        ins = product3(pe, ps[:, i, m * S:(m + 1) * S], at(w.weights(i, m * DT, DT)), ys.tiles(), DT)
                    ins.then_inc(w.used, 1)


def stage_ffn1(nc, k, L, vecs, wgu_dram, wd_dram):
    with Stage(nc, "ffn1") as st:
        h = st.sb("h", [P, DT, S])
        hs = Halves(st, "hs", DT)
        n_units = FT + DT
        w = Stream(st, "w", [2 * DT * P] * FT + [FT * P] * DT, 3)
        acts = Halves(st, "acts", FT)
        sig = st.sb("sig", [P, 2, S])
        ps = st.ps("ps", [P, 4, 512])
        sig_ready = st.sem("sig_ready")
        act_ready = st.sem("act_ready")
        added = st.sem("added")
        dve_step = st.sem("dve_step")
        n_vec, n_act, n_pe, normed = norm_engines(k, st, k.x, h, vecs[:, V1["ffn_norm"][0]:], RMS_EPS)
        with nc.Block() as block:

            @block.sync
            def _(sp):
                for i in range(FT):
                    w.load(sp, i, wgu_dram[bass.ds(L, 1), i].rearrange("a p n -> (a p) n"))
                for m in range(DT):
                    w.load(sp, FT + m, wd_dram[bass.ds(L, 1), m].rearrange("a p n -> (a p) n"))

            @block.vector
            def _(dve):
                ch = Chain(dve, dve_step)
                n_vec(dve, ch)
                hs.rest(dve, h)
                w.rest(dve, 0)
                w.rest(dve, 1)
                for i in range(n_units):
                    if i < FT:
                        dve.wait_ge(sig_ready, i + 1)
                        ch.link(dve.tensor_tensor(sig[:, i % 2], sig[:, i % 2], ps[:, i % 4, 0:S], ALU.mult))
                        dve.tensor_tensor(sig[:, i % 2], sig[:, i % 2], ps[:, i % 4, S:2 * S], ALU.mult)\
                            .then_inc(act_ready, 1)
                        if i + 2 < n_units:
                            w.rest(dve, i + 2)
                        dve.wait_ge(acts.rounded, i + 1)
                        dve.tensor_tensor(acts.low[:, i], sig[:, i % 2], acts.high[:, i], ALU.subtract)\
                            .then_inc(acts.split, 1)
                    else:
                        m = i - FT
                        dve.wait_ge(w.used, i + 1)
                        dve.tensor_tensor(k.x[:, m], k.x[:, m], ps[:, i % 4, 0:S], ALU.add).then_inc(added, 1)
                        if i + 2 < n_units:
                            w.rest(dve, i + 2)

            @block.scalar
            def _(act):
                w.round(act, 0)
                n_act(act)
                hs.round(act, h, normed)
                w.round(act, 1)
                for i in range(n_units):
                    act.wait_ge(w.used, i + 1)
                    if i < FT:
                        if i >= 2:
                            act.wait_ge(acts.split, i - 1)
                        act.activation(sig[:, i % 2], ps[:, i % 4, 0:S], ACT.Sigmoid).then_inc(sig_ready, 1)
                    if i + 2 < n_units:
                        w.round(act, i + 2)
                    if i < FT:
                        act.wait_ge(act_ready, i + 1)
                        act.activation(acts.high[:, i], sig[:, i % 2], ACT.Copy).then_inc(acts.rounded, 1)

            @block.tensor
            def _(pe):
                n_pe(pe)
                pe.wait_ge(hs.split, DT)
                for i in range(n_units):
                    w.ready(pe, i)
                    if 4 <= i < FT + 4:
                        pe.wait_ge(act_ready, i - 3)
                    if i < FT:
                        for g in range(2):
                            ins = product3(pe, ps[:, i % 4, g * S:(g + 1) * S], at(w.weights(i, g * DT, DT)), hs.tiles(), DT)
                    else:
                        if i == FT:
                            pe.wait_ge(acts.split, FT)
                        if i >= FT + 4:
                            pe.wait_ge(added, i - FT - 3)
                        ins = product3(pe, ps[:, i % 4, 0:S], at(w.weights(i, 0, FT)), acts.tiles(), FT)
                    ins.then_inc(w.used, 1)


def stage_norm(nc, k, name, vec_dram, col_g, col_b, n, eps):
    with Stage(nc, name) as st:
        gv = st.sb("gv", [P, n])
        tmp = st.sb("tmp", [P, DT, S])
        loaded = st.sem("loaded")
        dve_step = st.sem("dve_step")
        n_vec, n_act, n_pe, normed = norm_engines(k, st, k.x, tmp, gv[:, col_g:col_g + DT], eps,
                                                  None if col_b is None else gv[:, col_b:col_b + DT])
        with nc.Block() as block:

            @block.sync
            def _(sp):
                sp.dma_start(gv[:], vec_dram).then_inc(loaded, 16)

            @block.vector
            def _(dve):
                dve.wait_ge(loaded, 16)
                n_vec(dve, Chain(dve, dve_step))
                dve.wait_ge(normed, DT)
                dve.tensor_copy(k.x[:], tmp[:])

            @block.scalar
            def _(act):
                n_act(act)

            @block.tensor
            def _(pe):
                n_pe(pe)


def stage_store(nc, k, out):
    with Stage(nc, "store") as st:
        stored = st.sem("stored")
        with nc.Block() as block:

            @block.sync
            def _(sp):
                sp.dma_start(out.rearrange("p (t s) -> p t s", t=DT), k.x[:]).then_inc(stored, 16)
                sp.wait_ge(stored, 16)




def stage_project2(nc, k, L, w_dram, v_dram, vecs, b):
    with Stage(nc, "project2") as st:
        xs = Halves(st, "xs", DT)
        pair = 2 * DT * P
        n_pairs = (IN2_TILES + 1) // 2
        n_units = n_pairs + 1
        w = Stream(st, "w", [pair] * n_pairs + [DT * N_TOKM], 4)
        ps = st.ps("ps", [P, 4, 512])
        vec_loaded = st.sem("vec_loaded")
        copied = st.sem("copied")
        dst = [b.z[:, t] for t in range(4)] + [b.xbc[:, t, 3:] for t in range(6)] + \
              [b.rw[:, t, 1:] for t in range(7)] + [b.gl[:, t] for t in range(4)] + [b.ga[:]]

        with nc.Block() as block:

            @block.sync
            def _(sp):
                for i in range(n_units):
                    w.load(sp, i, w_dram[bass.ds(L, 1), :, i * pair:i * pair + w.sizes[i]].rearrange("a p n -> (a p) n"))
                    if i == 0:
                        sp.dma_start(vecs[:], v_dram[bass.ds(L, 1)].rearrange("a p n -> (a p) n"))\
                            .then_inc(vec_loaded, 16)
                sp.wait_ge(vec_loaded, 16)

            @block.vector
            def _(dve):
                xs.rest(dve, k.x, 2)
                for i in range(n_units):
                    w.rest(dve, i)

            @block.scalar
            def _(act):
                xs.round(act, k.x, None, 2)
                w.round(act, 0)
                w.round(act, 1)
                for i in range(n_units):
                    act.wait_ge(w.used, i + 1)
                    if i < n_pairs:
                        for j in range(2):
                            ins = act.activation(dst[2 * i + j], ps[:, i % 2, j * S:(j + 1) * S], ACT.Copy)
                        ins.then_inc(copied, 1)
                    else:
                        act.activation(b.tokm[:], ps[:, 2:4, 0:N_TOKM], ACT.Copy).then_inc(copied, 1)
                    if i + 2 < n_units:
                        w.round(act, i + 2)

            @block.tensor
            def _(pe):
                pe.wait_ge(xs.split, DT)
                for i in range(n_units):
                    w.ready(pe, i)
                    if i < n_pairs:
                        if i >= 2:
                            pe.wait_ge(copied, i - 1)
                        for j in range(2):
                            ins = product3(pe, ps[:, i % 2, j * S:(j + 1) * S], at(w.weights(i, j * DT, DT)),
                                           xs.tiles(), DT)
                    else:
                        for blk in range(SB):
                            ins = product3(pe, ps[:, 2 + blk, 0:N_TOKM], xs.block(blk),
                                           at(w.weights(i, 0, DT, N_TOKM)), DT)
                    ins.then_inc(w.used, 1)


def stage_ssd(nc, k, vecs, b, y):
    with Stage(nc, "ssd") as st:
        cx = st.sb("cx", [P, 6, S])
        sg = st.sb("sg", [P, 6, S])
        dt = st.sb("dt", [P, SB, 8])
        dta = st.sb("dta", [P, SB, 8])
        tmp = st.sb("tmp", [P, SB, 8])
        ea = st.sb("ea", [P, 8])
        G = st.sb("G", [P, SB, 8, P])
        xd = st.sb("xd", [P, SB, 8, 64])
        cb = st.sb("cb", [P, 2, 3 * P])
        E = st.sb("E", [P, 2, 3 * P])
        M = st.sb("M", [P, 2, 3 * P])
        sq = st.sb("sq", [P, 4, S])
        lnv = st.sb("lnv", [P, 2, S])
        rstd = st.sb("rstd", [P, 2, S])
        psT = st.ps("psT", [P, SB, 512])
        psC = st.ps("psC", [P, 2, 512])
        psD = st.ps("psD", [P, 2, 512])
        psY = st.ps("psY", [P, 2, 512])
        dve_step, act_step = st.sem("dve_step"), st.sem("act_step")
        conv_ready, sig_ready, x_ready = st.sem("conv_ready"), st.sem("sig_ready"), st.sem("x_ready")
        dt_pre, dt_exp, dt_ready = st.sem("dt_pre"), st.sem("dt_exp"), st.sem("dt_ready")
        xT_done, xd_ready = st.sem("xT_done"), st.sem("xd_ready")
        cb_done, G_ready = st.sem("cb_done"), st.sem("G_ready")
        decay_done, E_ready, M_ready = st.sem("decay_done"), st.sem("E_ready"), st.sem("M_ready")
        y_done, squares, sums, rstd_ready = st.sem("y_done"), st.sem("squares"), st.sem("sums"), st.sem("rstd_ready")
        z_sig = st.sem("z_sig")
        vec = lambda n, i=0: vecs[:, V2[n][0] + i:V2[n][0] + i + 1]
        vecn = lambda n: vecs[:, V2[n][0]:V2[n][0] + V2[n][1]]
        psYt = psY[:].rearrange("p b (t s) -> p (b t) s", t=2)

        with nc.Block() as block:

            @block.vector
            def _(dve):
                ch = Chain(dve, dve_step)
                ch.link(dve.tensor_tensor(dt[:], b.tokm[:, :, 0:8], bc(vecn("dt_bias"), SB, 1), ALU.add))
                ch.link(dve.tensor_scalar(tmp[:], dt[:], -1.0, None, ALU.mult))
                dve.tensor_tensor(tmp[:], tmp[:], dt[:], ALU.max).then_inc(dt_pre, 1)
                for t in range(6):
                    ch.link(dve.tensor_scalar(cx[:, t], b.xbc[:, t, 0:S], vec("conv_w", t), vec("conv_b", t),
                                              ALU.mult, ALU.add))
                    for tap in (1, 2, 3):
                        ins = dve.scalar_tensor_tensor(cx[:, t], b.xbc[:, t, tap:tap + S], vec("conv_w", 6 * tap + t),
                                                       cx[:, t], ALU.mult, ALU.add)
                        if tap < 3:
                            ch.link(ins)
                    ins.then_inc(conv_ready, 1)
                dve.wait_ge(dt_exp, 1)
                ch.link(dve.tensor_scalar(dt[:], dt[:], 0.0, None, ALU.max))
                ch.link(dve.tensor_tensor(dt[:], dt[:], tmp[:], ALU.add))
                ch.link(dve.tensor_tensor(dta[:], dt[:], bc(ea[:], SB, 1), ALU.mult))
                dve.tensor_scalar(dta[:], dta[:], -1.0, None, ALU.mult).then_inc(dt_ready, 1)
                dve.wait_ge(dt_ready, 1)
                for h in range(8):
                    for blk in range(SB):
                        dve.tensor_scalar(G[:, blk, h], k.c("gt"), dta[:, blk, h:h + 1], None, ALU.mult)\
                            .then_inc(G_ready, 1)
                dve.wait_ge(sig_ready, 1)
                dve.wait_ge(conv_ready, 6)
                dve.tensor_tensor(cx[:], cx[:], sg[:], ALU.mult).then_inc(x_ready, 1)
                dve.wait_ge(cb_done, 1)
                for g in range(2):
                    ins = dve.tensor_tensor(cb[:, g], psC[:, g, 0:3 * P], k.c("le3"), ALU.mult)
                    ch.link(ins)
                dve.wait_ge(xT_done, 1)
                for blk in range(SB):
                    dve.tensor_tensor(xd[:, blk], psT[:, blk].rearrange("p (h c) -> p h c", h=8),
                                      bc(dt[:, blk], 64, 2), ALU.mult).then_inc(xd_ready, 1)
                for h in range(8):
                    dve.wait_ge(E_ready, h + 1)
                    if h >= 2:
                        dve.wait_ge(y_done, h - 1)
                    dve.tensor_tensor(M[:, h % 2], E[:, h % 2], cb[:, h // 4], ALU.mult).then_inc(M_ready, 1)
                dve.wait_ge(y_done, 8)
                for t in range(4):
                    ins = dve.scalar_tensor_tensor(y[:, t], cx[:, t], vec("ssd_d", t), psYt[:, t], ALU.mult, ALU.add)
                    ch.link(ins)
                dve.wait_ge(z_sig, 1)
                ch.link(dve.tensor_tensor(y[:, 0:4], y[:, 0:4], b.z[:], ALU.mult))
                ch.link(dve.tensor_tensor(y[:, 0:4], y[:, 0:4], sg[:, 0:4], ALU.mult))
                dve.tensor_tensor(sq[:], y[:, 0:4], y[:, 0:4], ALU.mult).then_inc(squares, 1)
                dve.wait_ge(rstd_ready, 1)
                for t in range(4):
                    dve.scalar_tensor_tensor(y[:, t], y[:, t], vec("ssd_norm", t), rstd[:, t // 2], ALU.mult, ALU.mult)

            @block.scalar
            def _(act):
                ch = Chain(act, act_step)
                act.wait_ge(dt_pre, 1)
                ch.link(act.activation(ea[:], vecn("a_log"), ACT.Exp))
                ch.link(act.activation(tmp[:], tmp[:], ACT.Exp, scale=-1.0))
                act.activation(tmp[:], tmp[:], ACT.Ln, bias=k.eps[1.0]).then_inc(dt_exp, 1)
                act.wait_ge(conv_ready, 6)
                act.activation(sg[:], cx[:], ACT.Sigmoid).then_inc(sig_ready, 1)
                act.wait_ge(x_ready, 1)
                act.activation(sg[:, 0:4], b.z[:], ACT.Sigmoid).then_inc(z_sig, 1)
                for h in range(8):
                    act.wait_ge(decay_done, h + 1)
                    if h >= 2:
                        act.wait_ge(M_ready, h - 1)
                    act.activation(E[:, h % 2], psD[:, h % 2, 0:3 * P], ACT.Exp).then_inc(E_ready, 1)
                act.wait_ge(sums, 1)
                ch.link(act.activation(lnv[:].rearrange("p g s -> p (g s)"), psT[:, 0], ACT.Ln, bias=k.eps[RMS_EPS],
                                       scale=1.0 / 256))
                act.activation(rstd[:], lnv[:], ACT.Exp, scale=-0.5).then_inc(rstd_ready, 1)

            @block.tensor
            def _(pe):
                def decay(h):
                    pe.wait_ge(G_ready, 2 * h + 2)
                    if h >= 2:
                        pe.wait_ge(E_ready, h - 1)
                    d = psD[:, h % 2]
                    le3 = k.c("le3")
                    pe.matmul(d[:, 0:2 * P], G[:, 0, h], le3[:, 0:2 * P], start=True, stop=False)
                    pe.matmul(d[:, P:2 * P], dta[:, 1, h:h + 1].broadcast_to([P, P]), le3[:, 0:P], start=False, stop=True)
                    pe.matmul(d[:, 2 * P:3 * P], G[:, 1, h], le3[:, 0:P], start=True, stop=True).then_inc(decay_done, 1)

                decay(0)
                decay(1)
                pe.wait_ge(x_ready, 1)
                for g in range(2):
                    rows = slice(64 * g, 64 * g + 64)
                    pe.matmul(psC[:, g, 0:S], cx[rows, 4, 0:P], cx[rows, 5], start=True, stop=True)
                    ins = pe.matmul(psC[:, g, S:S + P], cx[rows, 4, P:S], cx[rows, 5, P:S], start=True, stop=True)
                ins.then_inc(cb_done, 1)
                for blk in range(SB):
                    for t in range(4):
                        ins = pe.transpose(psT[:, blk, t * P:(t + 1) * P], cx[:, t, blk * P:(blk + 1) * P], k.c("ident"))
                ins.then_inc(xT_done, 1)
                pe.wait_ge(xd_ready, 2)
                for h in range(8):
                    pe.wait_ge(M_ready, h + 1)
                    rows, t = slice(64 * (h % 2), 64 * (h % 2) + 64), h // 2
                    pe.matmul(psYt[rows, t], xd[:, 0, h], M[:, h % 2, 0:S], start=True, stop=False)
                    pe.matmul(psYt[rows, t, P:S], xd[:, 1, h], M[:, h % 2, S:S + P], start=False, stop=True)\
                        .then_inc(y_done, 1)
                    if h + 2 < 8:
                        decay(h + 2)
                pe.wait_ge(squares, 1)
                for g in range(2):
                    for t in range(2):
                        ins = pe.matmul(psT[:, 0, g * S:(g + 1) * S], k.c("ones"), sq[:, 2 * g + t],
                                        start=t == 0, stop=t == 1)
                ins.then_inc(sums, 1)


def stage_rwkv(nc, k, vecs, b, lr_dram, L, y):
    with Stage(nc, "rwkv") as st:
        lrw = st.sb("lrw", [P, 256])
        ps_ = st.sb("shifted", [P, 7, S])
        lact = st.sb("lact", [P, S])
        wa = st.sb("wa", [P, 4, S])
        gg = st.sb("gg", [P, 2, S])
        cum = st.sb("cum", [P, 2, S])
        ex = st.sb("ex", [P, 3, 2, S])
        kk = st.sb("kk", [P, 2, S])
        t1 = st.sb("t1", [P, 2, S])
        t2 = st.sb("t2", [P, 2, S])
        F = st.sb("F", [P, 4, 2, S])
        A_, B_, K_, R_ = range(4)
        tok = st.sb("tok", [P, 4, SB, 256])
        U = HEADS * SB
        mN = st.sb("mN", [P, 2, U, P])
        mX = st.sb("mX", [P, U, P])
        mM = st.sb("mM", [P, 3, U, P])
        W = st.sb("W", [P, 3, SB, HEADS, 64])
        QT = st.sb("QT", [P, CPB, SB * 2, P])
        EE = st.sb("EE", [P, CPB, SB * 2, P])
        St = st.sb("St", [P, NCH, 2, P])
        Rp = st.sb("Rp", [P, 2, S])
        yy = st.sb("yy", [P, 2, S])
        lnv = st.sb("lnv", [P, 2, S])
        rstd = st.sb("rstd", [P, 2, S])
        ps = st.ps("ps", [P, 8, 512])
        lr_loaded = st.sem("lr_loaded")
        dve_step, act_step = st.sem("dve_step"), st.sem("act_step")
        (low_ready, lact_ready, kksq_ready, low_done, logits_ready, kknorm_ready, sig_ready, gate_copied, sums_ready,
         exps_ready, F_ready, masked_done, masked, tok_done, tok_copied, power_done, power_copied, inv_done,
         inv_updated, mv_done, mv_copied, w_done, w_copied, q_done, e_done, q_ready, e_ready, state_done,
         state_ready, rp_done, rp_ready, intra_done, intra_copied, inter_done, yy_ready, bonus_ready, mean_done,
         bonus_done, sq_ready, var_done, rstd_ready) = [st.sem(n) for n in (
             "low_ready lact_ready kksq_ready low_done logits_ready kknorm_ready sig_ready gate_copied sums_ready "
             "exps_ready F_ready masked_done masked tok_done tok_copied power_done power_copied inv_done "
             "inv_updated mv_done mv_copied w_done w_copied q_done e_done q_ready e_ready state_done "
             "state_ready rp_done rp_ready intra_done intra_copied inter_done yy_ready bonus_ready mean_done "
             "bonus_done sq_ready var_done rstd_ready").split()]
        vec = lambda n, i=0: vecs[:, V2[n][0] + i:V2[n][0] + i + 1]
        flat = lambda a: a.rearrange("p a s -> p (a s)")
        unit = lambda h, blk: ((h % 2) * SB + blk) * 2 + h // 2
        ones64 = k.c("ones64")
        bank2 = lambda i: ps[:, i:i + 2].rearrange("p b (u n) -> p (b u) n", u=4)
        r_, k_, v_ = ps_[:, 0:2], ps_[:, 2:4], ps_[:, 4:6]

        with nc.Block() as block:

            @block.sync
            def _(sp):
                sp.dma_start(lrw[:], lr_dram[bass.ds(L, 1)].rearrange("a p n -> (a p) n")).then_inc(lr_loaded, 16)

            @block.vector
            def _(dve):
                ch = Chain(dve, dve_step)
                ch.link(dve.tensor_tensor(ps_[:], b.rw[:, :, 0:S], b.rw[:, :, 1:], ALU.subtract))
                dve.scalar_tensor_tensor(ps_[:, 6], ps_[:, 6], vec("mu", 6), b.rw[:, 6, 1:], ALU.mult, ALU.add)\
                    .then_inc(low_ready, 1)
                for t in (2, 3, 0, 1, 4, 5):
                    ins = dve.scalar_tensor_tensor(ps_[:, t], ps_[:, t], vec("mu", t), b.rw[:, t, 1:], ALU.mult, ALU.add)
                ch.link(ins)
                for t in range(2):
                    ins = dve.tensor_scalar(kk[:, t], k_[:, t], vec("k_k", t), None, ALU.mult)
                ch.link(ins)
                dve.tensor_tensor(t1[:], kk[:], kk[:], ALU.mult).then_inc(kksq_ready, 1)
                dve.wait_ge(low_done, 1)
                for t in range(4):
                    ins = dve.tensor_scalar(wa[:, t], ps[:, t // 2, (t % 2) * S:(t % 2 + 1) * S],
                                            vec("w0" if t < 2 else "a0", t % 2), None, ALU.add)
                ins.then_inc(logits_ready, 1)
                dve.wait_ge(kknorm_ready, 1)
                ch.link(dve.tensor_tensor(kk[:], kk[:], rstd[:], ALU.mult))
                dve.wait_ge(sig_ready, 1)
                ch.link(dve.tensor_scalar(wa[:, 0:2], wa[:, 0:2], -float(np.exp(-0.5)), None, ALU.mult))
                ch.link(dve.tensor_tensor_scan(flat(cum[:]), k.c("keep"), flat(wa[:, 0:2]), 0.0, ALU.mult, ALU.add))
                dve.tensor_tensor(t2[:], cum[:], wa[:, 0:2], ALU.subtract).then_inc(sums_ready, 1)
                for t in range(2):
                    ins = dve.tensor_scalar(t1[:, t], wa[:, 2 + t], 1.0, vec("k_a", t), ALU.subtract, ALU.mult)
                ch.link(ins)
                ch.link(dve.scalar_tensor_tensor(k_, t1[:], 1.0, k_, ALU.add, ALU.mult))
                ch.link(dve.tensor_tensor(t1[:], kk[:], wa[:, 2:4], ALU.mult))
                dve.wait_ge(exps_ready, 1)
                dve.scalar_tensor_tensor(F[:, A_], kk[:], -1.0, ex[:, 2], ALU.mult, ALU.mult)
                dve.tensor_tensor(F[:, B_], t1[:], ex[:, 1], ALU.mult)
                dve.tensor_tensor(F[:, K_], k_, ex[:, 1], ALU.mult)
                dve.tensor_tensor(F[:, R_], r_, ex[:, 0], ALU.mult).then_inc(F_ready, 1)
                for i, m in enumerate(("cl_strict", "cu_strict", "cu_strict", "cu_incl", "cu_incl")):
                    dst = mN[:, i] if i < 2 else mM[:, i - 2]
                    dve.wait_ge(masked_done, i + 1)
                    dve.tensor_tensor(dst, bank2(2 * (i % 3)), bc(k.c(m), U, 1), ALU.mult).then_inc(masked, 1)
                    if i == 1:
                        dve.wait_ge(masked, 2)
                        ch.link(dve.tensor_tensor(mX[:], mN[:, 1], bc(k.c("ident"), U, 1), ALU.add))
                for j in range(4):
                    dve.wait_ge(inv_done, j + 1)
                    dve.tensor_tensor(mX[:], mX[:], bank2(4), ALU.add).then_inc(inv_updated, 1)
                    dve.wait_ge(inv_updated, j + 1)
                dve.wait_ge(w_done, 1)
                dve.tensor_copy(W[:, 2].rearrange("p b h c -> p (b h c)"), ps[:, 7]).then_inc(w_copied, 1)
                dve.wait_ge(q_done, 1)
                psQ = ps[:, 0:4].rearrange("p j (n c) -> p (j n) c", n=4)
                qt = QT[:].rearrange("p j n c -> p (j n) c")
                ch.link(dve.tensor_tensor(qt, psQ, bc(ones64, 16, 1), ALU.mult))
                dve.tensor_tensor(qt, qt, bc(k.c("ident"), 16, 1), ALU.add).then_inc(q_ready, 1)
                dve.wait_ge(e_done, 1)
                for c in range(NCH):
                    for pr in range(2):
                        j, n = c % CPB, (c // CPB) * 2 + pr
                        ins = dve.scalar_tensor_tensor(EE[:, j, n], ps[:, 4 + j, n * P:(n + 1) * P],
                                                       ex[:, 0, pr, C * c + C - 1:C * c + C], ones64, ALU.mult, ALU.mult)
                ins.then_inc(e_ready, 1)
                dve.wait_ge(e_ready, 1)
                dve.tensor_copy(St[:, 1], EE[:, 0, 0:2]).then_inc(state_ready, 1)
                dve.wait_ge(rp_done, 1)
                dve.tensor_tensor(flat(Rp[:]), flat(F[:, R_]), ps[:, 2], ALU.add).then_inc(rp_ready, 1)
                for c in range(1, NCH - 1):
                    dve.wait_ge(state_done, c)
                    for pr in range(2):
                        ins = dve.scalar_tensor_tensor(St[:, c + 1, pr], ps[:, pr, (c % 4) * P:(c % 4 + 1) * P],
                                                       ex[:, 0, pr, C * c + C - 1:C * c + C],
                                                       EE[:, c % CPB, (c // CPB) * 2 + pr], ALU.mult, ALU.add)
                    ins.then_inc(state_ready, 1)
                for t in range(2):
                    ins = dve.scalar_tensor_tensor(t1[:, t], r_[:, t], vec("r_k", t), k_[:, t], ALU.mult, ALU.mult)
                ins.then_inc(bonus_ready, 1)
                dve.wait_ge(intra_copied, 1)
                dve.wait_ge(inter_done, 1)
                psI = ps[:, 4].rearrange("p (a s) -> p a s", a=2)
                dve.tensor_tensor(yy[:, :, C:], yy[:, :, C:], psI[:, :, C:], ALU.add).then_inc(yy_ready, 1)
                dve.wait_ge(mean_done, 1)
                ch.link(dve.scalar_tensor_tensor(flat(yy[:]), ps[:, 5], -1.0 / 64, flat(yy[:]), ALU.mult, ALU.add))
                dve.tensor_tensor(t2[:], yy[:], yy[:], ALU.mult).then_inc(sq_ready, 1)
                dve.wait_ge(bonus_done, 1)
                ch.link(dve.tensor_tensor(flat(v_), ps[:, 6], flat(v_), ALU.mult))
                dve.wait_ge(rstd_ready, 1)
                for t in range(2):
                    ins = dve.scalar_tensor_tensor(yy[:, t], yy[:, t], vec("ln_g", t), rstd[:, t], ALU.mult, ALU.mult)
                ch.link(ins)
                for t in range(2):
                    ins = dve.scalar_tensor_tensor(yy[:, t], yy[:, t], vec("ln_b", t), v_[:, t], ALU.add, ALU.add)
                ch.link(ins)
                dve.wait_ge(gate_copied, 1)
                dve.tensor_tensor(y[:, 4:6], yy[:], gg[:], ALU.mult)

            @block.scalar
            def _(act):
                ch = Chain(act, act_step)
                act.wait_ge(low_ready, 1)
                act.activation(lact[0:32, :], ps_[0:32, 6], ACT.Tanh)
                act.activation(lact[32:64, :], ps_[32:64, 6], ACT.Copy)
                act.activation(lact[64:128, :], ps_[64:128, 6], ACT.Sigmoid).then_inc(lact_ready, 1)
                act.wait_ge(low_done, 1)
                act.activation(flat(gg[:]), ps[:, 2], ACT.Copy).then_inc(gate_copied, 1)
                ch.link(act.activation(flat(lnv[:]), ps[:, 3], ACT.Ln, bias=k.eps[1e-12]))
                act.activation(rstd[:], lnv[:], ACT.Exp, scale=-0.5).then_inc(kknorm_ready, 1)
                act.wait_ge(logits_ready, 1)
                act.activation(wa[:], wa[:], ACT.Sigmoid).then_inc(sig_ready, 1)
                act.wait_ge(sums_ready, 1)
                act.activation(ex[:, 0], cum[:], ACT.Exp)
                act.activation(ex[:, 1], cum[:], ACT.Exp, scale=-1.0)
                act.activation(ex[:, 2], t2[:], ACT.Exp).then_inc(exps_ready, 1)
                for i in range(2):
                    act.wait_ge(tok_done, i + 1)
                    act.activation(tok[:, 2 * i].rearrange("p b f -> p (b f)"), ps[:, 6], ACT.Copy)
                    act.activation(tok[:, 2 * i + 1].rearrange("p b f -> p (b f)"), ps[:, 7], ACT.Copy)\
                        .then_inc(tok_copied, 1)
                act.wait_ge(mv_done, 1)
                act.activation(W[:, 0].rearrange("p b h c -> p (b h c)"), ps[:, 6], ACT.Copy).then_inc(mv_copied, 1)
                for j in range(4):
                    act.wait_ge(power_done, j + 1)
                    ins = act.activation(mN[:, 0], bank2(0), ACT.Copy)
                    if j < 3:
                        ins = act.activation(mN[:, 1], bank2(2), ACT.Copy)
                    ins.then_inc(power_copied, 1)
                act.wait_ge(w_done, 1)
                act.activation(W[:, 1].rearrange("p b h c -> p (b h c)"), ps[:, 6], ACT.Copy).then_inc(w_copied, 1)
                act.wait_ge(intra_done, 1)
                act.activation(flat(yy[:]), ps[:, 3], ACT.Copy).then_inc(intra_copied, 1)
                act.wait_ge(var_done, 1)
                ch.link(act.activation(flat(lnv[:]), ps[:, 7], ACT.Ln, bias=k.eps[64e-5], scale=1.0 / 64))
                act.activation(rstd[:], lnv[:], ACT.Exp, scale=-0.5).then_inc(rstd_ready, 1)

            @block.tensor
            def _(pe):
                def heads64(bank, src):
                    for t in range(2):
                        ins = pe.matmul(ps[:, bank, t * S:(t + 1) * S], ones64, src[:, t], start=True, stop=True)
                    return ins

                pe.wait_ge(lr_loaded, 16)
                pe.wait_ge(lact_ready, 1)
                for bank, rows in ((0, slice(0, 32)), (1, slice(32, 64)), (2, slice(64, 128))):
                    for t in range(2):
                        pe.matmul(ps[:, bank, t * S:(t + 1) * S], lrw[rows, t * P:(t + 1) * P], lact[rows, :],
                                  start=True, stop=True)
                pe.wait_ge(kksq_ready, 1)
                heads64(3, t1).then_inc(low_done, 1)
                pe.wait_ge(F_ready, 1)
                pe.wait_ge(gate_copied, 1)

                def transposes(srcs):
                    for bank, src in srcs:
                        for blk in range(SB):
                            for t in range(2):
                                ins = pe.transpose(ps[:, bank, (blk * 2 + t) * P:(blk * 2 + t + 1) * P],
                                                   src[:, t, blk * P:(blk + 1) * P], k.c("ident"))
                    ins.then_inc(tok_done, 1)

                for i, (a, c) in enumerate(((A_, B_), (B_, A_), (K_, A_), (B_, R_), (K_, R_))):
                    if i >= 3:
                        pe.wait_ge(masked, i - 2)
                    for h in range(HEADS):
                        rows = slice(64 * (h % 2), 64 * (h % 2) + 64)
                        for blk in range(SB):
                            cols = slice(blk * P, (blk + 1) * P)
                            ins = pe.matmul(bank2(2 * (i % 3))[:, unit(h, blk)], F[rows, a, h // 2, cols],
                                            F[rows, c, h // 2, cols], start=True, stop=True)
                    ins.then_inc(masked_done, 1)
                    if i == 1:
                        transposes(((6, F[:, A_]), (7, F[:, B_])))
                pe.wait_ge(tok_copied, 1)
                transposes(((6, F[:, K_]), (7, v_)))

                def squares(j):
                    for u in range(U):
                        ins = pe.matmul(bank2(0)[:, u], mN[:, 1, u], mN[:, 0, u], start=True, stop=True)
                    if j < 3:
                        for u in range(U):
                            ins = pe.matmul(bank2(2)[:, u], mN[:, 0, u], mN[:, 1, u], start=True, stop=True)
                    ins.then_inc(power_done, 1)

                pe.wait_ge(masked, 5)
                squares(0)
                pe.wait_ge(tok_copied, 2)
                for blk in range(SB):
                    for h in range(HEADS):
                        ins = pe.matmul(ps[:, 6, (blk * HEADS + h) * 64:(blk * HEADS + h + 1) * 64],
                                        mM[:, 0, unit(h, blk)], tok[:, 3, blk, h * 64:(h + 1) * 64], start=True, stop=True)
                ins.then_inc(mv_done, 1)
                for j in range(4):
                    pe.wait_ge(power_copied, j + 1)
                    if j >= 1:
                        pe.wait_ge(inv_updated, j)
                    for u in range(U):
                        ins = pe.matmul(bank2(4)[:, u], mN[:, 0, u], mX[:, u], start=True, stop=True)
                    ins.then_inc(inv_done, 1)
                    if j < 3:
                        squares(j + 1)
                pe.wait_ge(inv_updated, 4)
                pe.wait_ge(mv_copied, 1)
                for blk in range(SB):
                    for h in range(HEADS):
                        at = (blk * HEADS + h) * 64
                        pe.matmul(ps[:, 6, at:at + 64], mX[:, unit(h, blk)], W[:, 0, blk, h], start=True, stop=True)
                        ins = pe.matmul(ps[:, 7, at:at + 64], mX[:, unit(h, blk)], tok[:, A_, blk, h * 64:(h + 1) * 64],
                                        start=True, stop=True)
                ins.then_inc(w_done, 1)
                pe.wait_ge(w_copied, 2)
                Wp = W[:].rearrange("p w b h c -> p w b (h c)")
                for what, done in ((0, q_done), (1, e_done)):
                    for blk in range(SB):
                        for pr in range(2):
                            cols, n = slice(pr * P, (pr + 1) * P), blk * 2 + pr
                            for j in range(CPB):
                                rows = slice(C * j, C * j + C)
                                if what == 0:
                                    ins = pe.matmul(ps[:, j, n * P:(n + 1) * P], Wp[rows, 2, blk, cols],
                                                    tok[rows, B_, blk, cols], start=True, stop=True)
                                else:
                                    pe.matmul(ps[:, 4 + j, n * P:(n + 1) * P], tok[rows, B_, blk, cols],
                                              Wp[rows, 1, blk, cols], start=True, stop=False)
                                    ins = pe.matmul(ps[:, 4 + j, n * P:(n + 1) * P], tok[rows, K_, blk, cols],
                                                    tok[rows, 3, blk, cols], start=False, stop=True)
                    ins.then_inc(done, 1)
                pe.wait_ge(q_ready, 1)
                for h in range(HEADS):
                    rows = slice(64 * (h % 2), 64 * (h % 2) + 64)
                    for blk in range(SB):
                        at = (h // 2) * S + blk * P
                        ins = pe.matmul(ps[rows, 2, at:at + P], W[:, 2, blk, h], mM[:, 1, unit(h, blk)],
                                        start=True, stop=True)
                ins.then_inc(rp_done, 1)
                for h in range(HEADS):
                    rows = slice(64 * (h % 2), 64 * (h % 2) + 64)
                    for blk in range(SB):
                        at = (h // 2) * S + blk * P
                        pe.matmul(ps[rows, 3, at:at + P], W[:, 1, blk, h], mM[:, 1, unit(h, blk)], start=True, stop=False)
                        ins = pe.matmul(ps[rows, 3, at:at + P], tok[:, 3, blk, h * 64:(h + 1) * 64],
                                        mM[:, 2, unit(h, blk)], start=False, stop=True)
                ins.then_inc(intra_done, 1)
                pe.wait_ge(e_ready, 1)
                pe.wait_ge(rp_ready, 1)
                for c in range(1, NCH):
                    pe.wait_ge(state_ready, c)
                    if c < NCH - 1:
                        for pr in range(2):
                            ins = pe.matmul(ps[:, pr, (c % 4) * P:(c % 4 + 1) * P], QT[:, c % CPB, (c // CPB) * 2 + pr],
                                            St[:, c, pr], start=True, stop=True)
                        ins.then_inc(state_done, 1)
                    for pr in range(2):
                        ins = pe.matmul(ps[:, 4, pr * S + C * c:pr * S + C * (c + 1)], St[:, c, pr],
                                        Rp[:, pr, C * c:C * (c + 1)], start=True, stop=True)
                ins.then_inc(inter_done, 1)
                pe.wait_ge(bonus_ready, 1)
                heads64(6, t1).then_inc(bonus_done, 1)
                pe.wait_ge(yy_ready, 1)
                heads64(5, yy).then_inc(mean_done, 1)
                pe.wait_ge(sq_ready, 1)
                heads64(7, t2).then_inc(var_done, 1)


def stage_gla(nc, k, vecs, b, wa2_dram, L, y):
    with Stage(nc, "gla") as st:
        wa2 = st.sb("wa2", [N_GA, P])
        x1 = st.sb("x1", [P, S])
        x2 = st.sb("x2", [P, S])
        cum = st.sb("cum", [P, S])
        qt = st.sb("qt", [P, S])
        kt = st.sb("kt", [P, S])
        el = st.sb("el", [P, S])
        en = st.sb("en", [P, S])
        ktok = st.sb("ktok", [P, SB, P])
        sT = st.sb("sT", [P, HEADS, SB, P])
        EE = st.sb("EE", [P, CPB, SB, 256])
        St = st.sb("St", [P, NCH, 256])
        o = st.sb("o", [P, 2, S])
        sg = st.sb("sg", [P, 2, S])
        sq = st.sb("sq", [P, 2, S])
        lnv = st.sb("lnv", [P, 2, S])
        rstd = st.sb("rstd", [P, 2, S])
        ps = st.ps("ps", [P, 8, 512])
        (wa_loaded, dve_step, act_step, gate_done, abs_ready, ln_ready, sums_ready, exps_ready, qk_ready, k_done,
         k_copied, score_done, score_masked, intra_done, o_copied, e_done, states_ready, inter_done, sq_ready, sum_done,
         rstd_ready, sig_ready) = [st.sem(n) for n in (
             "wa_loaded dve_step act_step gate_done abs_ready ln_ready sums_ready exps_ready qk_ready k_done "
             "k_copied score_done score_masked intra_done o_copied e_done states_ready inter_done sq_ready sum_done "
             "rstd_ready sig_ready").split()]
        vec = lambda n, i=0: vecs[:, V2[n][0] + i:V2[n][0] + i + 1]
        vtok = b.tokm[:, :, 8:8 + 256]
        flat = lambda a: a.rearrange("p a s -> p (a s)")

        with nc.Block() as block:

            @block.sync
            def _(sp):
                sp.dma_start(wa2[:], wa2_dram[bass.ds(L, 1)].rearrange("a p n -> (a p) n")).then_inc(wa_loaded, 16)

            @block.vector
            def _(dve):
                ch = Chain(dve, dve_step)
                dve.wait_ge(gate_done, 1)
                ch.link(dve.tensor_scalar(x1[:], ps[:, 0, 0:S], vec("b_a"), None, ALU.add))
                ch.link(dve.tensor_scalar(x2[:], x1[:], -1.0, None, ALU.mult))
                dve.tensor_tensor(x2[:], x2[:], x1[:], ALU.max).then_inc(abs_ready, 1)
                ch.link(dve.tensor_scalar(x1[:], x1[:], 0.0, None, ALU.min))
                dve.wait_ge(ln_ready, 1)
                ch.link(dve.tensor_tensor(x1[:], x1[:], x2[:], ALU.subtract))
                ch.link(dve.tensor_scalar(x1[:], x1[:], 1.0 / 16, None, ALU.mult))
                dve.tensor_tensor_scan(cum[:], k.c("keep")[:, 0:S], x1[:], 0.0, ALU.mult, ALU.add).then_inc(sums_ready, 1)
                dve.wait_ge(exps_ready, 1)
                dve.scalar_tensor_tensor(qt[:], b.gl[:, 0], float(32 ** -0.5), el[:], ALU.mult, ALU.mult)
                dve.tensor_tensor(kt[:], b.gl[:, 1], en[:], ALU.mult).then_inc(qk_ready, 1)
                dve.wait_ge(score_done, 1)
                dve.tensor_tensor(sT[:], ps[:, 0:4, 0:SB * P].rearrange("p h (b c) -> p h b c", b=SB),
                                  bc(bc(k.c("cu_incl"), SB, 1), HEADS, 1), ALU.mult).then_inc(score_masked, 1)
                dve.wait_ge(e_done, 1)
                for c in range(NCH - 1):
                    j, blk = c % CPB, c // CPB
                    dst = St[:, 1] if c == 0 else EE[:, j, blk]
                    ins = dve.scalar_tensor_tensor(dst, ps[:, 4 + j, blk * 256:(blk + 1) * 256],
                                                   el[:, C * c + C - 1:C * c + C], k.c("gla_heads"), ALU.mult, ALU.mult)
                ch.link(ins)
                for c in range(1, NCH - 1):
                    ins = dve.scalar_tensor_tensor(St[:, c + 1], St[:, c], el[:, C * c + C - 1:C * c + C],
                                                   EE[:, c % CPB, c // CPB], ALU.mult, ALU.add)
                    ch.link(ins)
                dve.tensor_copy(St[:, 0, 0:1], St[:, NCH - 1, 0:1]).then_inc(states_ready, 1)
                dve.wait_ge(o_copied, 1)
                dve.wait_ge(inter_done, 1)
                psI = ps[:, 6].rearrange("p (a s) -> p a s", a=2)
                ch.link(dve.tensor_tensor(o[:, :, C:], o[:, :, C:], psI[:, :, C:], ALU.add))
                dve.tensor_tensor(sq[:], o[:], o[:], ALU.mult).then_inc(sq_ready, 1)
                dve.wait_ge(sig_ready, 1)
                ch.link(dve.tensor_tensor(sg[:], sg[:], b.gl[:, 2:4], ALU.mult))
                dve.wait_ge(rstd_ready, 1)
                for t in range(2):
                    ins = dve.scalar_tensor_tensor(o[:, t], o[:, t], vec("gla_norm", t), rstd[:, t], ALU.mult, ALU.mult)
                ch.link(ins)
                dve.tensor_tensor(y[:, 6:8], o[:], sg[:], ALU.mult)

            @block.scalar
            def _(act):
                ch = Chain(act, act_step)
                act.activation(sg[:], b.gl[:, 2:4], ACT.Sigmoid).then_inc(sig_ready, 1)
                act.wait_ge(abs_ready, 1)
                ch.link(act.activation(x2[:], x2[:], ACT.Exp, scale=-1.0))
                act.activation(x2[:], x2[:], ACT.Ln, bias=k.eps[1.0]).then_inc(ln_ready, 1)
                act.wait_ge(sums_ready, 1)
                act.activation(el[:], cum[:], ACT.Exp)
                act.activation(en[:], cum[:], ACT.Exp, scale=-1.0).then_inc(exps_ready, 1)
                act.wait_ge(k_done, 1)
                act.activation(flat(ktok[:]), ps[:, 7, 0:SB * P], ACT.Copy).then_inc(k_copied, 1)
                act.wait_ge(intra_done, 1)
                act.activation(flat(o[:]), ps[:, 0], ACT.Copy).then_inc(o_copied, 1)
                act.wait_ge(sum_done, 1)
                ch.link(act.activation(flat(lnv[:]), ps[:, 1], ACT.Ln, bias=k.eps[RMS_EPS], scale=1.0 / 64))
                act.activation(rstd[:], lnv[:], ACT.Exp, scale=-0.5).then_inc(rstd_ready, 1)

            @block.tensor
            def _(pe):
                pe.wait_ge(wa_loaded, 16)
                pe.matmul(ps[:, 0, 0:S], wa2[:], b.ga[0:N_GA, :], start=True, stop=True).then_inc(gate_done, 1)
                pe.wait_ge(qk_ready, 1)
                for blk in range(SB):
                    ins = pe.transpose(ps[:, 7, blk * P:(blk + 1) * P], kt[:, blk * P:(blk + 1) * P], k.c("ident"))
                ins.then_inc(k_done, 1)
                for blk in range(SB):
                    cols = slice(blk * P, (blk + 1) * P)
                    for h in range(HEADS):
                        rows = slice(32 * h, 32 * h + 32)
                        ins = pe.matmul(ps[:, h, cols], kt[rows, cols], qt[rows, cols], start=True, stop=True,
                                        tile_position=(32 * h, 0) if h == 3 else None)
                ins.then_inc(score_done, 1)
                pe.wait_ge(k_copied, 1)
                for blk in range(SB):
                    for j in range(CPB):
                        rows = slice(C * j, C * j + C)
                        ins = pe.matmul(ps[:, 4 + j, blk * 256:(blk + 1) * 256], ktok[rows, blk], vtok[rows, blk],
                                        start=True, stop=True, tile_position=(32 * j, 0) if j == 3 else None)
                ins.then_inc(e_done, 1)
                pe.wait_ge(score_masked, 1)
                for h in range(HEADS):
                    rows = slice(64 * (h % 2), 64 * (h % 2) + 64)
                    for blk in range(SB):
                        at = (h // 2) * S + blk * P
                        ins = pe.matmul(ps[rows, 0, at:at + P], vtok[:, blk, h * 64:(h + 1) * 64], sT[:, h, blk],
                                        start=True, stop=True)
                ins.then_inc(intra_done, 1)
                pe.wait_ge(states_ready, 1)
                for c in range(1, NCH):
                    for pr in range(2):
                        ins = pe.matmul(ps[:, 6, pr * S + C * c:pr * S + C * (c + 1)], St[:, c, pr * P:(pr + 1) * P],
                                        qt[:, C * c:C * (c + 1)], start=True, stop=True)
                ins.then_inc(inter_done, 1)
                pe.wait_ge(sq_ready, 1)
                for t in range(2):
                    ins = pe.matmul(ps[:, 1, t * S:(t + 1) * S], k.c("ones64"), sq[:, t], start=True, stop=True)
                ins.then_inc(sum_done, 1)


def stage_output2(nc, k, L, vecs, y, w_dram):
    with Stage(nc, "output2") as st:
        unit = 2 * DT * P
        w = Stream(st, "w", [unit] * 4, 4)
        ys = Halves(st, "ys", DT)
        xr = st.sb("xr", [P, DT, S])
        ps = st.ps("ps", [P, 4, 512])
        added, dve_step = st.sem("added"), st.sem("dve_step")
        g, bb = V2["ln1_g"][0], V2["ln1_b"][0]
        n_vec, n_act, n_pe, normed = norm_engines(k, st, xr, k.x, vecs[:, g:g + DT], LN_EPS, vecs[:, bb:bb + DT])
        with nc.Block() as block:

            @block.sync
            def _(sp):
                for i in range(4):
                    w.load(sp, i, w_dram[bass.ds(L, 1), :, i * unit:(i + 1) * unit].rearrange("a p n -> (a p) n"))

            @block.vector
            def _(dve):
                ys.rest(dve, y, 2)
                w.rest(dve, 0)
                w.rest(dve, 1)
                for m in range(4):
                    dve.wait_ge(w.used, m + 1)
                    xm = lambda a: a[:, 2 * m:2 * m + 2].rearrange("p a s -> p (a s)")
                    dve.scalar_tensor_tensor(xm(xr), xm(k.x), ALPHA, ps[:, m], ALU.mult, ALU.add).then_inc(added, 1)
                    if m + 2 < 4:
                        w.rest(dve, m + 2)
                dve.wait_ge(added, 4)
                n_vec(dve, Chain(dve, dve_step))

            @block.scalar
            def _(act):
                ys.round(act, y, None, 2)
                for i in range(4):
                    w.round(act, i)
                n_act(act)

            @block.tensor
            def _(pe):
                pe.wait_ge(ys.split, DT)
                for i in range(4):
                    w.ready(pe, i)
                    for m in range(2):
                        ins = product3(pe, ps[:, i, m * S:(m + 1) * S], at(w.weights(i, m * DT, DT)), ys.tiles(), DT)
                    ins.then_inc(w.used, 1)
                pe.wait_ge(added, 4)
                n_pe(pe)


class Buffers:
    pass


def make_buffers(nc, ctx):
    b = Buffers()

    def sb(name, shape):
        return ctx.enter_context(nc.sbuf_tensor(name, shape, F32))

    b.vecs = sb("vecs2", [P, N_V2])
    b.y = sb("y2", [P, DT, S])
    b.z = sb("z2", [P, 4, S])
    b.xbc = sb("xbc2", [P, 6, S + 3])
    b.rw = sb("rw2", [P, 7, S + 1])
    b.gl = sb("gl2", [P, 4, S])
    b.ga = sb("ga2", [P, S])
    b.tokm = sb("tokm2", [P, SB, N_TOKM])
    with Stage(nc, "pads") as st:
        padded = st.sem("padded")
        with nc.Block() as block:

            @block.vector
            def _(dve):
                dve.memset(b.xbc[:, :, 0:3], 0.0).then_inc(padded, 1)
                dve.memset(b.rw[:, :, 0:1], 0.0).then_inc(padded, 1)
                dve.wait_ge(padded, 2)
    return b


class Routes:
    pass


def make_routes(nc, ctx):
    m = Routes()

    def sb(name, shape, dt=F32):
        return ctx.enter_context(nc.sbuf_tensor(name, shape, dt))

    m.parts = sb("parts", [P, 3, SB, D], BF16)
    m.slot = sb("slot", [P, SB, N_PASS])
    m.gate = sb("gate", [P, SB, N_PASS])
    m.over_expert = sb("over_expert", [P, N_OVER], I32)
    m.n_over = sb("n_over", [P, 1], I32)
    return m


def stage_route(nc, k, L, vecs, w_dram, m):
    with Stage(nc, "route") as st:
        w = st.sb("w", [P, DT, N_ROUTE])
        lg = st.sb("lg", [P, SB, N_ROUTE])
        r1 = st.sb("r1", [P, SB, D])
        one = st.sb("one", [P, 12, SB])
        grp = st.sb("grp", [P, 4, SB, N_GROUPS])
        sel = st.sb("sel", [P, SB, EPG, N_GROUPS])
        e8 = st.sb("e8", [P, 8, SB, EPG])
        A = st.sb("A", [P, SB, N_EXP])
        row = st.sb("row", [P, 5, N_EXP])
        big = st.sb("big", [P, 4, N_OVER, N_EXP])
        bigt = st.sb("bigt", [P, SB, N_OVER, N_EXP])
        onef = st.sb("onef", [P, 3, N_OVER])
        ps = st.ps("ps", [P, 4, 512])
        psl = st.ps("psl", [P, 512])
        psr = st.ps("psr", [P, 512])
        (w_loaded, dve_step, xT_done, logits_done, hi_ready, mid_ready, rest_ready, parts_ready, gexp_pre, gexp_ready,
         eexp_pre, eexp_ready, assigned, ranked) = [st.sem(n) for n in (
             "w_loaded dve_step xT_done logits_done hi_ready mid_ready rest_ready parts_ready gexp_pre gexp_ready "
             "eexp_pre eexp_ready assigned ranked").split()]
        b0 = V2["b_route"][0]
        G4, OH, GX, GE = range(4)

        with nc.Block() as block:

            @block.sync
            def _(sp):
                sp.dma_start(w[:], w_dram[bass.ds(L, 1)].rearrange("a p (k c) -> (a p) k c", k=DT)).then_inc(w_loaded, 16)

            @block.vector
            def _(dve):
                ch = Chain(dve, dve_step)
                link = ch.link

                def one_hot(dst, key, x, mx, n):
                    link(dve.tensor_tensor(key, x, bc(mx, n, 2), ALU.is_equal))
                    link(dve.tensor_tensor(key, key, bc(k.c("rank")[:, 0:n], SB, 1), ALU.mult))
                    link(dve.reduce_max(one[:, 11], key, AX.X))
                    link(dve.tensor_tensor(dst, key, bc(one[:, 11], n, 2), ALU.is_equal))

                dve.wait_ge(logits_done, 1)
                link(dve.tensor_tensor(lg[:], psl[:, 0:SB * N_ROUTE].rearrange("p (b c) -> p b c", b=SB),
                                       bc(vecs[:, b0:b0 + N_ROUTE], SB, 1), ALU.add))
                gl = lg[:, :, 0:N_GROUPS]
                link(dve.reduce_max(one[:, 0], gl, AX.X))
                one_hot(grp[:, OH], grp[:, G4], gl, one[:, 0], N_GROUPS)
                dve.tensor_tensor(grp[:, GX], gl, bc(one[:, 0], N_GROUPS, 2), ALU.subtract).then_inc(gexp_pre, 1)
                link(dve.tensor_tensor(sel[:].rearrange("p b e g -> p b g e"),
                                       lg[:, :, N_GROUPS:].rearrange("p b (g e) -> p b g e", g=N_GROUPS),
                                       bc(grp[:, OH], EPG, 3), ALU.mult))
                link(dve.tensor_reduce(e8[:, 0], sel[:], AX.X, ALU.add))
                link(dve.reduce_max(one[:, 1], e8[:, 0], AX.X))
                one_hot(e8[:, 1], e8[:, 3], e8[:, 0], one[:, 1], EPG)
                link(dve.scalar_tensor_tensor(e8[:, 4], e8[:, 1], NEG, e8[:, 0], ALU.mult, ALU.add))
                link(dve.reduce_max(one[:, 2], e8[:, 4], AX.X))
                one_hot(e8[:, 2], e8[:, 3], e8[:, 4], one[:, 2], EPG)
                dve.tensor_tensor(one[:, 3], one[:, 2], one[:, 1], ALU.subtract).then_inc(eexp_pre, 1)
                dve.wait_ge(gexp_ready, 1)
                link(dve.tensor_reduce(one[:, 4], grp[:, GE], AX.X, ALU.add))
                link(dve.reciprocal(one[:, 5], one[:, 4]))
                dve.wait_ge(eexp_ready, 1)
                link(dve.tensor_scalar(one[:, 7], one[:, 6], 1.0, None, ALU.add))
                link(dve.reciprocal(one[:, 8], one[:, 7]))
                link(dve.tensor_tensor(one[:, 9], one[:, 8], one[:, 5], ALU.mult))
                link(dve.tensor_tensor(one[:, 10], one[:, 9], one[:, 6], ALU.mult))
                link(dve.tensor_tensor(e8[:, 5], e8[:, 1], e8[:, 2], ALU.add))
                link(dve.tensor_tensor(e8[:, 6], e8[:, 1], bc(one[:, 9], EPG, 2), ALU.mult))
                link(dve.tensor_tensor(e8[:, 7], e8[:, 2], bc(one[:, 10], EPG, 2), ALU.mult))
                link(dve.tensor_tensor(e8[:, 6], e8[:, 6], e8[:, 7], ALU.add))
                for blk in range(SB):
                    grid = lambda a: a[:, blk].rearrange("p (g e) -> p g e", g=N_GROUPS)
                    ins = dve.tensor_tensor(grid(A), bc(e8[:, 5, blk], N_GROUPS, 1), bc(grp[:, OH, blk], EPG, 2), ALU.mult)
                    link(dve.tensor_tensor(m.gate[:, blk, 0:N_EXP].rearrange("p (g e) -> p g e", g=N_GROUPS),
                                           bc(e8[:, 6, blk], N_GROUPS, 1), bc(grp[:, OH, blk], EPG, 2), ALU.mult))
                dve.tensor_copy(row[:, 0], A[:, 1]).then_inc(assigned, 1)
                dve.wait_ge(hi_ready, 1)
                x4 = ps[:].rearrange("p (b q) n -> p b (q n)", b=SB)
                dve.tensor_tensor(r1[:], x4, m.parts[:, 0], ALU.subtract).then_inc(rest_ready, 1)
                dve.wait_ge(ranked, 1)
                rank = psr[:, 0:SB * N_EXP].rearrange("p (b e) -> p b e", b=SB)
                slot = m.slot[:, :, 0:N_EXP]
                link(dve.scalar_tensor_tensor(slot, rank, 1.0, A[:], ALU.add, ALU.mult))
                link(dve.tensor_scalar(slot, slot, -1.0, None, ALU.add))
                cnt = psr[:, SB * N_EXP:(SB + 1) * N_EXP]
                link(dve.tensor_scalar(row[:, 1], cnt, float(SLOTS), None, ALU.is_gt))
                for n in (2, 3):
                    link(dve.tensor_scalar(row[:, 2], cnt, float(n * SLOTS), None, ALU.is_gt))
                    link(dve.tensor_tensor(row[:, 1], row[:, 1], row[:, 2], ALU.add))
                link(dve.tensor_tensor_scan(row[:, 3], k.c("ones")[:, 0:N_EXP], row[:, 1], 0.0, ALU.mult, ALU.add))
                link(dve.tensor_tensor(row[:, 4], row[:, 3], row[:, 1], ALU.subtract))
                link(dve.tensor_copy(m.n_over[:], row[:, 3, N_EXP - 1:N_EXP]))
                grid = lambda n: k.c(n).rearrange("p (s e) -> p s e", s=N_OVER)
                link(dve.tensor_tensor(big[:, 0], bc(row[:, 3], N_OVER, 1), grid("steps"), ALU.is_gt))
                link(dve.tensor_tensor(big[:, 1], bc(row[:, 4], N_OVER, 1), grid("steps"), ALU.is_le))
                link(dve.tensor_tensor(big[:, 0], big[:, 0], big[:, 1], ALU.mult))
                link(dve.tensor_tensor(big[:, 1], big[:, 0], grid("experts"), ALU.mult))
                link(dve.tensor_reduce(onef[:, 0], big[:, 1], AX.X, ALU.add))
                link(dve.tensor_copy(m.over_expert[:], onef[:, 0]))
                link(dve.tensor_tensor(big[:, 2], grid("steps"), bc(row[:, 4], N_OVER, 1), ALU.subtract))
                link(dve.scalar_tensor_tensor(big[:, 2], big[:, 2], 1.0, big[:, 0], ALU.add, ALU.mult))
                link(dve.tensor_reduce(onef[:, 1], big[:, 2], AX.X, ALU.add))
                link(dve.tensor_scalar(onef[:, 2], onef[:, 1], float(SLOTS), 1.0, ALU.mult, ALU.add))
                for blk in range(SB):
                    link(dve.scalar_tensor_tensor(bigt[:, blk], bc(m.slot[:, blk, 0:N_EXP], N_OVER, 1), 1.0, big[:, 0],
                                                  ALU.add, ALU.mult))
                    link(dve.tensor_reduce(m.slot[:, blk, N_EXP:], bigt[:, blk], AX.X, ALU.add))
                    link(dve.tensor_tensor(m.slot[:, blk, N_EXP:], m.slot[:, blk, N_EXP:], onef[:, 2], ALU.subtract))
                    link(dve.tensor_tensor(bigt[:, blk], bc(m.gate[:, blk, 0:N_EXP], N_OVER, 1), big[:, 0], ALU.mult))
                    link(dve.tensor_reduce(m.gate[:, blk, N_EXP:], bigt[:, blk], AX.X, ALU.add))
                dve.wait_ge(mid_ready, 1)
                dve.tensor_tensor(r1[:], r1[:], m.parts[:, 1], ALU.subtract).then_inc(rest_ready, 1)

            @block.scalar
            def _(act):
                act.wait_ge(gexp_pre, 1)
                act.activation(grp[:, GE], grp[:, GX], ACT.Exp).then_inc(gexp_ready, 1)
                act.wait_ge(xT_done, 1)
                x4 = ps[:].rearrange("p (b q) n -> p b (q n)", b=SB)
                act.activation(m.parts[:, 0], x4, ACT.Copy).then_inc(hi_ready, 1)
                act.wait_ge(eexp_pre, 1)
                act.activation(one[:, 6], one[:, 3], ACT.Exp).then_inc(eexp_ready, 1)
                act.wait_ge(rest_ready, 1)
                act.activation(m.parts[:, 1], r1[:], ACT.Copy).then_inc(mid_ready, 1)
                act.wait_ge(rest_ready, 2)
                act.activation(m.parts[:, 2], r1[:], ACT.Copy).then_inc(parts_ready, 1)

            @block.tensor
            def _(pe):
                pe.wait_ge(w_loaded, 16)
                for blk in range(SB):
                    for kk in range(DT):
                        ins = pe.matmul(psl[:, blk * N_ROUTE:(blk + 1) * N_ROUTE], k.x[:, kk, blk * P:(blk + 1) * P],
                                        w[:, kk], start=kk == 0, stop=kk == DT - 1)
                ins.then_inc(logits_done, 1)
                for blk in range(SB):
                    for t in range(DT):
                        at = blk * D + t * P
                        ins = pe.transpose(ps[:, at // 512, at % 512:at % 512 + P], k.x[:, t, blk * P:(blk + 1) * P],
                                           k.c("ident"))
                ins.then_inc(xT_done, 1)
                pe.wait_ge(assigned, 1)
                pe.matmul(psr[:, 0:N_EXP], k.c("lt"), A[:, 0], start=True, stop=True)
                pe.matmul(psr[:, N_EXP:2 * N_EXP], k.c("lt"), A[:, 1], start=True, stop=False)
                pe.matmul(psr[:, N_EXP:2 * N_EXP], k.c("ones"), A[:, 0], start=False, stop=True)
                pe.matmul(psr[:, 2 * N_EXP:3 * N_EXP], k.c("ones"), A[:, 0], start=True, stop=False)
                pe.matmul(psr[:, 2 * N_EXP:3 * N_EXP], k.c("ones"), A[:, 1], start=False, stop=True).then_inc(ranked, 1)


def stage_experts(nc, k, L, m, wg_dram, wu_dram, wd_dram, first, n, name, base_scale):
    with Stage(nc, name) as st:
        wgu = st.sb("wgu", [P, 2, 2, DT, EFF])
        wd = st.sb("wd", [P, 2, 4, D])
        selg = st.sb("selg", [P, 2, SB, P])
        selb = st.sb("selb", [P, 2, SB, SLOTS], BF16)
        selT = st.sb("selT", [P, 2, S])
        xc = st.sb("xc", [P, DT, SLOTS])
        sig = st.sb("sig", [P, S])
        hh = st.sb("hh", [P, S])
        hT = st.sb("hT", [P, 2, P])
        yc = st.sb("yc", [P, 512])
        zero = st.sb("zero", [P, 512])
        psG = st.ps("psG", [P, 512])
        psX = st.ps("psX", [P, 512])
        psS = st.ps("psS", [P, 512])
        psD = st.ps("psD", [P, 512])
        psY = st.ps("psY", [P, 4, 512])
        gu_loaded = [st.sem("gu_loaded0"), st.sem("gu_loaded1")]
        d_loaded = [st.sem("d_loaded0"), st.sem("d_loaded1")]
        (dve_step, zero_ready, sel_ready, gathered, xc_ready, gu_done, sig_ready, h_ready, selT_done, selT_ready,
         hT_done, hT_ready, down_done, yc_ready, scattered, y_done) = [st.sem(s) for s in (
             "dve_step zero_ready sel_ready gathered xc_ready gu_done sig_ready h_ready selT_done selT_ready "
             "hT_done hT_ready down_done yc_ready scattered y_done").split()]
        main = first == 0

        def passes(eng, body):
            body(0, 0, True, False)
            body(1, 1, False, False)
            with eng.Fori(1, n // 2 - 1) as it:
                body(2 * it, 0, False, False)
                body(2 * it + 1, 1, False, False)
            body(n - 2, 0, False, False)
            body(n - 1, 1, False, True)

        with nc.Block() as block:

            @block.sync
            def _(sp):
                def load(e, par, is_first, is_last):
                    if main:
                        at = L * N_EXP + e
                    else:
                        at = L * N_EXP + sp.value_load(m.over_expert[0:1, bass.ds(e, 1)], min_val=0, max_val=N_EXP - 1)
                    if not (isinstance(e, int) and e < 2):
                        sp.wait_ge(gu_done, e - 1)
                    for i, w in enumerate((wg_dram, wu_dram)):
                        sp.dma_start(wgu[:, par, i], w[bass.ds(at, 1)].rearrange("a (k p) n -> (a p) k n", p=P))\
                            .then_inc(gu_loaded[par], 16)
                    if not (isinstance(e, int) and e < 2):
                        sp.wait_ge(down_done, e - 1)
                    sp.dma_start(wd[:, par], wd_dram[bass.ds(at, 1)].rearrange("a (t p) n -> (a p) t n", p=P))\
                        .then_inc(d_loaded[par], 16)

                passes(sp, load)

            @block.vector
            def _(dve):
                ch = Chain(dve, dve_step)

                def select(e, par):
                    if not (isinstance(e, int) and e < 2):
                        dve.wait_ge(selT_done, e - 1)
                    for blk in range(SB):
                        col = m.slot[:, blk, bass.ds(first + e, 1)]
                        dve.tensor_scalar(selb[:, par, blk], k.c("slots")[:, 0:SLOTS], col, None, ALU.is_equal)
                        ins = dve.tensor_scalar(selg[:, par, blk], k.c("slots"), col, m.gate[:, blk, bass.ds(first + e, 1)],
                                                ALU.is_equal, ALU.mult)
                    ins.then_inc(sel_ready, 1)

                def step(e, par, is_first, is_last):
                    if not is_last:
                        select(e + 1, 1 - par)
                    dve.wait_ge(sig_ready, e + 1)
                    dve.tensor_tensor(sig[:], sig[:], psG[:, 0:S], ALU.mult).then_inc(dve_step, 1)
                    dve.wait_ge(dve_step, e + 1)
                    dve.tensor_tensor(hh[:], sig[:], psG[:, S:2 * S], ALU.mult).then_inc(h_ready, 1)

                dve.memset(zero[:], 0.0).then_inc(zero_ready, 1)
                select(0, 0)
                passes(dve, step)
                dve.wait_ge(y_done, 1)
                xf = k.x[:].rearrange("p (b t) s -> p b (t s)", b=4)
                dve.scalar_tensor_tensor(xf, xf, base_scale, psY[:], ALU.mult, ALU.add)

            @block.scalar
            def _(act):
                def take(e):
                    act.wait_ge(gathered, e + 1)
                    act.activation(xc[:].rearrange("p t c -> p (t c)"), psX[:], ACT.Copy).then_inc(xc_ready, 1)

                def step(e, par, is_first, is_last):
                    act.wait_ge(gu_done, e + 1)
                    if not is_first:
                        act.wait_ge(h_ready, e)
                    act.activation(sig[:], psG[:, 0:S], ACT.Sigmoid).then_inc(sig_ready, 1)
                    act.wait_ge(selT_done, e + 1)
                    if not (isinstance(e, int) and e < 2):
                        act.wait_ge(scattered, e - 1)
                    act.activation(selT[:, par], psS[:, 0:S], ACT.Copy).then_inc(selT_ready, 1)
                    if not is_last:
                        take(e + 1)
                    act.wait_ge(hT_done, e + 1)
                    act.activation(hT[:].rearrange("p c n -> p (c n)"), psS[:, S:2 * S], ACT.Copy).then_inc(hT_ready, 1)
                    act.wait_ge(down_done, e + 1)
                    act.activation(yc[:], psD[:], ACT.Copy).then_inc(yc_ready, 1)

                take(0)
                passes(act, step)

            @block.tensor
            def _(pe):
                def gather(e, par):
                    pe.wait_ge(sel_ready, e + 1)
                    for t in range(DT):
                        for i in range(3):
                            for blk in range(SB):
                                ins = pe.matmul(psX[:, t * SLOTS:(t + 1) * SLOTS], m.parts[:, i, blk, t * P:(t + 1) * P],
                                                selb[:, par, blk], start=i == 0 and blk == 0, stop=i == 2 and blk == SB - 1)
                    ins.then_inc(gathered, 1)

                def scatter(par, e):
                    pe.wait_ge(yc_ready, e + 1)
                    for t in range(4):
                        for i in range(2):
                            rows = slice(SLOTS * i, SLOTS * i + SLOTS)
                            ins = pe.matmul(psY[:, 2 * i + t // 2, (t % 2) * S:(t % 2 + 1) * S],
                                            yc[rows, t * P:(t + 1) * P], selT[rows, par], start=False, stop=False)
                    ins.then_inc(scattered, 1)

                def step(e, par, is_first, is_last):
                    pe.wait_ge(gu_loaded[par], (e + (2 - par)) * 16)
                    pe.wait_ge(xc_ready, e + 1)
                    if not is_first:
                        pe.wait_ge(h_ready, e)
                    for kk in range(DT):
                        for j in range(2):
                            out = psG[SLOTS * j:SLOTS * (j + 1), :].rearrange("p (g c) -> p g c", g=2)
                            ins = pe.matmul(out, xc[:, kk], wgu[:, par, :, kk, j * S:(j + 1) * S],
                                            start=kk == 0, stop=kk == DT - 1)
                    ins.then_inc(gu_done, 1)
                    if not is_first:
                        pe.wait_ge(hT_ready, e)
                    for blk in range(SB):
                        ins = pe.transpose(psS[:, blk * P:(blk + 1) * P], selg[:, par, blk], k.c("ident"))
                    ins.then_inc(selT_done, 1)
                    if not is_last:
                        gather(e + 1, 1 - par)
                    pe.wait_ge(h_ready, e + 1)
                    pe.wait_ge(selT_ready, e + 1)
                    for c in range(2):
                        ins = pe.transpose(psS[:, S + c * P:S + (c + 1) * P], hh[:, c * P:(c + 1) * P], k.c("ident"))
                    ins.then_inc(hT_done, 1)
                    if not is_first:
                        scatter(1 - par, e - 1)
                    pe.wait_ge(d_loaded[par], half_count(e, par))
                    pe.wait_ge(hT_ready, e + 1)
                    for j in range(2):
                        for c in range(2):
                            for i in range(2):
                                rows = slice(SLOTS * i, SLOTS * i + SLOTS)
                                ins = pe.matmul(psD[rows, :], hT[:, c, j * SLOTS:(j + 1) * SLOTS],
                                                wd[:, par, 2 * j + c, i * 512:(i + 1) * 512],
                                                start=j == 0 and c == 0, stop=j == 1 and c == 1)
                    ins.then_inc(down_done, 1)

                def half_count(e, par):
                    return (e + (2 - par)) * 8

                pe.wait_ge(zero_ready, 1)
                for i in range(4):
                    pe.matmul(psY[:, i], k.c("ident"), zero[:], start=True, stop=False)
                gather(0, 0)
                passes(pe, step)
                scatter((n - 1) % 2, n - 1)
                for i in range(4):
                    ins = pe.matmul(psY[:, i], k.c("ident"), zero[:], start=False, stop=True)
                ins.then_inc(y_done, 1)


def stage_norm2(nc, k, vecs):
    with Stage(nc, "norm2") as st:
        tmp = st.sb("tmp", [P, DT, S])
        dve_step = st.sem("dve_step")
        g, b = V2["ln2_g"][0], V2["ln2_b"][0]
        n_vec, n_act, n_pe, normed = norm_engines(k, st, k.x, tmp, vecs[:, g:g + DT], LN_EPS, vecs[:, b:b + DT])
        with nc.Block() as block:

            @block.vector
            def _(dve):
                n_vec(dve, Chain(dve, dve_step))
                dve.wait_ge(normed, DT)
                dve.tensor_copy(k.x[:], tmp[:])

            @block.scalar
            def _(act):
                n_act(act)

            @block.tensor
            def _(pe):
                n_pe(pe)


def program(nc, a, out):
    with ExitStack() as whole:
        k = Kit(nc, whole)
        stage_load(nc, k, a["x_t"], a["const"])

        with ExitStack() as first:
            def sb(name, shape):
                return first.enter_context(nc.sbuf_tensor(name, shape, F32))

            vecs, proj = sb("vecs1", [P, N_V1]), sb("proj1", [P, N_IN1_TILES, S])
            vtok, y = sb("vtok1", [P, SB, P]), sb("y1", [P, DT, S])
            with nc.Fori(0, DEPTH) as L:
                stage_project1(nc, k, L, a["w_in1"], a["vec1"], vecs, proj, vtok)
                stage_mixers1(nc, k, L, proj, vtok, vecs, a["w_uq"], a["w_ukv"], a["pool_w"], y)
                stage_output1(nc, k, L, vecs, y, a["w_o"])
                stage_ffn1(nc, k, L, vecs, a["w_gu"], a["w_dn"])
            stage_norm(nc, k, "final_norm", a["fin_g"], 0, None, DT, RMS_EPS)

        stage_norm(nc, k, "ln_in", a["ln_in"], 0, DT, 2 * DT, LN_EPS)
        b, m = make_buffers(nc, whole), make_routes(nc, whole)
        experts = a["moe_gate"], a["moe_up"], a["moe_down"]
        with nc.Fori(0, DEPTH) as L:
            stage_project2(nc, k, L, a["w_in2"], a["vec2"], b.vecs, b)
            stage_ssd(nc, k, b.vecs, b, b.y)
            stage_rwkv(nc, k, b.vecs, b, a["lr2"], L, b.y)
            stage_gla(nc, k, b.vecs, b, a["wa2"], L, b.y)
            stage_output2(nc, k, L, b.vecs, b.y, a["w_out"])
            stage_route(nc, k, L, b.vecs, a["w_route"], m)
            stage_experts(nc, k, L, m, *experts, 0, N_EXP, "experts", ALPHA)
            n_over = nc.values_load(m.n_over[0:1, 0:1], min_val=0, max_val=N_OVER)
            with nc.If(n_over > 0):
                stage_experts(nc, k, L, m, *experts, N_EXP, N_OVER, "further", 1.0)
            with nc.Else():
                nc.all_engine_barrier()
            stage_norm2(nc, k, b.vecs)
        stage_store(nc, k, out)


def feat_cols(a):
    return np.swapaxes(a.reshape(*a.shape[:-1], -1, P), -1, -2)


def rows_to_all(a):
    return np.broadcast_to(a[:, None, :], (a.shape[0], P, a.shape[1]))


def tiles_kc(w, cols):
    L, K, _ = w.shape
    parts = [np.transpose(w[:, :, c].reshape(L, K // P, P, len(c)), (0, 2, 1, 3)).reshape(L, P, -1) for c in cols]
    return np.ascontiguousarray(np.concatenate(parts, 2))


def lay_out1(i):
    r = np.arange
    kr = list(r(384, 400)) + list(r(400, 416))
    kr_swapped = list(r(400, 416)) + list(r(384, 400))
    conv, pool, qs = 416, 416 + 768, 416 + 768 + 256
    head = lambda h: list(r(qs + 64 * h, qs + 64 * h + 64))
    cols = [list(r(0, 128)), list(r(128, 256)), list(r(256, 384)), kr + kr_swapped + kr + kr_swapped]
    cols += [list(r(conv + 128 * t, conv + 128 * t + 128)) for t in range(6)]
    cols += [list(r(pool + 128 * t, pool + 128 * t + 128)) for t in range(2)]
    cols += [head(0) + head(2), head(1) + head(3), list(r(qs + 256, qs + 384)), list(r(qs + 384, qs + 512))]
    uq = [96 * h + c for h in range(HEADS) for c in list(r(96)) + list(r(80, 96)) + list(r(64, 80))]
    L = DEPTH
    w_uq = np.transpose(i["w_uq"][:, :, uq].reshape(L, 2, P, 512), (0, 2, 1, 3)).reshape(L, P, -1)
    ukv = [128 * h + c for h in range(HEADS) for c in r(64)] + [128 * h + 64 + c for h in range(HEADS) for c in r(64)]
    pool_w = np.transpose(i["pool_w"].reshape(L, 2, P, 64), (0, 2, 1, 3)).reshape(L, P, -1)
    gate, up = i["w_gate_up"][:, :, :D_FF], i["w_gate_up"][:, :, D_FF:]
    gu = np.stack([gate.reshape(L, DT, P, FT, P), up.reshape(L, DT, P, FT, P)], 0)
    gu = np.transpose(gu, (1, 4, 3, 0, 2, 5)).reshape(L, FT, P, -1)
    down = np.transpose(i["w_down"].reshape(L, FT, P, DT, P), (0, 3, 2, 1, 4)).reshape(L, DT, P, -1)
    vec = [feat_cols(i["attn_norm"]), feat_cols(i["mla_q_norm"]), feat_cols(i["mla_kv_norm"]),
           *[feat_cols(i["conv_w"][:, t]) for t in range(3)], feat_cols(i["pool_scale"]), feat_cols(i["mix_norm"]),
           feat_cols(i["ffn_norm"]), rows_to_all(i["swa_sinks"])]
    c = np.ascontiguousarray
    return {
        "x_t": c(feat_cols(np.transpose(i["x"][0])[None].reshape(D, S).T).transpose(1, 2, 0).reshape(P, DT * S)),
        "w_in1": tiles_kc(i["w_in"], cols),
        "vec1": c(np.concatenate(vec, 2)),
        "w_uq": c(w_uq),
        "w_ukv": c(i["w_ukv"][:, :, ukv]),
        "pool_w": c(pool_w),
        "w_o": tiles_kc(i["w_o"], [list(r(128 * m, 128 * m + 128)) for m in range(DT)]),
        "w_gu": c(gu),
        "w_dn": c(down),
        "fin_g": c(feat_cols(i["final_norm"])),
    }


def lay_out2(i):
    r = lambda a, b: list(range(a, b))
    tiles = [r(P * t, P * t + P) for t in range(10)] + [r(1288 + P * t, 1288 + P * t + P) for t in range(7)]
    tiles += [r(2184, 2312), r(2312, 2440), r(2696, 2824), r(2824, 2952), r(2952, 2968 + P - N_GA), r(1280, 1288) + r(2440, 2696)]
    L = DEPTH
    c = np.ascontiguousarray
    vec = [*[feat_cols(i["ssd_conv_w"][:, t]) for t in range(4)], feat_cols(i["ssd_conv_b"]),
           rows_to_all(i["ssd_dt_bias"]), rows_to_all(i["ssd_a_log"]), feat_cols(np.repeat(i["ssd_d"], 64, 1)),
           feat_cols(i["ssd_norm_g"]), feat_cols(i["rwkv_mu"]), feat_cols(i["rwkv_w0"]), feat_cols(i["rwkv_a0"]),
           feat_cols(i["rwkv_k_k"]), feat_cols(i["rwkv_k_a"]), feat_cols(i["rwkv_r_k"].reshape(L, 256)),
           feat_cols(i["rwkv_ln_g"]), feat_cols(i["rwkv_ln_b"]), feat_cols(i["gla_b_a"]), feat_cols(i["gla_norm_g"]),
           feat_cols(i["ln1_g"]), feat_cols(i["ln1_b"]), feat_cols(i["ln2_g"]), feat_cols(i["ln2_b"]),
           rows_to_all(i["moe_b_rg"]), rows_to_all(i["moe_b_re"])]
    w_in = np.concatenate([i["w_in"], np.zeros((L, D, P - N_GA), np.float32)], 2)
    route = np.concatenate([i["moe_w_rg"], i["moe_w_re"]], 2)
    return {
        "w_in2": tiles_kc(w_in, tiles),
        "vec2": c(np.concatenate(vec, 2)),
        "lr2": c(np.concatenate([i["rwkv_w2"], i["rwkv_a2"], i["rwkv_g2"]], 1)),
        "wa2": c(i["gla_w_a2"]),
        "w_out": tiles_kc(i["w_out"], [r(P * m, P * m + P) for m in range(DT)]),
        "w_route": tiles_kc(route, [r(0, N_ROUTE)]),
        "ln_in": c(np.concatenate([feat_cols(i["ln_in_g"]), feat_cols(i["ln_in_b"])], 1)),
    }


def kernel(**inputs):
    import numpy as _np
    import concourse.bacc as _bacc
    from concourse import mybir as _mybir
    from concourse.bass_utils import run_bass_kernel_spmd as _run

    given = {n: _np.asarray(v) for n, v in inputs.items()}
    second = {n[:-2]: v for n, v in given.items() if n.endswith("_2")}
    arrays = {**lay_out1(given), **lay_out2(second), "const": CONST_ARRAY}
    for n in ("gate", "up", "down"):
        w = second["moe_w_" + n]
        arrays["moe_" + n] = w.reshape((-1,) + w.shape[2:])
    nc = _bacc.Bacc("TRN2", target_bir_lowering=False, num_devices=1)
    aps = {n: nc.dram_tensor(f"in_{n}", v.shape, _mybir.dt.from_np(v.dtype), kind="ExternalInput").ap()
           for n, v in arrays.items()}
    out = nc.dram_tensor("out_t", (P, DT * S), _mybir.dt.float32, kind="ExternalOutput").ap()
    program(nc, aps, out)
    r = _run(nc, [{f"in_{n}": v for n, v in arrays.items()}], core_ids=[0])
    y = r.results[0]["out_t"].reshape(P, DT, S)
    return _np.ascontiguousarray(_np.transpose(y, (2, 1, 0)).reshape(1, S, D))
```

```python
from contextlib import ExitStack

import numpy as np

import concourse.bass as bass
from concourse import mybir

F32 = mybir.dt.float32
F32R = mybir.dt.float32r
BF16 = mybir.dt.bfloat16
ALU = mybir.AluOpType
ACT = mybir.ActivationFunctionType
AX = mybir.AxisListType

P = 128
D = 1024
S = 256
DT = D // P
SB = S // P
DEPTH = 2
RMS_EPS = 1e-6
LN_EPS = 1e-5
NEG = -1.0e30

HEADS = 4
NOPE, ROPE, HD = 64, 32, 64
MLA_SCALE = float(1.0 / np.sqrt(NOPE + ROPE))
SWA_SCALE = float(1.0 / np.sqrt(HD))
SWA_WINDOW = 128
D_FF = 2816
FT = D_FF // P
IN1_WIDTHS = [128] * 16
IN1_OFF = [sum(IN1_WIDTHS[:i]) for i in range(len(IN1_WIDTHS))]
IN1_COLS = sum(IN1_WIDTHS)
T_CQ, T_CKV, T_KR, T_GB, T_GC, T_UC, T_UP, T_QS, T_KS = 0, 2, 3, 4, 6, 8, 10, 12, 14
N_IN1_TILES = 15

V1 = dict(attn_norm=(0, 8), q_norm=(8, 2), kv_norm=(10, 1), conv_w=(11, 6), pool_scale=(17, 2),
          mix_norm=(19, 8), ffn_norm=(27, 8), sinks=(35, 4))
N_V1 = 39

C = 32
NCH = S // C
CPB = P // C
IN2_TILES = 21
N_GA = 16
N_TOKM = 8 + 256
IN2_COLS = (IN2_TILES + 1) * P + N_TOKM
N_GROUPS, EPG, N_EXP, EFF = 4, 8, 32, 512
N_ROUTE = N_GROUPS + N_EXP
SLOTS = 64
N_OVER = 2 * S // SLOTS
N_PASS = N_EXP + N_OVER
I32 = mybir.dt.int32
ALPHA = float((2 * DEPTH) ** 0.25)
V2 = dict(conv_w=(0, 24), conv_b=(24, 6), dt_bias=(30, 8), a_log=(38, 8), ssd_d=(46, 4), ssd_norm=(50, 4),
          mu=(54, 7), w0=(61, 2), a0=(63, 2), k_k=(65, 2), k_a=(67, 2), r_k=(69, 2), ln_g=(71, 2), ln_b=(73, 2),
          b_a=(75, 1), gla_norm=(76, 2), ln1_g=(78, 8), ln1_b=(86, 8),
          b_route=(94, 36))
N_V2 = 130

CONST = {}


def const_pack():
    r, c = np.arange(P)[:, None], np.arange(P)[None, :]
    same = r // C == c // C
    inv = (1.0 / (np.float32(10000.0) ** (np.arange(0, ROPE, 2, dtype=np.float32) / np.float32(ROPE))))
    ang = np.arange(S, dtype=np.float32)[None, :] * inv.astype(np.float32)[:, None]
    cos, sin = np.cos(ang).astype(np.float32), np.sin(ang).astype(np.float32)
    rope = np.zeros((P, S), np.float32)
    rope[64:96] = np.concatenate([cos, cos])
    rope[96:128] = np.concatenate([-sin, sin])
    q, k = np.arange(P)[:, None] + P, np.arange(2 * P)[None, :]
    dist = q - k
    slopes = [2.0 ** (-8.0 * (i + 1) / HEADS) for i in range(HEADS)]
    swa = [np.where((dist >= 0) & (dist < SWA_WINDOW), -s * dist, NEG) for s in slopes]
    mla = np.where(dist >= 0, 0.0, NEG)
    t = np.arange(S) + 1
    invc = np.stack([np.concatenate([np.tile(1.0 / np.minimum(t, w), (64, 1)) for w in ws])
                     for ws in ((2, 4), (8, 16))], 1)
    gla_heads = (np.arange(P)[:, None] // 32 == np.arange(256)[None, :] // 64)
    parts = [("ident", r == c), ("ones", np.ones((P, P))), ("ones64", r // 64 == c // 64),
             ("le3", np.concatenate([r <= c, np.ones((P, P)), r <= c], 1)), ("lt", r < c), ("gt", r > c), ("cu_incl", same & (r <= c)), ("cu_strict", same & (r < c)),
             ("cl_strict", same & (r > c)), ("rope", rope), ("mla", mla), ("swa", np.concatenate(swa, 1)),
             ("invc", invc.reshape(P, 2 * S)), ("keep", np.tile((np.arange(2 * S) % C != 0), (P, 1))),
             ("gla_heads", gla_heads), ("rank", np.tile(64.0 - np.arange(64.0), (P, 1))), ("slots", np.tile(np.arange(P) % SLOTS, (P, 1))),
             ("steps", np.tile(np.repeat(np.arange(N_OVER), N_EXP), (P, 1))),
             ("experts", np.tile(np.arange(N_OVER * N_EXP) % N_EXP, (P, 1)))]
    at = 0
    for name, m in parts:
        CONST[name] = (at, m.shape[1])
        at += m.shape[1]
    return np.ascontiguousarray(np.concatenate([np.asarray(m, np.float32) for _, m in parts], 1))


CONST_ARRAY = const_pack()
N_CONST = CONST_ARRAY.shape[1]


class Chain:

    def __init__(self, eng, sem):
        self.eng, self.sem, self.n = eng, sem, 0

    def link(self, ins):
        self.n += 1
        ins.then_inc(self.sem, 1)
        self.eng.wait_ge(self.sem, self.n)


class Stage:

    def __init__(self, nc, name):
        self.nc, self.name, self.ctx, self.sems = nc, name, ExitStack(), []

    def __enter__(self):
        return self

    def __exit__(self, *a):
        for s in self.sems:
            self.nc.sync.sem_clear(s)
        self.ctx.close()

    def sem(self, name):
        s = self.ctx.enter_context(self.nc.semaphore(f"{self.name}_{name}"))
        self.sems.append(s)
        return s

    def sb(self, name, shape, dt=F32):
        return self.ctx.enter_context(self.nc.sbuf_tensor(f"{self.name}_{name}", shape, dt))

    def ps(self, name, shape, dt=F32):
        return self.ctx.enter_context(self.nc.psum_tensor(f"{self.name}_{name}", shape, dt))


def bc(ap, n, axis):
    ap = ap.unsqueeze(axis)
    return ap.broadcast_to([n if i == axis else d for i, d in enumerate(ap.shape)])


def norm_engines(k, st, x, out, gain, eps, bias=None, tag="n"):
    ln = bias is not None
    sq = st.sb(tag + "_sq", [P, DT, S]) if ln or out is x else out
    lnv = st.sb(tag + "_lnv", [P, S])
    rstd = st.sb(tag + "_rstd", [P, S])
    mean = st.sb(tag + "_mean", [P, S]) if ln else None
    psum = st.ps(tag + "_ps", [P, 2, 512])
    centered = st.sem(tag + "_centered")
    squares = st.sem(tag + "_squares")
    sums = st.sem(tag + "_sums")
    rstd_ready = st.sem(tag + "_rstd_ready")
    ln_done = st.sem(tag + "_ln_done")
    normed = st.sem(tag + "_normed")
    src = out if ln else x
    extra = 1 if ln else 0

    def vector(dve, ch):
        if ln:
            dve.wait_ge(sums, 1)
            ch.link(dve.tensor_scalar(mean[:], psum[:, 0, 0:S], 1.0 / D, None, ALU.mult))
            for t in range(DT):
                dve.tensor_tensor(out[:, t], x[:, t], mean[:], ALU.subtract).then_inc(centered, 1)
            dve.wait_ge(centered, DT)
        dve.wait_ge(rstd_ready, 1)
        for t in range(DT):
            ins = dve.scalar_tensor_tensor(out[:, t], src[:, t], gain[:, t:t + 1], rstd[:], ALU.mult, ALU.mult)
            if ln:
                ch.link(ins)
                ins = dve.tensor_scalar(out[:, t], out[:, t], bias[:, t:t + 1], None, ALU.add)
            ins.then_inc(normed, 1)

    def scalar(act):
        for t in range(DT):
            if ln:
                act.wait_ge(centered, t + 1)
            act.activation(sq[:, t], src[:, t], ACT.Square).then_inc(squares, 1)
        act.wait_ge(sums, 1 + extra)
        act.activation(lnv[:], psum[:, 1, 0:S], ACT.Ln, bias=k.eps[eps], scale=1.0 / D).then_inc(ln_done, 1)
        act.wait_ge(ln_done, 1)
        act.activation(rstd[:], lnv[:], ACT.Exp, scale=-0.5).then_inc(rstd_ready, 1)

    def tensor(pe):
        if ln:
            for t in range(DT):
                ins = pe.matmul(psum[:, 0, 0:S], k.c("ones"), x[:, t], start=t == 0, stop=t == DT - 1)
            ins.then_inc(sums, 1)
        for t in range(DT):
            pe.wait_ge(squares, t + 1)
            ins = pe.matmul(psum[:, 1, 0:S], k.c("ones"), sq[:, t], start=t == 0, stop=t == DT - 1)
        ins.then_inc(sums, 1)

    return vector, scalar, tensor, normed


class Stream:

    def __init__(self, st, tag, sizes, slots, split_slots=2):
        self.sizes, self.slots, self.n2 = sizes, slots, split_slots
        n = max(sizes)
        self.raw = st.sb(tag + "_raw", [P, slots, n])
        self.high = st.sb(tag + "_high", [P, split_slots, n], F32R)
        self.low = st.sb(tag + "_low", [P, split_slots, n], F32R)
        self.loaded = [st.sem(f"{tag}_loaded{i}") for i in range(slots)]
        self.rounded = st.sem(tag + "_rounded")
        self.split = st.sem(tag + "_split")
        self.used = st.sem(tag + "_used")

    def halves(self, i):
        h = self.sizes[i] // 2
        return ((0, h), (h, self.sizes[i]))

    def load(self, sp, i, src):
        if i >= self.slots:
            sp.wait_ge(self.split, 2 * (i - self.slots + 1))
        sp.dma_start(self.raw[:, i % self.slots, 0:self.sizes[i]], src).then_inc(self.loaded[i % self.slots], 16)

    def round(self, act, i):
        act.wait_ge(self.loaded[i % self.slots], 16 * (i // self.slots + 1))
        if i >= self.n2:
            act.wait_ge(self.used, i - self.n2 + 1)
        for a, b in self.halves(i):
            act.activation(self.high[:, i % self.n2, a:b], self.raw[:, i % self.slots, a:b], ACT.Copy)\
                .then_inc(self.rounded, 1)

    def rest(self, dve, i):
        for n, (a, b) in enumerate(self.halves(i)):
            dve.wait_ge(self.rounded, 2 * i + n + 1)
            dve.tensor_tensor(self.low[:, i % self.n2, a:b], self.raw[:, i % self.slots, a:b],
                              self.high[:, i % self.n2, a:b], ALU.subtract).then_inc(self.split, 1)

    def weights(self, i, off, n, width=P):
        return [w[:, i % self.n2, off * width:(off + n) * width].rearrange("p (k c) -> p k c", k=n)
                for w in (self.high, self.low)]

    def ready(self, pe, i):
        pe.wait_ge(self.split, 2 * (i + 1))


def product3(pe, out, stationary, moving, n, split=None):
    (sh, sl), (mh, ml) = stationary, moving
    for kk in range(n):
        if split is not None:
            pe.wait_ge(split, kk + 1)
        pe.matmul(out, sh(kk), mh(kk), start=kk == 0, stop=False)
        pe.matmul(out, sh(kk), ml(kk), start=False, stop=False)
        ins = pe.matmul(out, sl(kk), mh(kk), start=False, stop=kk == n - 1)
    return ins


class Halves:

    def __init__(self, st, tag, n):
        self.high = st.sb(tag + "_high", [P, n, S], F32R)
        self.low = st.sb(tag + "_low", [P, n, S], F32R)
        self.rounded = st.sem(tag + "_rounded")
        self.split = st.sem(tag + "_split")
        self.n = n

    def round(self, act, src, ready=None, step=1):
        for t in range(0, self.n, step):
            if ready is not None:
                act.wait_ge(ready, t + step)
            act.activation(self.high[:, t:t + step], src[:, t:t + step], ACT.Copy).then_inc(self.rounded, step)

    def rest(self, dve, src, step=1):
        for t in range(0, self.n, step):
            dve.wait_ge(self.rounded, t + step)
            dve.tensor_tensor(self.low[:, t:t + step], src[:, t:t + step], self.high[:, t:t + step], ALU.subtract)\
                .then_inc(self.split, step)

    def tiles(self):
        return [lambda kk, w=w: w[:, kk] for w in (self.high, self.low)]

    def block(self, blk):
        return [lambda kk, w=w: w[:, kk, blk * P:(blk + 1) * P] for w in (self.high, self.low)]


def at(pair):
    return [lambda kk, w=w: w[:, kk] for w in pair]


class Kit:

    def __init__(self, nc, ctx):
        self.nc = nc
        self.x = ctx.enter_context(nc.sbuf_tensor("x_resid", [P, DT, S], F32))
        self.const = ctx.enter_context(nc.sbuf_tensor("const", [P, N_CONST], F32))
        self.eps_sb = ctx.enter_context(nc.sbuf_tensor("eps_sb", [P, 5], F32))
        self.eps = {RMS_EPS: self.eps_sb[:, 0:1], LN_EPS: self.eps_sb[:, 1:2], 64e-5: self.eps_sb[:, 2:3],
                    1e-12: self.eps_sb[:, 3:4], 1.0: self.eps_sb[:, 4:5]}

    def c(self, name):
        at, n = CONST[name]
        return self.const[:, at:at + n]


def stage_load(nc, k, x_in, const_in):
    with Stage(nc, "load") as st:
        loaded = st.sem("loaded")
        eps_set = st.sem("eps_set")
        with nc.Block() as block:

            @block.sync
            def _(sp):
                sp.dma_start(k.x[:], x_in.rearrange("p (t s) -> p t s", t=DT)).then_inc(loaded, 16)
                sp.dma_start(k.const[:], const_in).then_inc(loaded, 16)
                sp.wait_ge(loaded, 32)

            @block.vector
            def _(dve):
                for i, e in enumerate((RMS_EPS, LN_EPS, 64e-5, 1e-12, 1.0)):
                    dve.memset(k.eps_sb[:, i:i + 1], e).then_inc(eps_set, 1)
                dve.wait_ge(eps_set, 5)


def stage_project1(nc, k, L, w_dram, v_dram, vecs, proj, vtok):
    with Stage(nc, "project1") as st:
        h = st.sb("h", [P, DT, S])
        hs = Halves(st, "hs", DT)
        unit = 2 * DT * P
        w = Stream(st, "w", [unit] * 8, 4)
        ps = st.ps("ps", [P, 4, 512])
        vec_loaded = st.sem("vec_loaded")
        copied = st.sem("copied")
        dve_step = st.sem("dve_step")
        n_vec, n_act, n_pe, normed = norm_engines(k, st, k.x, h, vecs[:, V1["attn_norm"][0]:], RMS_EPS)

        with nc.Block() as block:

            @block.sync
            def _(sp):
                sp.dma_start(vecs[:], v_dram[bass.ds(L, 1)].rearrange("a p n -> (a p) n")).then_inc(vec_loaded, 16)
                for i in range(8):
                    w.load(sp, i, w_dram[bass.ds(L, 1), :, i * unit:(i + 1) * unit].rearrange("a p n -> (a p) n"))

            @block.vector
            def _(dve):
                dve.wait_ge(vec_loaded, 16)
                n_vec(dve, Chain(dve, dve_step))
                hs.rest(dve, h)
                for i in range(8):
                    w.rest(dve, i)

            @block.scalar
            def _(act):
                n_act(act)
                w.round(act, 0)
                hs.round(act, h, normed)
                w.round(act, 1)
                for i in range(8):
                    act.wait_ge(w.used, i + 1)
                    if i < 7:
                        act.activation(proj[:, 2 * i:2 * i + 2].rearrange("p a s -> p (a s)"), ps[:, i % 4], ACT.Copy)\
                            .then_inc(copied, 1)
                    else:
                        act.activation(proj[:, 14], ps[:, i % 4, 0:S], ACT.Copy)
                        act.activation(vtok[:].rearrange("p b f -> p (b f)"), ps[:, i % 4, S:2 * S], ACT.Copy)\
                            .then_inc(copied, 1)
                    if i + 2 < 8:
                        w.round(act, i + 2)

            @block.tensor
            def _(pe):
                n_pe(pe)
                for i in range(8):
                    w.ready(pe, i)
                    if i >= 4:
                        pe.wait_ge(copied, i - 3)
                    ins = product3(pe, ps[:, i % 4, 0:S], at(w.weights(i, 0, DT)), hs.tiles(), DT,
                                   hs.split if i == 0 else None)
                    if i < 7:
                        ins = product3(pe, ps[:, i % 4, S:2 * S], at(w.weights(i, DT, DT)), hs.tiles(), DT)
                    else:
                        for blk in range(SB):
                            ins = product3(pe, ps[:, i % 4, S + blk * P:S + (blk + 1) * P], hs.block(blk),
                                           at(w.weights(i, DT, DT)), DT)
                    ins.then_inc(w.used, 1)


def stage_mixers1(nc, k, L, proj, vtok, vecs, wuq_dram, wukv_dram, poolw_dram, y):
    with Stage(nc, "mixers1") as st:
        wuq = st.sb("wuq", [P, 2, HEADS, P])
        wukv = st.sb("wukv", [P, 2, 256])
        poolw = st.sb("poolw", [P, 2, 64])
        cn = st.sb("cn", [P, 3, S])
        sq = st.sb("sqc", [P, 3, S])
        lnv = st.sb("lnvc", [P, 2, S])
        rstd = st.sb("rstdc", [P, 2, S])
        qT = st.sb("qT", [P, HEADS, S])
        kT = st.sb("kT", [P, HEADS, S])
        rot = st.sb("rot", [P, HEADS, S])
        vm = st.sb("vm", [P, SB, 256])
        prob = st.sb("prob", [P, 2, HEADS, S])
        probT = st.sb("probT", [P, HEADS * SB, P])
        mx = st.sb("mx", [P, 2, HEADS])
        nmx = st.sb("nmx", [P, 2, HEADS])
        den = st.sb("den", [P, 2, HEADS])
        snk = st.sb("snk", [P, 2, HEADS])
        rden = st.sb("rden", [P, 2, HEADS])
        zc = st.sb("zc", [P, 2, S + 2])
        ct = st.sb("ct", [P, 2, S])
        up = st.sb("up", [P, 2, S + 16])
        s2 = st.sb("s2", [P, 2, S + 16])
        s4 = st.sb("s4", [P, 2, S + 16])
        s8 = st.sb("s8", [P, 2, S + 16])
        s16 = st.sb("s16", [P, 2, S + 16])
        pooled = st.sb("pooled", [P, 2, S])
        psA = st.ps("psA", [P, 4, 512])
        psT = st.ps("psT", [P, 2, 512])
        psY = st.ps("psY", [P, 512])
        psX = st.ps("psX", [P, 512])
        w_loaded = st.sem("w_loaded")
        squares = st.sem("squares")
        sums = st.sem("sums")
        ln_done = st.sem("ln_done")
        rstd_ready = st.sem("rstd_ready")
        latent_ready = st.sem("latent_ready")
        q_done = st.sem("q_done")
        k_done = st.sem("k_done")
        v_done = st.sem("v_done")
        kv_copied = st.sem("kv_copied")
        q_copied = st.sem("q_copied")
        rope_ready = st.sem("rope_ready")
        scores_done = st.sem("scores_done")
        scores_read = st.sem("scores_read")
        max_ready = st.sem("max_ready")
        exp_done = st.sem("exp_done")
        probs_ready = st.sem("probs_ready")
        transposed = st.sem("transposed")
        probT_ready = st.sem("probT_ready")
        attended = st.sem("attended")
        y_copied = st.sem("y_copied")
        pool_ready = st.sem("pool_ready")
        pool_mixed = st.sem("pool_mixed")
        dve_step = st.sem("dve_step")
        gp_step = st.sem("gp_step")
        units = [(1, 0), (1, 1), (0, 0), (0, 1)]
        vec = lambda n, i=0: vecs[:, V1[n][0] + i:V1[n][0] + i + 1]

        with nc.Block() as block:

            @block.sync
            def _(sp):
                sp.dma_start(wuq[:], wuq_dram[bass.ds(L, 1)].rearrange("a p (k h c) -> (a p) k h c", k=2, h=HEADS))\
                    .then_inc(w_loaded, 16)
                sp.dma_start(wukv[:], wukv_dram[bass.ds(L, 1)].rearrange("a p (k c) -> (a p) k c", k=2))\
                    .then_inc(w_loaded, 16)
                sp.dma_start(poolw[:], poolw_dram[bass.ds(L, 1)].rearrange("a p (k c) -> (a p) k c", k=2))\
                    .then_inc(w_loaded, 16)

            @block.gpsimd
            def _(gp):
                ch = Chain(gp, gp_step)
                gp.memset(zc[:, :, 0:2], 0.0)
                gp.memset(up[:, :, 0:16], 0.0)
                gp.memset(s2[:, :, 0:16], 0.0)
                gp.memset(s4[:, :, 0:16], 0.0)
                gp.memset(s8[:, :, 0:16], 0.0)
                ch.link(gp.tensor_tensor(zc[:, :, 2:], proj[:, T_GC:T_GC + 2], proj[:, T_UC:T_UC + 2], ALU.mult))
                ch.link(gp.tensor_copy(up[:, :, 16:], proj[:, T_UP:T_UP + 2]))
                for t in range(2):
                    yt = y[:, 2 + t]
                    ch.link(gp.tensor_scalar(yt, zc[:, t, 0:S], vec("conv_w", t), None, ALU.mult))
                    for tap in (1, 2):
                        ch.link(gp.tensor_scalar(ct[:, t], zc[:, t, tap:tap + S], vec("conv_w", 2 * tap + t), None,
                                                 ALU.mult))
                        ch.link(gp.tensor_tensor(yt, yt, ct[:, t], ALU.add))
                    ch.link(gp.tensor_tensor(yt, yt, proj[:, T_GB + t], ALU.mult))
                for a, b, w in ((up, s2, 1), (s2, s4, 2), (s4, s8, 4), (s8, s16, 8)):
                    ch.link(gp.tensor_tensor(b[:, :, 16:], a[:, :, 16:], a[:, :, 16 - w:S + 16 - w], ALU.add))
                invc = k.c("invc").rearrange("p (t s) -> p t s", t=2)
                for i, s in enumerate((s2, s4, s8, s16)):
                    rows, t = slice(64 * (i % 2), 64 * (i % 2) + 64), i // 2
                    ch.link(gp.tensor_tensor(pooled[rows, t], s[rows, t, 16:], invc[rows, t], ALU.mult))
                gp.tensor_tensor(pooled[:], pooled[:], up[:, :, 16:], ALU.subtract).then_inc(pool_ready, 1)

            @block.vector
            def _(dve):
                ch = Chain(dve, dve_step)
                dve.tensor_tensor(sq[:], proj[:, 0:3], proj[:, 0:3], ALU.mult).then_inc(squares, 1)
                dve.wait_ge(rstd_ready, 1)
                for t in range(3):
                    dve.scalar_tensor_tensor(cn[:, t], proj[:, t], vec("q_norm", t) if t < 2 else vec("kv_norm"),
                                             rstd[:, 0 if t < 2 else 1], ALU.mult, ALU.mult).then_inc(latent_ready, 1)
                cos, sin = k.c("rope")[64:96, :], k.c("rope")[96:128, :]
                dve.wait_ge(q_done, 1)
                psq = psA[:].rearrange("p b (h s) -> p (b h) s", h=2)
                ch.link(dve.tensor_tensor(rot[64:96], psq[96:128, 0:HEADS], bc(sin, HEADS, 1), ALU.mult))
                ch.link(dve.tensor_tensor(qT[64:96], psq[64:96, 0:HEADS], bc(cos, HEADS, 1), ALU.mult))
                dve.tensor_tensor(qT[64:96], qT[64:96], rot[64:96], ALU.add).then_inc(rope_ready, 1)
                dve.wait_ge(rope_ready, 1)
                ch.link(dve.tensor_tensor(rot[64:96, 0], proj[96:128, T_KR], sin, ALU.mult))
                ch.link(dve.tensor_tensor(rot[64:96, 1], proj[64:96, T_KR], cos, ALU.mult))
                dve.tensor_tensor(kT[64:96], bc(rot[64:96, 0], HEADS, 1), bc(rot[64:96, 1], HEADS, 1), ALU.add)\
                    .then_inc(rope_ready, 1)
                dve.wait_ge(pool_mixed, 1)
                for t in range(2):
                    dve.tensor_scalar(y[:, 4 + t], psX[:, t * S:(t + 1) * S], vec("pool_scale", t), None, ALU.mult)

                def soften(u):
                    mla, blk = units[u]
                    n, pr = P * (blk + 1), prob[:, u % 2]
                    if mla:
                        bias = bc(k.c("mla")[:, 2 * P - n:], HEADS, 1)
                    else:
                        bias = k.c("swa").rearrange("p (h c) -> p h c", h=HEADS)[:, :, 2 * P - n:]
                    dve.wait_ge(scores_done, u + 1)
                    sc = psA[:, 2 * (u % 2):2 * (u % 2) + 2].rearrange("p b (h c) -> p (b h) c", h=2)
                    if not mla:
                        pass
                    ins = dve.scalar_tensor_tensor(pr[:, :, 0:n], sc[:, :, 0:n], MLA_SCALE if mla else SWA_SCALE, bias,
                                                   ALU.mult, ALU.add)
                    ins.then_inc(scores_read, 1)
                    dve.wait_ge(scores_read, u + 1)
                    ch.link(dve.reduce_max(mx[:, u % 2], pr[:, :, 0:n], AX.X))
                    if not mla:
                        sinks = vecs[:, V1["sinks"][0]:V1["sinks"][0] + HEADS]
                        ch.link(dve.tensor_tensor(mx[:, u % 2], mx[:, u % 2], sinks, ALU.max))
                        ch.link(dve.tensor_tensor(snk[:, u % 2], sinks, mx[:, u % 2], ALU.subtract))
                    dve.tensor_scalar(nmx[:, u % 2], mx[:, u % 2], -1.0, None, ALU.mult).then_inc(max_ready, 1)

                def normalise(u):
                    mla, blk = units[u]
                    n, pr = P * (blk + 1), prob[:, u % 2]
                    dve.wait_ge(exp_done, u + 1)
                    if not mla:
                        ch.link(dve.tensor_tensor(den[:, u % 2], den[:, u % 2], snk[:, u % 2], ALU.add))
                    ch.link(dve.reciprocal(rden[:, u % 2], den[:, u % 2]))
                    dve.tensor_tensor(pr[:, :, 0:n], pr[:, :, 0:n], bc(rden[:, u % 2], n, 2), ALU.mult)\
                        .then_inc(probs_ready, 1)

                soften(0)
                for u in range(4):
                    if u < 3:
                        if u >= 1:
                            dve.wait_ge(transposed, u)
                        soften(u + 1)
                    normalise(u)

            @block.scalar
            def _(act):
                act.wait_ge(sums, 1)
                act.activation(lnv[:, 0], psX[:, 0:S], ACT.Ln, bias=k.eps[RMS_EPS], scale=1.0 / 256).then_inc(ln_done, 1)
                act.activation(lnv[:, 1], psX[:, S:2 * S], ACT.Ln, bias=k.eps[RMS_EPS], scale=1.0 / 128)\
                    .then_inc(ln_done, 1)
                act.wait_ge(ln_done, 2)
                act.activation(rstd[:], lnv[:], ACT.Exp, scale=-0.5).then_inc(rstd_ready, 1)
                act.wait_ge(q_done, 1)
                act.wait_ge(rope_ready, 1)
                psq = psA[:].rearrange("p b (h s) -> p (b h) s", h=2)
                act.activation(qT[0:64], psq[0:64, 0:HEADS], ACT.Copy).then_inc(q_copied, 1)
                act.wait_ge(k_done, 1)
                act.activation(kT[0:64], psq[0:64, HEADS:], ACT.Copy).then_inc(kv_copied, 1)
                act.wait_ge(v_done, 1)
                act.activation(vm[:].rearrange("p b f -> p (b f)"), psY[:], ACT.Copy).then_inc(kv_copied, 1)

                def exps(u):
                    mla, blk = units[u]
                    n, pr = P * (blk + 1), prob[:, u % 2]
                    act.wait_ge(max_ready, u + 1)
                    for h in range(HEADS):
                        ins = act.activation(pr[:, h, 0:n], pr[:, h, 0:n], ACT.Exp, bias=nmx[:, u % 2, h:h + 1],
                                             accum_out=den[:, u % 2, h:h + 1])
                    if not mla:
                        ins = act.activation(snk[:, u % 2], snk[:, u % 2], ACT.Exp)
                    ins.then_inc(exp_done, 1)

                exps(0)
                for u in range(4):
                    mla, blk = units[u]
                    if u < 3:
                        exps(u + 1)
                    nt = HEADS * (blk + 1)
                    act.wait_ge(transposed, u + 1)
                    act.activation(probT[:, 0:nt].rearrange("p t q -> p (t q)"),
                                   psT[:].rearrange("p b n -> p (b n)")[:, 0:nt * P], ACT.Copy).then_inc(probT_ready, 1)
                    act.wait_ge(attended, u + 1)
                    act.activation(y[:, 0 if mla else 6:2 if mla else 8, blk * P:(blk + 1) * P],
                                   psY[:].rearrange("p (t s) -> p t s", t=2)[:, :, 0:P], ACT.Copy).then_inc(y_copied, 1)

            @block.tensor
            def _(pe):
                pe.wait_ge(squares, 1)
                for t in range(2):
                    pe.matmul(psX[:, 0:S], k.c("ones"), sq[:, t], start=t == 0, stop=t == 1)
                pe.matmul(psX[:, S:2 * S], k.c("ones"), sq[:, 2], start=True, stop=True).then_inc(sums, 1)
                pe.wait_ge(w_loaded, 48)
                pe.wait_ge(latent_ready, 3)
                psq = psA[:].rearrange("p b (h s) -> p (b h) s", h=2)
                for h in range(HEADS):
                    for t in range(2):
                        ins = pe.matmul(psq[:, h], wuq[:, t, h], cn[:, t], start=t == 0, stop=t == 1)
                ins.then_inc(q_done, 1)
                for h in range(HEADS):
                    ins = pe.matmul(psq[0:64, HEADS + h], wukv[:, 0, h * 64:(h + 1) * 64], cn[:, 2], start=True, stop=True)
                ins.then_inc(k_done, 1)
                for blk in range(SB):
                    ins = pe.matmul(psY[:, blk * S:(blk + 1) * S], cn[:, 2, blk * P:(blk + 1) * P], wukv[:, 1],
                                    start=True, stop=True)
                ins.then_inc(v_done, 1)
                pe.wait_ge(ln_done, 2)
                pe.wait_ge(pool_ready, 1)
                for g in range(4):
                    rows, t = slice(64 * (g % 2), 64 * (g % 2) + 64), g // 2
                    ins = pe.matmul(psX[rows, t * S:(t + 1) * S], poolw[rows, t], pooled[rows, t], start=True, stop=True)
                ins.then_inc(pool_mixed, 1)

                def scores(u):
                    mla, blk = units[u]
                    n = P * (blk + 1)
                    qs = slice(blk * P, (blk + 1) * P)
                    sc = psA[:, 2 * (u % 2):2 * (u % 2) + 2].rearrange("p b (h c) -> p (b h) c", h=2)
                    if u >= 2:
                        pe.wait_ge(scores_read, u - 1)
                    for h in range(HEADS):
                        if mla:
                            ins = pe.matmul(sc[:, h, 0:n], qT[0:96, h, qs], kT[0:96, h, 0:n], start=True, stop=True)
                        else:
                            rows = slice(64 * (h // 2), 64 * (h // 2) + 64)
                            ins = pe.matmul(sc[:, h, 0:n], proj[rows, T_QS + h % 2, qs], proj[rows, T_KS, 0:n],
                                            start=True, stop=True)
                    ins.then_inc(scores_done, 1)

                pe.wait_ge(q_copied, 1)
                pe.wait_ge(kv_copied, 2)
                pe.wait_ge(rope_ready, 2)
                scores(0)
                scores(1)
                for u in range(4):
                    mla, blk = units[u]
                    pe.wait_ge(probs_ready, u + 1)
                    if u >= 1:
                        pe.wait_ge(probT_ready, u)
                    for h in range(HEADS):
                        for kb in range(blk + 1):
                            at = (h * (blk + 1) + kb) * P
                            ins = pe.transpose(psT[:, at // 512, at % 512:at % 512 + P],
                                               prob[:, u % 2, h, kb * P:(kb + 1) * P], k.c("ident"))
                    ins.then_inc(transposed, 1)
                    if u < 2:
                        scores(u + 2)
                    pe.wait_ge(probT_ready, u + 1)
                    if u >= 1:
                        pe.wait_ge(y_copied, u)
                    for h in range(HEADS):
                        rows = slice(64 * (h % 2), 64 * (h % 2) + 64)
                        for kb in range(blk + 1):
                            v = vm[:, kb, h * 64:(h + 1) * 64] if mla else vtok[:, kb, (h // 2) * 64:(h // 2) * 64 + 64]
                            ins = pe.matmul(psY[rows, (h // 2) * S:(h // 2) * S + P], v, probT[:, h * (blk + 1) + kb],
                                            start=kb == 0, stop=kb == blk)
                    ins.then_inc(attended, 1)


def stage_output1(nc, k, L, vecs, y, wo_dram):
    with Stage(nc, "output1") as st:
        unit = 2 * DT * P
        w = Stream(st, "w", [unit] * 4, 4)
        sq = st.sb("sq", [P, DT, S])
        lnv = st.sb("lnv", [P, 4, S])
        rstd = st.sb("rstd", [P, 4, S])
        yn = st.sb("yn", [P, DT, S])
        ys = Halves(st, "ys", DT)
        psG = st.ps("psG", [P, 2, 512])
        ps = st.ps("ps", [P, 4, 512])
        squares = st.sem("squares")
        sums = st.sem("sums")
        ln_done = st.sem("ln_done")
        rstd_ready = st.sem("rstd_ready")
        normed = st.sem("normed")
        added = st.sem("added")
        with nc.Block() as block:

            @block.sync
            def _(sp):
                for i in range(4):
                    w.load(sp, i, wo_dram[bass.ds(L, 1), :, i * unit:(i + 1) * unit].rearrange("a p n -> (a p) n"))

            @block.vector
            def _(dve):
                dve.tensor_tensor(sq[:], y[:], y[:], ALU.mult).then_inc(squares, 1)
                w.rest(dve, 0)
                dve.wait_ge(rstd_ready, 1)
                g0 = V1["mix_norm"][0]
                for t in range(DT):
                    dve.scalar_tensor_tensor(yn[:, t], y[:, t], vecs[:, g0 + t:g0 + t + 1], rstd[:, t // 2],
                                             ALU.mult, ALU.mult).then_inc(normed, 1)
                ys.rest(dve, yn)
                w.rest(dve, 1)
                for m in range(4):
                    dve.wait_ge(w.used, m + 1)
                    xm = k.x[:, 2 * m:2 * m + 2].rearrange("p a s -> p (a s)")
                    dve.tensor_tensor(xm, xm, ps[:, m], ALU.add).then_inc(added, 1)
                    if m + 2 < 4:
                        w.rest(dve, m + 2)

            @block.scalar
            def _(act):
                w.round(act, 0)
                act.wait_ge(sums, 1)
                act.activation(lnv[:].rearrange("p g s -> p (g s)"), psG[:].rearrange("p b n -> p (b n)"), ACT.Ln,
                               bias=k.eps[RMS_EPS], scale=1.0 / 256).then_inc(ln_done, 1)
                act.wait_ge(ln_done, 1)
                act.activation(rstd[:], lnv[:], ACT.Exp, scale=-0.5).then_inc(rstd_ready, 1)
                ys.round(act, yn, normed)
                for i in range(1, 4):
                    w.round(act, i)

            @block.tensor
            def _(pe):
                pe.wait_ge(squares, 1)
                for g in range(4):
                    for t in range(2):
                        ins = pe.matmul(psG[:, g // 2, (g % 2) * S:(g % 2 + 1) * S], k.c("ones"), sq[:, 2 * g + t],
                                        start=t == 0, stop=t == 1)
                ins.then_inc(sums, 1)
                for i in range(4):
                    w.ready(pe, i)
                    for m in range(2):
                        ins = product3(pe, ps[:, i, m * S:(m + 1) * S], at(w.weights(i, m * DT, DT)), ys.tiles(), DT,
                                       ys.split if i + m == 0 else None)
                    ins.then_inc(w.used, 1)


def stage_ffn1(nc, k, L, vecs, wgu_dram, wd_dram):
    with Stage(nc, "ffn1") as st:
        h = st.sb("h", [P, DT, S])
        hs = Halves(st, "hs", DT)
        n_units = FT + DT
        w = Stream(st, "w", [2 * DT * P] * FT + [FT * P] * DT, 3)
        acts = Halves(st, "acts", FT)
        sig = st.sb("sig", [P, 2, S])
        ps = st.ps("ps", [P, 4, 512])
        sig_ready = st.sem("sig_ready")
        act_ready = st.sem("act_ready")
        added = st.sem("added")
        dve_step = st.sem("dve_step")
        n_vec, n_act, n_pe, normed = norm_engines(k, st, k.x, h, vecs[:, V1["ffn_norm"][0]:], RMS_EPS)
        with nc.Block() as block:

            @block.sync
            def _(sp):
                for i in range(FT):
                    w.load(sp, i, wgu_dram[bass.ds(L, 1), i].rearrange("a p n -> (a p) n"))
                for m in range(DT):
                    w.load(sp, FT + m, wd_dram[bass.ds(L, 1), m].rearrange("a p n -> (a p) n"))

            @block.vector
            def _(dve):
                ch = Chain(dve, dve_step)
                n_vec(dve, ch)
                hs.rest(dve, h)
                w.rest(dve, 0)
                w.rest(dve, 1)
                for i in range(n_units):
                    if i < FT:
                        dve.wait_ge(sig_ready, i + 1)
                        ch.link(dve.tensor_tensor(sig[:, i % 2], sig[:, i % 2], ps[:, i % 4, 0:S], ALU.mult))
                        dve.tensor_tensor(sig[:, i % 2], sig[:, i % 2], ps[:, i % 4, S:2 * S], ALU.mult)\
                            .then_inc(act_ready, 1)
                        if i + 2 < n_units:
                            w.rest(dve, i + 2)
                        dve.wait_ge(acts.rounded, i + 1)
                        dve.tensor_tensor(acts.low[:, i], sig[:, i % 2], acts.high[:, i], ALU.subtract)\
                            .then_inc(acts.split, 1)
                    else:
                        m = i - FT
                        dve.wait_ge(w.used, i + 1)
                        dve.tensor_tensor(k.x[:, m], k.x[:, m], ps[:, i % 4, 0:S], ALU.add).then_inc(added, 1)
                        if i + 2 < n_units:
                            w.rest(dve, i + 2)

            @block.scalar
            def _(act):
                n_act(act)
                w.round(act, 0)
                hs.round(act, h, normed)
                w.round(act, 1)
                for i in range(n_units):
                    act.wait_ge(w.used, i + 1)
                    if i < FT:
                        if i >= 2:
                            act.wait_ge(acts.split, i - 1)
                        act.activation(sig[:, i % 2], ps[:, i % 4, 0:S], ACT.Sigmoid).then_inc(sig_ready, 1)
                    if i + 2 < n_units:
                        w.round(act, i + 2)
                    if i < FT:
                        act.wait_ge(act_ready, i + 1)
                        act.activation(acts.high[:, i], sig[:, i % 2], ACT.Copy).then_inc(acts.rounded, 1)

            @block.tensor
            def _(pe):
                n_pe(pe)
                for i in range(n_units):
                    w.ready(pe, i)
                    if 4 <= i < FT + 4:
                        pe.wait_ge(act_ready, i - 3)
                    if i < FT:
                        for g in range(2):
                            ins = product3(pe, ps[:, i % 4, g * S:(g + 1) * S], at(w.weights(i, g * DT, DT)), hs.tiles(), DT,
                                           hs.split if i + g == 0 else None)
                    else:
                        if i == FT:
                            pe.wait_ge(acts.split, FT)
                        if i >= FT + 4:
                            pe.wait_ge(added, i - FT - 3)
                        ins = product3(pe, ps[:, i % 4, 0:S], at(w.weights(i, 0, FT)), acts.tiles(), FT)
                    ins.then_inc(w.used, 1)


def stage_norm(nc, k, name, vec_dram, col_g, col_b, n, eps, store=None):
    with Stage(nc, name) as st:
        gv = st.sb("gv", [P, n])
        loaded = st.sem("loaded")
        stored = st.sem("stored")
        dve_step = st.sem("dve_step")
        n_vec, n_act, n_pe, normed = norm_engines(k, st, k.x, k.x, gv[:, col_g:col_g + DT], eps,
                                                  None if col_b is None else gv[:, col_b:col_b + DT])
        with nc.Block() as block:

            @block.sync
            def _(sp):
                sp.dma_start(gv[:], vec_dram).then_inc(loaded, 16)
                if store is not None:
                    half = DT // 2
                    for i in range(2):
                        sp.wait_ge(normed, half * (i + 1))
                        sp.dma_start(store.rearrange("p (t s) -> p t s", t=DT)[:, half * i:half * (i + 1)],
                                     k.x[:, half * i:half * (i + 1)]).then_inc(stored, 16)
                    sp.wait_ge(stored, 32)

            @block.vector
            def _(dve):
                dve.wait_ge(loaded, 16)
                n_vec(dve, Chain(dve, dve_step))

            @block.scalar
            def _(act):
                n_act(act)

            @block.tensor
            def _(pe):
                n_pe(pe)


def stage_store(nc, k, out):
    with Stage(nc, "store") as st:
        stored = st.sem("stored")
        with nc.Block() as block:

            @block.sync
            def _(sp):
                sp.dma_start(out.rearrange("p (t s) -> p t s", t=DT), k.x[:]).then_inc(stored, 16)
                sp.wait_ge(stored, 16)




def stage_project2(nc, k, L, w_dram, v_dram, ln_dram, vecs, b):
    with Stage(nc, "project2") as st:
        xs = Halves(st, "xs", DT)
        pair = 2 * DT * P
        n_pairs = (IN2_TILES + 1) // 2
        n_units = n_pairs + 1
        w = Stream(st, "w", [pair] * n_pairs + [DT * N_TOKM], 4)
        ps = st.ps("ps", [P, 4, 512])
        gb = st.sb("gb", [P, 2 * DT])
        vec_loaded, ln_loaded = st.sem("vec_loaded"), st.sem("ln_loaded")
        copied, dve_step = st.sem("copied"), st.sem("dve_step")
        n_vec, n_act, n_pe, normed = norm_engines(k, st, k.x, k.x, gb[:, 0:DT], LN_EPS, gb[:, DT:2 * DT])
        vec = lambda n, i=0: vecs[:, V2[n][0] + i:V2[n][0] + i + 1]
        dst = [b.z[:, t] for t in range(4)] + [b.xbc[:, t, 3:] for t in range(6)] + \
              [b.rw[:, t, 1:] for t in range(7)] + [b.gl[:, t] for t in range(4)] + [b.ga[:]]

        with nc.Block() as block:

            @block.sync
            def _(sp):
                sp.dma_start(gb[:], ln_dram[bass.ds(L, 1)].rearrange("a p n -> (a p) n")).then_inc(ln_loaded, 16)
                for i in range(n_units):
                    w.load(sp, i, w_dram[bass.ds(L, 1), :, i * pair:i * pair + w.sizes[i]].rearrange("a p n -> (a p) n"))
                    if i == 0:
                        sp.dma_start(vecs[:], v_dram[bass.ds(L, 1)].rearrange("a p n -> (a p) n"))\
                            .then_inc(vec_loaded, 16)
                sp.wait_ge(vec_loaded, 16)

            @block.vector
            def _(dve):
                ch = Chain(dve, dve_step)

                def convolve(cs):
                    for c in cs:
                        ins = dve.tensor_scalar(b.cx[:, c], b.xbc[:, c, 0:S], vec("conv_w", c), vec("conv_b", c),
                                                ALU.mult, ALU.add)
                    for tap in (1, 2, 3):
                        ch.link(ins)
                        for c in cs:
                            ins = dve.scalar_tensor_tensor(b.cx[:, c], b.xbc[:, c, tap:tap + S],
                                                           vec("conv_w", 6 * tap + c), b.cx[:, c], ALU.mult, ALU.add)

                def shift(cs):
                    for c in cs:
                        ins = dve.tensor_tensor(b.shifted[:, c], b.rw[:, c, 0:S], b.rw[:, c, 1:], ALU.subtract)
                    ch.link(ins)
                    for c in cs:
                        dve.scalar_tensor_tensor(b.shifted[:, c], b.shifted[:, c], vec("mu", c), b.rw[:, c, 1:],
                                                 ALU.mult, ALU.add)

                dve.wait_ge(ln_loaded, 16)
                n_vec(dve, ch)
                xs.rest(dve, k.x)
                dve.wait_ge(vec_loaded, 16)
                for i in range(n_units):
                    w.rest(dve, i)
                    if 4 <= i < 11:
                        dve.wait_ge(copied, i - 1)
                    if 4 <= i < 7:
                        convolve((2 * i - 8, 2 * i - 7))
                    elif 7 <= i < 11:
                        shift([c for c in (2 * i - 14, 2 * i - 13) if c < 7])

            @block.scalar
            def _(act):
                n_act(act)
                w.round(act, 0)
                xs.round(act, k.x, normed)
                w.round(act, 1)
                for i in range(n_units):
                    act.wait_ge(w.used, i + 1)
                    if i < n_pairs:
                        for j in range(2):
                            ins = act.activation(dst[2 * i + j], ps[:, i % 2, j * S:(j + 1) * S], ACT.Copy)
                        ins.then_inc(copied, 1)
                    else:
                        act.activation(b.tokm[:], ps[:, 2:4, 0:N_TOKM], ACT.Copy).then_inc(copied, 1)
                    if i + 2 < n_units:
                        w.round(act, i + 2)

            @block.tensor
            def _(pe):
                n_pe(pe)
                for i in range(n_units):
                    w.ready(pe, i)
                    if i < n_pairs:
                        if i >= 2:
                            pe.wait_ge(copied, i - 1)
                        for j in range(2):
                            ins = product3(pe, ps[:, i % 2, j * S:(j + 1) * S], at(w.weights(i, j * DT, DT)),
                                           xs.tiles(), DT, xs.split if i + j == 0 else None)
                    else:
                        for blk in range(SB):
                            ins = product3(pe, ps[:, 2 + blk, 0:N_TOKM], xs.block(blk),
                                           at(w.weights(i, 0, DT, N_TOKM)), DT)
                    ins.then_inc(w.used, 1)


def stage_ssd_gla(nc, k, vecs, b, wa2_dram, L, y):
    with Stage(nc, "ssd_gla") as st:
        cx = b.cx
        sg = st.sb("sg", [P, 6, S])
        dt = st.sb("dt", [P, SB, 8])
        dta = st.sb("dta", [P, SB, 8])
        tmp = st.sb("tmp", [P, SB, 8])
        ea = st.sb("ea", [P, 8])
        G = st.sb("G", [P, SB, 8, P])
        xd = st.sb("xd", [P, SB, 8, 64])
        cb = st.sb("cb", [P, 2, 3 * P])
        E = st.sb("E", [P, 2, 3 * P])
        M = st.sb("M", [P, 2, 3 * P])
        sq = st.sb("sq", [P, 4, S])
        lnv = st.sb("lnv", [P, 2, S])
        rstd = st.sb("rstd", [P, 2, S])
        psA = st.ps("psA", [P, 2, 512])
        psD = st.ps("psD", [P, 2, 512])
        wa2 = st.sb("wa2", [N_GA, P])
        x1 = st.sb("x1", [P, S])
        x2 = st.sb("x2", [P, S])
        cum = st.sb("cum", [P, S])
        qt = st.sb("qt", [P, S])
        kt = st.sb("kt", [P, S])
        el = st.sb("el", [P, S])
        en = st.sb("en", [P, S])
        ktok = st.sb("ktok", [P, SB, P])
        sT = st.sb("sT", [P, HEADS, SB, P])
        EE = st.sb("EE", [P, CPB, SB, 256])
        St = st.sb("St", [P, NCH, 256])
        o = st.sb("o", [P, 2, S])
        g_sg = st.sb("g_sg", [P, 2, S])
        g_sq = st.sb("g_sq", [P, 2, S])
        g_lnv = st.sb("g_lnv", [P, 2, S])
        g_rstd = st.sb("g_rstd", [P, 2, S])
        ps = st.ps("ps", [P, 4, 512])
        (dve_step, act_step, sig_ready, x_ready, z_sig, dt_pre, dt_exp, dt_ready, G_ready, cb_done, cb_masked, xT_done,
         xd_ready, decay_done, E_ready, M_ready, y_done, squares, sums, rstd_ready) = [st.sem(n) for n in (
             "dve_step act_step sig_ready x_ready z_sig dt_pre dt_exp dt_ready G_ready cb_done cb_masked xT_done "
             "xd_ready decay_done E_ready M_ready y_done squares sums rstd_ready").split()]
        (wa_loaded, gate_done, abs_ready, ln_ready, cums_ready, exps_ready, qk_ready, k_done, k_copied, score_done,
         score_masked, e_done, states_ready, o_done, o_copied, g_squares, g_sums, g_rstd_ready,
         g_sig_ready) = [st.sem(n) for n in (
             "wa_loaded gate_done abs_ready ln_ready cums_ready exps_ready qk_ready k_done k_copied score_done "
             "score_masked e_done states_ready o_done o_copied g_squares g_sums g_rstd_ready "
             "g_sig_ready").split()]
        vec = lambda n, i=0: vecs[:, V2[n][0] + i:V2[n][0] + i + 1]
        vecn = lambda n: vecs[:, V2[n][0]:V2[n][0] + V2[n][1]]
        vtok = b.tokm[:, :, 8:8 + 256]
        flat = lambda a: a.rearrange("p a s -> p (a s)")
        psYt = psA[:].rearrange("p b (t s) -> p (b t) s", t=2)
        yh = y[:, 0:4]

        with nc.Block() as block:

            @block.sync
            def _(sp):
                sp.dma_start(wa2[:], wa2_dram[bass.ds(L, 1)].rearrange("a p n -> (a p) n")).then_inc(wa_loaded, 16)

            @block.vector
            def _(dve):
                ch = Chain(dve, dve_step)

                def masked_decay(h):
                    dve.wait_ge(E_ready, h + 1)
                    if h >= 2:
                        dve.wait_ge(y_done, h - 1)
                    dve.tensor_tensor(M[:, h % 2], E[:, h % 2], cb[:, h // 4], ALU.mult).then_inc(M_ready, 1)

                def state(c):
                    return dve.scalar_tensor_tensor(St[:, c + 1], St[:, c], el[:, C * c + C - 1:C * c + C],
                                                    EE[:, c % CPB, c // CPB], ALU.mult, ALU.add)

                ch.link(dve.tensor_tensor(dt[:], b.tokm[:, :, 0:8], bc(vecn("dt_bias"), SB, 1), ALU.add))
                ch.link(dve.tensor_scalar(tmp[:], dt[:], -1.0, None, ALU.mult))
                dve.tensor_tensor(tmp[:], tmp[:], dt[:], ALU.max).then_inc(dt_pre, 1)
                dve.wait_ge(gate_done, 1)
                ch.link(dve.tensor_scalar(x1[:], ps[:, 0, 0:S], vec("b_a"), None, ALU.add))
                ch.link(dve.tensor_scalar(x2[:], x1[:], -1.0, None, ALU.mult))
                dve.tensor_tensor(x2[:], x2[:], x1[:], ALU.max).then_inc(abs_ready, 1)
                dve.wait_ge(sig_ready, 1)
                dve.tensor_tensor(cx[:], cx[:], sg[:], ALU.mult).then_inc(x_ready, 1)
                ch.link(dve.tensor_scalar(x1[:], x1[:], 0.0, None, ALU.min))
                dve.wait_ge(ln_ready, 1)
                ch.link(dve.tensor_tensor(x1[:], x1[:], x2[:], ALU.subtract))
                ch.link(dve.tensor_scalar(x1[:], x1[:], 1.0 / 16, None, ALU.mult))
                dve.tensor_tensor_scan(cum[:], k.c("keep")[:, 0:S], x1[:], 0.0, ALU.mult, ALU.add).then_inc(cums_ready, 1)
                dve.wait_ge(dt_exp, 1)
                ch.link(dve.tensor_scalar(dt[:], dt[:], 0.0, None, ALU.max))
                ch.link(dve.tensor_tensor(dt[:], dt[:], tmp[:], ALU.add))
                ch.link(dve.tensor_tensor(dta[:], dt[:], bc(ea[:], SB, 1), ALU.mult))
                dve.tensor_scalar(dta[:], dta[:], -1.0, None, ALU.mult).then_inc(dt_ready, 1)
                dve.wait_ge(cb_done, 1)
                for g in range(2):
                    ins = dve.tensor_tensor(cb[:, g], psA[:, g, 0:3 * P], k.c("le3"), ALU.mult)
                ins.then_inc(cb_masked, 1)
                dve.wait_ge(exps_ready, 1)
                dve.scalar_tensor_tensor(qt[:], b.gl[:, 0], float(32 ** -0.5), el[:], ALU.mult, ALU.mult)
                dve.tensor_tensor(kt[:], b.gl[:, 1], en[:], ALU.mult).then_inc(qk_ready, 1)
                dve.wait_ge(dt_ready, 1)
                for h in range(8):
                    for blk in range(SB):
                        dve.tensor_scalar(G[:, blk, h], k.c("gt"), dta[:, blk, h:h + 1], None, ALU.mult)\
                            .then_inc(G_ready, 1)
                dve.wait_ge(score_done, 1)
                dve.tensor_tensor(sT[:], ps[:, 0:4, 0:SB * P].rearrange("p h (b c) -> p h b c", b=SB),
                                  bc(bc(k.c("cu_incl"), SB, 1), HEADS, 1), ALU.mult).then_inc(score_masked, 1)
                dve.wait_ge(xT_done, 1)
                for blk in range(SB):
                    dve.tensor_tensor(xd[:, blk], psA[:, blk].rearrange("p (h c) -> p h c", h=8),
                                      bc(dt[:, blk], 64, 2), ALU.mult).then_inc(xd_ready, 1)
                dve.wait_ge(cb_masked, 1)
                masked_decay(0)
                masked_decay(1)
                dve.wait_ge(e_done, 1)
                for c in range(NCH - 1):
                    j, blk = c % CPB, c // CPB
                    dst = St[:, 1] if c == 0 else EE[:, j, blk]
                    ins = dve.scalar_tensor_tensor(dst, ps[:, j, blk * 256:(blk + 1) * 256],
                                                   el[:, C * c + C - 1:C * c + C], k.c("gla_heads"), ALU.mult, ALU.mult)
                ch.link(ins)
                for c in range(1, 4):
                    ch.link(state(c))
                masked_decay(2)
                for c in range(4, NCH - 2):
                    ch.link(state(c))
                state(NCH - 2).then_inc(states_ready, 1)
                masked_decay(3)
                masked_decay(4)
                masked_decay(5)
                dve.wait_ge(o_copied, 1)
                psI = ps[:, 1].rearrange("p (a s) -> p a s", a=2)
                ch.link(dve.tensor_tensor(o[:, :, C:], o[:, :, C:], psI[:, :, C:], ALU.add))
                dve.tensor_tensor(g_sq[:], o[:], o[:], ALU.mult).then_inc(g_squares, 1)
                masked_decay(6)
                masked_decay(7)
                dve.wait_ge(g_sig_ready, 1)
                dve.tensor_tensor(g_sg[:], g_sg[:], b.gl[:, 2:4], ALU.mult)
                dve.wait_ge(z_sig, 1)
                ch.link(dve.tensor_tensor(sg[:, 0:4], sg[:, 0:4], b.z[:], ALU.mult))
                dve.wait_ge(y_done, 8)
                for t in range(4):
                    ins = dve.scalar_tensor_tensor(y[:, t], cx[:, t], vec("ssd_d", t), psYt[:, t], ALU.mult, ALU.add)
                ch.link(ins)
                ch.link(dve.tensor_tensor(yh, yh, sg[:, 0:4], ALU.mult))
                dve.tensor_tensor(sq[:], yh, yh, ALU.mult).then_inc(squares, 1)
                dve.wait_ge(g_rstd_ready, 1)
                for t in range(2):
                    ins = dve.scalar_tensor_tensor(o[:, t], o[:, t], vec("gla_norm", t), g_rstd[:, t], ALU.mult, ALU.mult)
                ch.link(ins)
                dve.tensor_tensor(y[:, 6:8], o[:], g_sg[:], ALU.mult)
                dve.wait_ge(rstd_ready, 1)
                for t in range(4):
                    dve.scalar_tensor_tensor(y[:, t], y[:, t], vec("ssd_norm", t), rstd[:, t // 2], ALU.mult, ALU.mult)

            @block.scalar
            def _(act):
                ch = Chain(act, act_step)

                def decay_exp(h):
                    act.wait_ge(decay_done, h + 1)
                    if h >= 2:
                        act.wait_ge(M_ready, h - 1)
                    act.activation(E[:, h % 2], psD[:, h % 2, 0:3 * P], ACT.Exp).then_inc(E_ready, 1)

                act.activation(sg[:], cx[:], ACT.Sigmoid).then_inc(sig_ready, 1)
                act.activation(g_sg[:], b.gl[:, 2:4], ACT.Sigmoid).then_inc(g_sig_ready, 1)
                act.wait_ge(x_ready, 1)
                act.activation(sg[:, 0:4], b.z[:], ACT.Sigmoid).then_inc(z_sig, 1)
                act.wait_ge(dt_pre, 1)
                act.activation(ea[:], vecn("a_log"), ACT.Exp)
                act.activation(tmp[:], tmp[:], ACT.Exp, scale=-1.0)
                act.wait_ge(abs_ready, 1)
                ch.link(act.activation(x2[:], x2[:], ACT.Exp, scale=-1.0))
                act.activation(x2[:], x2[:], ACT.Ln, bias=k.eps[1.0]).then_inc(ln_ready, 1)
                act.activation(tmp[:], tmp[:], ACT.Ln, bias=k.eps[1.0]).then_inc(dt_exp, 1)
                act.wait_ge(cums_ready, 1)
                act.activation(el[:], cum[:], ACT.Exp)
                act.activation(en[:], cum[:], ACT.Exp, scale=-1.0).then_inc(exps_ready, 1)
                act.wait_ge(k_done, 1)
                act.activation(flat(ktok[:]), psD[:, 0, 0:SB * P], ACT.Copy).then_inc(k_copied, 1)
                for h in range(6):
                    decay_exp(h)
                act.wait_ge(o_done, 1)
                act.activation(flat(o[:]), ps[:, 0], ACT.Copy).then_inc(o_copied, 1)
                decay_exp(6)
                decay_exp(7)
                act.wait_ge(g_sums, 1)
                act.activation(flat(g_lnv[:]), ps[:, 2], ACT.Ln, bias=k.eps[RMS_EPS], scale=1.0 / 64)
                act.wait_ge(sums, 1)
                ch.link(act.activation(flat(lnv[:]), ps[:, 3], ACT.Ln, bias=k.eps[RMS_EPS], scale=1.0 / 256))
                act.activation(rstd[:], lnv[:], ACT.Exp, scale=-0.5).then_inc(rstd_ready, 1)
                act.activation(g_rstd[:], g_lnv[:], ACT.Exp, scale=-0.5).then_inc(g_rstd_ready, 1)

            @block.tensor
            def _(pe):
                def decay(h):
                    pe.wait_ge(G_ready, 2 * h + 2)
                    if h >= 2:
                        pe.wait_ge(E_ready, h - 1)
                    d = psD[:, h % 2]
                    le3 = k.c("le3")
                    pe.matmul(d[:, 0:2 * P], G[:, 0, h], le3[:, 0:2 * P], start=True, stop=False)
                    pe.matmul(d[:, P:2 * P], dta[:, 1, h:h + 1].broadcast_to([P, P]), le3[:, 0:P], start=False, stop=True)
                    pe.matmul(d[:, 2 * P:3 * P], G[:, 1, h], le3[:, 0:P], start=True, stop=True).then_inc(decay_done, 1)

                def head(h):
                    pe.wait_ge(M_ready, h + 1)
                    rows, t = slice(64 * (h % 2), 64 * (h % 2) + 64), h // 2
                    pe.matmul(psYt[rows, t], xd[:, 0, h], M[:, h % 2, 0:S], start=True, stop=False)
                    pe.matmul(psYt[rows, t, P:S], xd[:, 1, h], M[:, h % 2, S:S + P], start=False, stop=True)\
                        .then_inc(y_done, 1)
                    if h + 2 < 8:
                        decay(h + 2)

                pe.wait_ge(wa_loaded, 16)
                pe.matmul(ps[:, 0, 0:S], wa2[:], b.ga[0:N_GA, :], start=True, stop=True).then_inc(gate_done, 1)
                pe.wait_ge(x_ready, 1)
                for g in range(2):
                    rows = slice(64 * g, 64 * g + 64)
                    pe.matmul(psA[:, g, 0:S], cx[rows, 4, 0:P], cx[rows, 5], start=True, stop=True)
                    ins = pe.matmul(psA[:, g, S:S + P], cx[rows, 4, P:S], cx[rows, 5, P:S], start=True, stop=True)
                ins.then_inc(cb_done, 1)
                pe.wait_ge(cb_masked, 1)
                for blk in range(SB):
                    for t in range(4):
                        ins = pe.transpose(psA[:, blk, t * P:(t + 1) * P], cx[:, t, blk * P:(blk + 1) * P], k.c("ident"))
                ins.then_inc(xT_done, 1)
                pe.wait_ge(qk_ready, 1)
                for blk in range(SB):
                    ins = pe.transpose(psD[:, 0, blk * P:(blk + 1) * P], kt[:, blk * P:(blk + 1) * P], k.c("ident"))
                ins.then_inc(k_done, 1)
                for blk in range(SB):
                    cols = slice(blk * P, (blk + 1) * P)
                    for h in range(HEADS):
                        rows = slice(32 * h, 32 * h + 32)
                        ins = pe.matmul(ps[:, h, cols], kt[rows, cols], qt[rows, cols], start=True, stop=True,
                                        tile_position=(32 * h, 0) if h == 3 else None)
                ins.then_inc(score_done, 1)
                pe.wait_ge(k_copied, 1)
                decay(0)
                decay(1)
                pe.wait_ge(score_masked, 1)
                for blk in range(SB):
                    for j in range(CPB):
                        rows = slice(C * j, C * j + C)
                        ins = pe.matmul(ps[:, j, blk * 256:(blk + 1) * 256], ktok[rows, blk], vtok[rows, blk],
                                        start=True, stop=True, tile_position=(32 * j, 0) if j == 3 else None)
                ins.then_inc(e_done, 1)
                pe.wait_ge(xd_ready, 2)
                for h in range(4):
                    head(h)
                pe.wait_ge(states_ready, 1)
                for h in range(HEADS):
                    rows = slice(64 * (h % 2), 64 * (h % 2) + 64)
                    for blk in range(SB):
                        at = (h // 2) * S + blk * P
                        pe.matmul(ps[rows, 0, at:at + P], vtok[:, blk, h * 64:(h + 1) * 64], sT[:, h, blk],
                                  start=True, stop=True)
                for c in range(1, NCH):
                    for pr in range(2):
                        ins = pe.matmul(ps[:, 1, pr * S + C * c:pr * S + C * (c + 1)], St[:, c, pr * P:(pr + 1) * P],
                                        qt[:, C * c:C * (c + 1)], start=True, stop=True)
                ins.then_inc(o_done, 1)
                for h in range(4, 8):
                    head(h)
                pe.wait_ge(g_squares, 1)
                for t in range(2):
                    ins = pe.matmul(ps[:, 2, t * S:(t + 1) * S], k.c("ones64"), g_sq[:, t], start=True, stop=True)
                ins.then_inc(g_sums, 1)
                pe.wait_ge(squares, 1)
                for g in range(2):
                    for t in range(2):
                        ins = pe.matmul(ps[:, 3, g * S:(g + 1) * S], k.c("ones"), sq[:, 2 * g + t],
                                        start=t == 0, stop=t == 1)
                ins.then_inc(sums, 1)


def stage_rwkv(nc, k, vecs, b, lr_dram, L, y):
    with Stage(nc, "rwkv") as st:
        lrw = st.sb("lrw", [P, 256])
        ps_ = b.shifted
        lact = st.sb("lact", [P, S])
        wa = st.sb("wa", [P, 4, S])
        gg = st.sb("gg", [P, 2, S])
        cum = st.sb("cum", [P, 2, S])
        ex = st.sb("ex", [P, 3, 2, S])
        kk = st.sb("kk", [P, 2, S])
        t1 = st.sb("t1", [P, 2, S])
        t2 = st.sb("t2", [P, 2, S])
        F = st.sb("F", [P, 4, 2, S])
        A_, B_, K_, R_ = range(4)
        tok = st.sb("tok", [P, 4, SB, 256])
        U = HEADS * SB
        mN = st.sb("mN", [P, 2, U, P])
        mX = st.sb("mX", [P, U, P])
        mM = st.sb("mM", [P, 3, U, P])
        W = st.sb("W", [P, 3, SB, HEADS, 64])
        QT = st.sb("QT", [P, CPB, SB * 2, P])
        EE = st.sb("EE", [P, CPB, SB * 2, P])
        St = st.sb("St", [P, NCH, 2, P])
        Rp = st.sb("Rp", [P, 2, S])
        yy = st.sb("yy", [P, 2, S])
        lnv = st.sb("lnv", [P, 2, S])
        rstd = st.sb("rstd", [P, 2, S])
        ps = st.ps("ps", [P, 8, 512])
        lr_loaded = st.sem("lr_loaded")
        dve_step, act_step = st.sem("dve_step"), st.sem("act_step")
        (lact_ready, kksq_ready, low_done, logits_ready, kknorm_ready, sig_ready, gate_copied, sums_ready,
         exps_ready, F_ready, masked_done, masked, tok_done, tok_copied, power_done, power_copied, inv_done,
         inv_updated, mv_done, mv_copied, w_done, w_copied, q_done, e_done, q_ready, e_ready, state_done,
         state_ready, rp_done, rp_ready, intra_done, intra_copied, inter_done, yy_ready, bonus_ready, mean_done,
         bonus_done, sq_ready, var_done, rstd_ready) = [st.sem(n) for n in (
             "lact_ready kksq_ready low_done logits_ready kknorm_ready sig_ready gate_copied sums_ready "
             "exps_ready F_ready masked_done masked tok_done tok_copied power_done power_copied inv_done "
             "inv_updated mv_done mv_copied w_done w_copied q_done e_done q_ready e_ready state_done "
             "state_ready rp_done rp_ready intra_done intra_copied inter_done yy_ready bonus_ready mean_done "
             "bonus_done sq_ready var_done rstd_ready").split()]
        vec = lambda n, i=0: vecs[:, V2[n][0] + i:V2[n][0] + i + 1]
        flat = lambda a: a.rearrange("p a s -> p (a s)")
        unit = lambda h, blk: ((h % 2) * SB + blk) * 2 + h // 2
        ones64 = k.c("ones64")
        bank2 = lambda i: ps[:, i:i + 2].rearrange("p b (u n) -> p (b u) n", u=4)
        r_, k_, v_ = ps_[:, 0:2], ps_[:, 2:4], ps_[:, 4:6]

        with nc.Block() as block:

            @block.sync
            def _(sp):
                sp.dma_start(lrw[:], lr_dram[bass.ds(L, 1)].rearrange("a p n -> (a p) n")).then_inc(lr_loaded, 16)

            @block.vector
            def _(dve):
                ch = Chain(dve, dve_step)
                for t in range(2):
                    ins = dve.tensor_scalar(kk[:, t], k_[:, t], vec("k_k", t), None, ALU.mult)
                ch.link(ins)
                dve.tensor_tensor(t1[:], kk[:], kk[:], ALU.mult).then_inc(kksq_ready, 1)
                dve.wait_ge(low_done, 1)
                for t in range(4):
                    ins = dve.tensor_scalar(wa[:, t], ps[:, t // 2, (t % 2) * S:(t % 2 + 1) * S],
                                            vec("w0" if t < 2 else "a0", t % 2), None, ALU.add)
                ins.then_inc(logits_ready, 1)
                dve.wait_ge(kknorm_ready, 1)
                ch.link(dve.tensor_tensor(kk[:], kk[:], rstd[:], ALU.mult))
                dve.wait_ge(sig_ready, 1)
                ch.link(dve.tensor_scalar(wa[:, 0:2], wa[:, 0:2], -float(np.exp(-0.5)), None, ALU.mult))
                ch.link(dve.tensor_tensor_scan(flat(cum[:]), k.c("keep"), flat(wa[:, 0:2]), 0.0, ALU.mult, ALU.add))
                dve.tensor_tensor(t2[:], cum[:], wa[:, 0:2], ALU.subtract).then_inc(sums_ready, 1)
                for t in range(2):
                    ins = dve.tensor_scalar(t1[:, t], wa[:, 2 + t], 1.0, vec("k_a", t), ALU.subtract, ALU.mult)
                ch.link(ins)
                ch.link(dve.scalar_tensor_tensor(k_, t1[:], 1.0, k_, ALU.add, ALU.mult))
                ch.link(dve.tensor_tensor(t1[:], kk[:], wa[:, 2:4], ALU.mult))
                dve.wait_ge(exps_ready, 1)
                dve.scalar_tensor_tensor(F[:, A_], kk[:], -1.0, ex[:, 2], ALU.mult, ALU.mult)
                dve.tensor_tensor(F[:, B_], t1[:], ex[:, 1], ALU.mult)
                dve.tensor_tensor(F[:, K_], k_, ex[:, 1], ALU.mult)
                dve.tensor_tensor(F[:, R_], r_, ex[:, 0], ALU.mult).then_inc(F_ready, 1)
                for i, m in enumerate(("cl_strict", "cu_strict", "cu_strict", "cu_incl", "cu_incl")):
                    dst = mN[:, i] if i < 2 else mM[:, i - 2]
                    dve.wait_ge(masked_done, i + 1)
                    dve.tensor_tensor(dst, bank2(2 * (i % 3)), bc(k.c(m), U, 1), ALU.mult).then_inc(masked, 1)
                    if i == 1:
                        dve.wait_ge(masked, 2)
                        ch.link(dve.tensor_tensor(mX[:], mN[:, 1], bc(k.c("ident"), U, 1), ALU.add))
                for j in range(4):
                    dve.wait_ge(inv_done, j + 1)
                    dve.tensor_tensor(mX[:], mX[:], bank2(4), ALU.add).then_inc(inv_updated, 1)
                    dve.wait_ge(inv_updated, j + 1)
                dve.wait_ge(w_done, 1)
                dve.tensor_copy(W[:, 2].rearrange("p b h c -> p (b h c)"), ps[:, 7]).then_inc(w_copied, 1)
                dve.wait_ge(q_done, 1)
                psQ = ps[:, 0:4].rearrange("p j (n c) -> p (j n) c", n=4)
                qt = QT[:].rearrange("p j n c -> p (j n) c")
                ch.link(dve.tensor_tensor(qt, psQ, bc(ones64, 16, 1), ALU.mult))
                dve.tensor_tensor(qt, qt, bc(k.c("ident"), 16, 1), ALU.add).then_inc(q_ready, 1)
                dve.wait_ge(e_done, 1)
                for c in range(NCH):
                    for pr in range(2):
                        j, n = c % CPB, (c // CPB) * 2 + pr
                        ins = dve.scalar_tensor_tensor(EE[:, j, n], ps[:, 4 + j, n * P:(n + 1) * P],
                                                       ex[:, 0, pr, C * c + C - 1:C * c + C], ones64, ALU.mult, ALU.mult)
                ins.then_inc(e_ready, 1)
                dve.wait_ge(e_ready, 1)
                dve.tensor_copy(St[:, 1], EE[:, 0, 0:2]).then_inc(state_ready, 1)
                dve.wait_ge(rp_done, 1)
                dve.tensor_tensor(flat(Rp[:]), flat(F[:, R_]), ps[:, 2], ALU.add).then_inc(rp_ready, 1)
                for c in range(1, NCH - 1):
                    dve.wait_ge(state_done, c)
                    for pr in range(2):
                        ins = dve.scalar_tensor_tensor(St[:, c + 1, pr], ps[:, pr, (c % 4) * P:(c % 4 + 1) * P],
                                                       ex[:, 0, pr, C * c + C - 1:C * c + C],
                                                       EE[:, c % CPB, (c // CPB) * 2 + pr], ALU.mult, ALU.add)
                    ins.then_inc(state_ready, 1)
                for t in range(2):
                    ins = dve.scalar_tensor_tensor(t1[:, t], r_[:, t], vec("r_k", t), k_[:, t], ALU.mult, ALU.mult)
                ins.then_inc(bonus_ready, 1)
                dve.wait_ge(intra_copied, 1)
                dve.wait_ge(inter_done, 1)
                psI = ps[:, 4].rearrange("p (a s) -> p a s", a=2)
                dve.tensor_tensor(yy[:, :, C:], yy[:, :, C:], psI[:, :, C:], ALU.add).then_inc(yy_ready, 1)
                dve.wait_ge(mean_done, 1)
                ch.link(dve.scalar_tensor_tensor(flat(yy[:]), ps[:, 5], -1.0 / 64, flat(yy[:]), ALU.mult, ALU.add))
                dve.tensor_tensor(t2[:], yy[:], yy[:], ALU.mult).then_inc(sq_ready, 1)
                dve.wait_ge(bonus_done, 1)
                ch.link(dve.tensor_tensor(flat(v_), ps[:, 6], flat(v_), ALU.mult))
                dve.wait_ge(rstd_ready, 1)
                for t in range(2):
                    ins = dve.scalar_tensor_tensor(yy[:, t], yy[:, t], vec("ln_g", t), rstd[:, t], ALU.mult, ALU.mult)
                ch.link(ins)
                for t in range(2):
                    ins = dve.scalar_tensor_tensor(yy[:, t], yy[:, t], vec("ln_b", t), v_[:, t], ALU.add, ALU.add)
                ch.link(ins)
                dve.wait_ge(gate_copied, 1)
                dve.tensor_tensor(y[:, 4:6], yy[:], gg[:], ALU.mult)

            @block.scalar
            def _(act):
                ch = Chain(act, act_step)
                act.activation(lact[0:32, :], ps_[0:32, 6], ACT.Tanh)
                act.activation(lact[32:64, :], ps_[32:64, 6], ACT.Copy)
                act.activation(lact[64:128, :], ps_[64:128, 6], ACT.Sigmoid).then_inc(lact_ready, 1)
                act.wait_ge(low_done, 1)
                act.activation(flat(gg[:]), ps[:, 2], ACT.Copy).then_inc(gate_copied, 1)
                ch.link(act.activation(flat(lnv[:]), ps[:, 3], ACT.Ln, bias=k.eps[1e-12]))
                act.activation(rstd[:], lnv[:], ACT.Exp, scale=-0.5).then_inc(kknorm_ready, 1)
                act.wait_ge(logits_ready, 1)
                act.activation(wa[:], wa[:], ACT.Sigmoid).then_inc(sig_ready, 1)
                act.wait_ge(sums_ready, 1)
                act.activation(ex[:, 0], cum[:], ACT.Exp)
                act.activation(ex[:, 1], cum[:], ACT.Exp, scale=-1.0)
                act.activation(ex[:, 2], t2[:], ACT.Exp).then_inc(exps_ready, 1)
                for i in range(2):
                    act.wait_ge(tok_done, i + 1)
                    act.activation(tok[:, 2 * i].rearrange("p b f -> p (b f)"), ps[:, 6], ACT.Copy)
                    act.activation(tok[:, 2 * i + 1].rearrange("p b f -> p (b f)"), ps[:, 7], ACT.Copy)\
                        .then_inc(tok_copied, 1)
                act.wait_ge(mv_done, 1)
                act.activation(W[:, 0].rearrange("p b h c -> p (b h c)"), ps[:, 6], ACT.Copy).then_inc(mv_copied, 1)
                for j in range(4):
                    act.wait_ge(power_done, j + 1)
                    ins = act.activation(mN[:, 0], bank2(0), ACT.Copy)
                    if j < 3:
                        ins = act.activation(mN[:, 1], bank2(2), ACT.Copy)
                    ins.then_inc(power_copied, 1)
                act.wait_ge(w_done, 1)
                act.activation(W[:, 1].rearrange("p b h c -> p (b h c)"), ps[:, 6], ACT.Copy).then_inc(w_copied, 1)
                act.wait_ge(intra_done, 1)
                act.activation(flat(yy[:]), ps[:, 3], ACT.Copy).then_inc(intra_copied, 1)
                act.wait_ge(var_done, 1)
                ch.link(act.activation(flat(lnv[:]), ps[:, 7], ACT.Ln, bias=k.eps[64e-5], scale=1.0 / 64))
                act.activation(rstd[:], lnv[:], ACT.Exp, scale=-0.5).then_inc(rstd_ready, 1)

            @block.tensor
            def _(pe):
                def heads64(bank, src):
                    for t in range(2):
                        ins = pe.matmul(ps[:, bank, t * S:(t + 1) * S], ones64, src[:, t], start=True, stop=True)
                    return ins

                pe.wait_ge(lr_loaded, 16)
                pe.wait_ge(lact_ready, 1)
                for bank, rows in ((0, slice(0, 32)), (1, slice(32, 64)), (2, slice(64, 128))):
                    for t in range(2):
                        pe.matmul(ps[:, bank, t * S:(t + 1) * S], lrw[rows, t * P:(t + 1) * P], lact[rows, :],
                                  start=True, stop=True)
                pe.wait_ge(kksq_ready, 1)
                heads64(3, t1).then_inc(low_done, 1)
                pe.wait_ge(F_ready, 1)
                pe.wait_ge(gate_copied, 1)

                def transposes(srcs):
                    for bank, src in srcs:
                        for blk in range(SB):
                            for t in range(2):
                                ins = pe.transpose(ps[:, bank, (blk * 2 + t) * P:(blk * 2 + t + 1) * P],
                                                   src[:, t, blk * P:(blk + 1) * P], k.c("ident"))
                    ins.then_inc(tok_done, 1)

                for i, (a, c) in enumerate(((A_, B_), (B_, A_), (K_, A_), (B_, R_), (K_, R_))):
                    if i >= 3:
                        pe.wait_ge(masked, i - 2)
                    for h in range(HEADS):
                        rows = slice(64 * (h % 2), 64 * (h % 2) + 64)
                        for blk in range(SB):
                            cols = slice(blk * P, (blk + 1) * P)
                            ins = pe.matmul(bank2(2 * (i % 3))[:, unit(h, blk)], F[rows, a, h // 2, cols],
                                            F[rows, c, h // 2, cols], start=True, stop=True)
                    ins.then_inc(masked_done, 1)
                    if i == 1:
                        transposes(((6, F[:, A_]), (7, F[:, B_])))
                pe.wait_ge(tok_copied, 1)
                transposes(((6, F[:, K_]), (7, v_)))

                def squares(j):
                    for u in range(U):
                        ins = pe.matmul(bank2(0)[:, u], mN[:, 1, u], mN[:, 0, u], start=True, stop=True)
                    if j < 3:
                        for u in range(U):
                            ins = pe.matmul(bank2(2)[:, u], mN[:, 0, u], mN[:, 1, u], start=True, stop=True)
                    ins.then_inc(power_done, 1)

                pe.wait_ge(masked, 5)
                squares(0)
                pe.wait_ge(tok_copied, 2)
                for blk in range(SB):
                    for h in range(HEADS):
                        ins = pe.matmul(ps[:, 6, (blk * HEADS + h) * 64:(blk * HEADS + h + 1) * 64],
                                        mM[:, 0, unit(h, blk)], tok[:, 3, blk, h * 64:(h + 1) * 64], start=True, stop=True)
                ins.then_inc(mv_done, 1)
                for j in range(4):
                    pe.wait_ge(power_copied, j + 1)
                    if j >= 1:
                        pe.wait_ge(inv_updated, j)
                    for u in range(U):
                        ins = pe.matmul(bank2(4)[:, u], mN[:, 0, u], mX[:, u], start=True, stop=True)
                    ins.then_inc(inv_done, 1)
                    if j < 3:
                        squares(j + 1)
                pe.wait_ge(inv_updated, 4)
                pe.wait_ge(mv_copied, 1)
                for blk in range(SB):
                    for h in range(HEADS):
                        at = (blk * HEADS + h) * 64
                        pe.matmul(ps[:, 6, at:at + 64], mX[:, unit(h, blk)], W[:, 0, blk, h], start=True, stop=True)
                        ins = pe.matmul(ps[:, 7, at:at + 64], mX[:, unit(h, blk)], tok[:, A_, blk, h * 64:(h + 1) * 64],
                                        start=True, stop=True)
                ins.then_inc(w_done, 1)
                pe.wait_ge(w_copied, 2)
                Wp = W[:].rearrange("p w b h c -> p w b (h c)")
                for what, done in ((0, q_done), (1, e_done)):
                    for blk in range(SB):
                        for pr in range(2):
                            cols, n = slice(pr * P, (pr + 1) * P), blk * 2 + pr
                            for j in range(CPB):
                                rows = slice(C * j, C * j + C)
                                if what == 0:
                                    ins = pe.matmul(ps[:, j, n * P:(n + 1) * P], Wp[rows, 2, blk, cols],
                                                    tok[rows, B_, blk, cols], start=True, stop=True)
                                else:
                                    pe.matmul(ps[:, 4 + j, n * P:(n + 1) * P], tok[rows, B_, blk, cols],
                                              Wp[rows, 1, blk, cols], start=True, stop=False)
                                    ins = pe.matmul(ps[:, 4 + j, n * P:(n + 1) * P], tok[rows, K_, blk, cols],
                                                    tok[rows, 3, blk, cols], start=False, stop=True)
                    ins.then_inc(done, 1)
                pe.wait_ge(q_ready, 1)
                for h in range(HEADS):
                    rows = slice(64 * (h % 2), 64 * (h % 2) + 64)
                    for blk in range(SB):
                        at = (h // 2) * S + blk * P
                        ins = pe.matmul(ps[rows, 2, at:at + P], W[:, 2, blk, h], mM[:, 1, unit(h, blk)],
                                        start=True, stop=True)
                ins.then_inc(rp_done, 1)
                for h in range(HEADS):
                    rows = slice(64 * (h % 2), 64 * (h % 2) + 64)
                    for blk in range(SB):
                        at = (h // 2) * S + blk * P
                        pe.matmul(ps[rows, 3, at:at + P], W[:, 1, blk, h], mM[:, 1, unit(h, blk)], start=True, stop=False)
                        ins = pe.matmul(ps[rows, 3, at:at + P], tok[:, 3, blk, h * 64:(h + 1) * 64],
                                        mM[:, 2, unit(h, blk)], start=False, stop=True)
                ins.then_inc(intra_done, 1)
                pe.wait_ge(e_ready, 1)
                pe.wait_ge(rp_ready, 1)
                for c in range(1, NCH):
                    pe.wait_ge(state_ready, c)
                    if c < NCH - 1:
                        for pr in range(2):
                            ins = pe.matmul(ps[:, pr, (c % 4) * P:(c % 4 + 1) * P], QT[:, c % CPB, (c // CPB) * 2 + pr],
                                            St[:, c, pr], start=True, stop=True)
                        ins.then_inc(state_done, 1)
                    for pr in range(2):
                        ins = pe.matmul(ps[:, 4, pr * S + C * c:pr * S + C * (c + 1)], St[:, c, pr],
                                        Rp[:, pr, C * c:C * (c + 1)], start=True, stop=True)
                ins.then_inc(inter_done, 1)
                pe.wait_ge(bonus_ready, 1)
                heads64(6, t1).then_inc(bonus_done, 1)
                pe.wait_ge(yy_ready, 1)
                heads64(5, yy).then_inc(mean_done, 1)
                pe.wait_ge(sq_ready, 1)
                heads64(7, t2).then_inc(var_done, 1)


def stage_output2(nc, k, L, y, w_dram):
    with Stage(nc, "output2") as st:
        unit = 2 * DT * P
        w = Stream(st, "w", [unit] * 4, 4)
        ys = Halves(st, "ys", DT)
        ps = st.ps("ps", [P, 4, 512])
        with nc.Block() as block:

            @block.sync
            def _(sp):
                for i in range(4):
                    w.load(sp, i, w_dram[bass.ds(L, 1), :, i * unit:(i + 1) * unit].rearrange("a p n -> (a p) n"))

            @block.vector
            def _(dve):
                ys.rest(dve, y, 2)
                w.rest(dve, 0)
                w.rest(dve, 1)
                for m in range(4):
                    dve.wait_ge(w.used, m + 1)
                    xm = k.x[:, 2 * m:2 * m + 2].rearrange("p a s -> p (a s)")
                    dve.scalar_tensor_tensor(xm, xm, ALPHA, ps[:, m], ALU.mult, ALU.add)
                    if m + 2 < 4:
                        w.rest(dve, m + 2)

            @block.scalar
            def _(act):
                ys.round(act, y, None, 2)
                for i in range(4):
                    w.round(act, i)

            @block.tensor
            def _(pe):
                for i in range(4):
                    w.ready(pe, i)
                    for m in range(2):
                        ins = product3(pe, ps[:, i, m * S:(m + 1) * S], at(w.weights(i, m * DT, DT)), ys.tiles(), DT,
                                       ys.split if i + m == 0 else None)
                    ins.then_inc(w.used, 1)


class Buffers:
    pass


def make_buffers(nc, ctx):
    b = Buffers()

    def sb(name, shape):
        return ctx.enter_context(nc.sbuf_tensor(name, shape, F32))

    b.vecs = sb("vecs2", [P, N_V2])
    b.y = sb("y2", [P, DT, S])
    b.z = sb("z2", [P, 4, S])
    b.xbc = sb("xbc2", [P, 6, S + 3])
    b.cx = sb("cx2", [P, 6, S])
    b.shifted = sb("shifted2", [P, 7, S])
    b.rw = sb("rw2", [P, 7, S + 1])
    b.gl = sb("gl2", [P, 4, S])
    b.ga = sb("ga2", [P, S])
    b.tokm = sb("tokm2", [P, SB, N_TOKM])
    with Stage(nc, "pads") as st:
        padded = st.sem("padded")
        with nc.Block() as block:

            @block.vector
            def _(dve):
                dve.memset(b.xbc[:, :, 0:3], 0.0).then_inc(padded, 1)
                dve.memset(b.rw[:, :, 0:1], 0.0).then_inc(padded, 1)
                dve.wait_ge(padded, 2)
    return b


class Routes:
    pass


def make_routes(nc, ctx):
    m = Routes()

    def sb(name, shape, dt=F32):
        return ctx.enter_context(nc.sbuf_tensor(name, shape, dt))

    m.parts = sb("parts", [P, 3, SB, D], BF16)
    m.slot = sb("slot", [P, SB, N_PASS])
    m.gate = sb("gate", [P, SB, N_PASS])
    m.over_expert = sb("over_expert", [P, N_OVER], I32)
    m.sums = sb("pass_sums", [P, 2, N_EXP])
    m.n_over = sb("n_over", [P, 1], I32)
    return m


class ExpertWeights(Stage):

    def __init__(self, nc, L, gate, up, down):
        super().__init__(nc, "weights")
        self.L, self.gate, self.up, self.down = L, gate, up, down
        self.gu = self.sb("gu", [P, 2, 2, DT, EFF])
        self.d = self.sb("d", [P, 2, 4, D])
        self.gu_loaded = [self.sem("gu_loaded0"), self.sem("gu_loaded1")]
        self.d_loaded = [self.sem("d_loaded0"), self.sem("d_loaded1")]

    def load_gate_up(self, sp, at, par, loaded):
        for i, w in enumerate((self.gate, self.up)):
            sp.dma_start(self.gu[:, par, i], w[bass.ds(at, 1)].rearrange("a (k p) n -> (a p) k n", p=P))\
                .then_inc(loaded, 16)

    def load_down(self, sp, at, par, loaded):
        sp.dma_start(self.d[:, par], self.down[bass.ds(at, 1)].rearrange("a (t p) n -> (a p) t n", p=P))\
            .then_inc(loaded, 16)


def stage_route(nc, k, L, vecs, w_dram, m, ew):
    with Stage(nc, "route") as st:
        w = st.sb("w", [P, DT, N_ROUTE])
        lg = st.sb("lg", [P, SB, N_ROUTE])
        r1 = st.sb("r1", [P, SB, D])
        one = st.sb("one", [P, 12, SB])
        grp = st.sb("grp", [P, 4, SB, N_GROUPS])
        sel = st.sb("sel", [P, SB, EPG, N_GROUPS])
        e8 = st.sb("e8", [P, 8, SB, EPG])
        A = st.sb("A", [P, SB, N_EXP])
        row = st.sb("row", [P, 5, N_EXP])
        ps = st.ps("ps", [P, 4, 512])
        psl = st.ps("psl", [P, 512])
        psr = st.ps("psr", [P, 512])
        g1, b1 = V2["ln1_g"][0], V2["ln1_b"][0]
        n_vec, n_act, n_pe, normed = norm_engines(k, st, k.x, k.x, vecs[:, g1:g1 + DT], LN_EPS, vecs[:, b1:b1 + DT])
        (w_loaded, dve_step, xT_done, logits_done, hi_ready, mid_ready, rest_ready, gexp_pre, gexp_ready,
         eexp_pre, eexp_ready, assigned, ranked) = [st.sem(n) for n in (
             "w_loaded dve_step xT_done logits_done hi_ready mid_ready rest_ready gexp_pre gexp_ready "
             "eexp_pre eexp_ready assigned ranked").split()]
        b0 = V2["b_route"][0]
        G4, OH, GX, GE = range(4)
        x4 = ps[:].rearrange("p (b q) n -> p b (q n)", b=SB)

        with nc.Block() as block:

            @block.sync
            def _(sp):
                sp.dma_start(w[:], w_dram[bass.ds(L, 1)].rearrange("a p (k c) -> (a p) k c", k=DT)).then_inc(w_loaded, 16)
                for e in range(2):
                    ew.load_gate_up(sp, L * N_EXP + e, e, ew.gu_loaded[e])
                    ew.load_down(sp, L * N_EXP + e, e, ew.d_loaded[e])

            @block.vector
            def _(dve):
                ch = Chain(dve, dve_step)
                link = ch.link

                def one_hot(dst, key, x, mx, n):
                    link(dve.tensor_tensor(key, x, bc(mx, n, 2), ALU.is_equal))
                    link(dve.tensor_tensor(key, key, bc(k.c("rank")[:, 0:n], SB, 1), ALU.mult))
                    link(dve.reduce_max(one[:, 11], key, AX.X))
                    link(dve.tensor_tensor(dst, key, bc(one[:, 11], n, 2), ALU.is_equal))

                n_vec(dve, ch)
                for blk in range(SB):
                    dve.wait_ge(hi_ready, blk + 1)
                    dve.tensor_tensor(r1[:, blk], x4[:, blk], m.parts[:, 0, blk], ALU.subtract).then_inc(rest_ready, 1)
                dve.wait_ge(logits_done, 1)
                link(dve.tensor_tensor(lg[:], psl[:, 0:SB * N_ROUTE].rearrange("p (b c) -> p b c", b=SB),
                                       bc(vecs[:, b0:b0 + N_ROUTE], SB, 1), ALU.add))
                gl = lg[:, :, 0:N_GROUPS]
                link(dve.reduce_max(one[:, 0], gl, AX.X))
                one_hot(grp[:, OH], grp[:, G4], gl, one[:, 0], N_GROUPS)
                dve.tensor_tensor(grp[:, GX], gl, bc(one[:, 0], N_GROUPS, 2), ALU.subtract).then_inc(gexp_pre, 1)
                link(dve.tensor_tensor(sel[:].rearrange("p b e g -> p b g e"),
                                       lg[:, :, N_GROUPS:].rearrange("p b (g e) -> p b g e", g=N_GROUPS),
                                       bc(grp[:, OH], EPG, 3), ALU.mult))
                link(dve.tensor_reduce(e8[:, 0], sel[:], AX.X, ALU.add))
                link(dve.reduce_max(one[:, 1], e8[:, 0], AX.X))
                one_hot(e8[:, 1], e8[:, 3], e8[:, 0], one[:, 1], EPG)
                link(dve.scalar_tensor_tensor(e8[:, 4], e8[:, 1], NEG, e8[:, 0], ALU.mult, ALU.add))
                link(dve.reduce_max(one[:, 2], e8[:, 4], AX.X))
                one_hot(e8[:, 2], e8[:, 3], e8[:, 4], one[:, 2], EPG)
                dve.tensor_tensor(one[:, 3], one[:, 2], one[:, 1], ALU.subtract).then_inc(eexp_pre, 1)
                dve.wait_ge(gexp_ready, 1)
                link(dve.tensor_reduce(one[:, 4], grp[:, GE], AX.X, ALU.add))
                link(dve.reciprocal(one[:, 5], one[:, 4]))
                dve.wait_ge(eexp_ready, 1)
                link(dve.tensor_scalar(one[:, 7], one[:, 6], 1.0, None, ALU.add))
                link(dve.reciprocal(one[:, 8], one[:, 7]))
                link(dve.tensor_tensor(one[:, 9], one[:, 8], one[:, 5], ALU.mult))
                link(dve.tensor_tensor(one[:, 10], one[:, 9], one[:, 6], ALU.mult))
                link(dve.tensor_tensor(e8[:, 5], e8[:, 1], e8[:, 2], ALU.add))
                link(dve.tensor_tensor(e8[:, 6], e8[:, 1], bc(one[:, 9], EPG, 2), ALU.mult))
                link(dve.tensor_tensor(e8[:, 7], e8[:, 2], bc(one[:, 10], EPG, 2), ALU.mult))
                link(dve.tensor_tensor(e8[:, 6], e8[:, 6], e8[:, 7], ALU.add))
                for blk in range(SB):
                    grid = lambda a: a[:, blk].rearrange("p (g e) -> p g e", g=N_GROUPS)
                    ins = dve.tensor_tensor(grid(A), bc(e8[:, 5, blk], N_GROUPS, 1), bc(grp[:, OH, blk], EPG, 2), ALU.mult)
                    link(dve.tensor_tensor(m.gate[:, blk, 0:N_EXP].rearrange("p (g e) -> p g e", g=N_GROUPS),
                                           bc(e8[:, 6, blk], N_GROUPS, 1), bc(grp[:, OH, blk], EPG, 2), ALU.mult))
                dve.tensor_copy(row[:, 0], A[:, 1]).then_inc(assigned, 1)
                dve.wait_ge(mid_ready, 1)
                dve.tensor_tensor(r1[:], r1[:], m.parts[:, 1], ALU.subtract).then_inc(rest_ready, 1)
                dve.wait_ge(ranked, 1)
                rank = psr[:, 0:SB * N_EXP].rearrange("p (b e) -> p b e", b=SB)
                slot = m.slot[:, :, 0:N_EXP]
                link(dve.scalar_tensor_tensor(slot, rank, 1.0, A[:], ALU.add, ALU.mult))
                link(dve.tensor_scalar(slot, slot, -1.0, None, ALU.add))
                cnt = psr[:, SB * N_EXP:(SB + 1) * N_EXP]
                link(dve.tensor_scalar(row[:, 1], cnt, float(SLOTS), None, ALU.is_gt))
                for n in (2, 3):
                    link(dve.tensor_scalar(row[:, 2], cnt, float(n * SLOTS), None, ALU.is_gt))
                    link(dve.tensor_tensor(row[:, 1], row[:, 1], row[:, 2], ALU.add))
                link(dve.tensor_tensor_scan(m.sums[:, 0], k.c("ones")[:, 0:N_EXP], row[:, 1], 0.0, ALU.mult, ALU.add))
                dve.tensor_tensor(m.sums[:, 1], m.sums[:, 0], row[:, 1], ALU.subtract)
                dve.tensor_copy(m.n_over[:], m.sums[:, 0, N_EXP - 1:N_EXP])

            @block.scalar
            def _(act):
                n_act(act)
                for blk in range(SB):
                    act.wait_ge(xT_done, blk + 1)
                    act.activation(m.parts[:, 0, blk], x4[:, blk], ACT.Copy).then_inc(hi_ready, 1)
                act.wait_ge(rest_ready, SB)
                act.activation(m.parts[:, 1], r1[:], ACT.Copy).then_inc(mid_ready, 1)
                act.wait_ge(gexp_pre, 1)
                act.activation(grp[:, GE], grp[:, GX], ACT.Exp).then_inc(gexp_ready, 1)
                act.wait_ge(eexp_pre, 1)
                act.activation(one[:, 6], one[:, 3], ACT.Exp).then_inc(eexp_ready, 1)
                act.wait_ge(rest_ready, SB + 1)
                act.activation(m.parts[:, 2], r1[:], ACT.Copy)

            @block.tensor
            def _(pe):
                n_pe(pe)
                for blk in range(SB):
                    for t in range(DT):
                        if blk == 0:
                            pe.wait_ge(normed, t + 1)
                        at = blk * D + t * P
                        ins = pe.transpose(ps[:, at // 512, at % 512:at % 512 + P], k.x[:, t, blk * P:(blk + 1) * P],
                                           k.c("ident"))
                    ins.then_inc(xT_done, 1)
                pe.wait_ge(w_loaded, 16)
                for blk in range(SB):
                    for kk in range(DT):
                        ins = pe.matmul(psl[:, blk * N_ROUTE:(blk + 1) * N_ROUTE], k.x[:, kk, blk * P:(blk + 1) * P],
                                        w[:, kk], start=kk == 0, stop=kk == DT - 1)
                ins.then_inc(logits_done, 1)
                pe.wait_ge(assigned, 1)
                pe.matmul(psr[:, 0:N_EXP], k.c("lt"), A[:, 0], start=True, stop=True)
                pe.matmul(psr[:, N_EXP:2 * N_EXP], k.c("lt"), A[:, 1], start=True, stop=False)
                pe.matmul(psr[:, N_EXP:2 * N_EXP], k.c("ones"), A[:, 0], start=False, stop=True)
                pe.matmul(psr[:, 2 * N_EXP:3 * N_EXP], k.c("ones"), A[:, 0], start=True, stop=False)
                pe.matmul(psr[:, 2 * N_EXP:3 * N_EXP], k.c("ones"), A[:, 1], start=False, stop=True).then_inc(ranked, 1)


def stage_plan(nc, k, m):
    with Stage(nc, "plan") as st:
        big = st.sb("big", [P, 3, N_OVER, N_EXP])
        bigt = st.sb("bigt", [P, SB, N_OVER, N_EXP])
        onef = st.sb("onef", [P, 3, N_OVER])
        dve_step = st.sem("dve_step")
        with nc.Block() as block:

            @block.vector
            def _(dve):
                link = Chain(dve, dve_step).link
                grid = lambda n: k.c(n).rearrange("p (s e) -> p s e", s=N_OVER)
                link(dve.tensor_tensor(big[:, 0], bc(m.sums[:, 0], N_OVER, 1), grid("steps"), ALU.is_gt))
                link(dve.tensor_tensor(big[:, 1], bc(m.sums[:, 1], N_OVER, 1), grid("steps"), ALU.is_le))
                link(dve.tensor_tensor(big[:, 0], big[:, 0], big[:, 1], ALU.mult))
                link(dve.tensor_tensor(big[:, 1], big[:, 0], grid("experts"), ALU.mult))
                link(dve.tensor_reduce(onef[:, 0], big[:, 1], AX.X, ALU.add))
                link(dve.tensor_copy(m.over_expert[:], onef[:, 0]))
                link(dve.tensor_tensor(big[:, 2], grid("steps"), bc(m.sums[:, 1], N_OVER, 1), ALU.subtract))
                link(dve.scalar_tensor_tensor(big[:, 2], big[:, 2], 1.0, big[:, 0], ALU.add, ALU.mult))
                link(dve.tensor_reduce(onef[:, 1], big[:, 2], AX.X, ALU.add))
                link(dve.tensor_scalar(onef[:, 2], onef[:, 1], float(SLOTS), 1.0, ALU.mult, ALU.add))
                for blk in range(SB):
                    link(dve.scalar_tensor_tensor(bigt[:, blk], bc(m.slot[:, blk, 0:N_EXP], N_OVER, 1), 1.0, big[:, 0],
                                                  ALU.add, ALU.mult))
                    link(dve.tensor_reduce(m.slot[:, blk, N_EXP:], bigt[:, blk], AX.X, ALU.add))
                    link(dve.tensor_tensor(m.slot[:, blk, N_EXP:], m.slot[:, blk, N_EXP:], onef[:, 2], ALU.subtract))
                    link(dve.tensor_tensor(bigt[:, blk], bc(m.gate[:, blk, 0:N_EXP], N_OVER, 1), big[:, 0], ALU.mult))
                    link(dve.tensor_reduce(m.gate[:, blk, N_EXP:], bigt[:, blk], AX.X, ALU.add))


def stage_experts(nc, k, L, m, ew, first, n, name, base_scale):
    with Stage(nc, name) as st:
        main = first == 0
        wgu, wd = ew.gu, ew.d
        selg = st.sb("selg", [P, 2, SB, P])
        selb = st.sb("selb", [P, 2, SB, SLOTS], BF16)
        selT = st.sb("selT", [P, 2, S])
        xc = st.sb("xc", [P, DT, SLOTS])
        sig = st.sb("sig", [P, S])
        hh = st.sb("hh", [P, S])
        hT = st.sb("hT", [P, 2, P])
        yc = st.sb("yc", [P, 512])
        zero = st.sb("zero", [P, 512], BF16)
        psG = st.ps("psG", [P, 512])
        psX = st.ps("psX", [P, 512])
        psS = st.ps("psS", [P, 512])
        psD = st.ps("psD", [P, 512])
        psY = st.ps("psY", [P, 4, 512])
        if main:
            gu_loaded, d_loaded = ew.gu_loaded, ew.d_loaded
        else:
            gu_loaded = [st.sem("gu_loaded0"), st.sem("gu_loaded1")]
            d_loaded = [st.sem("d_loaded0"), st.sem("d_loaded1")]
        (dve_step, zero_ready, sel_ready, gathered, xc_ready, gu_done, sig_ready, h_ready, selT_done, selT_ready,
         hT_done, hT_ready, down_done, yc_ready, scattered, y_done) = [st.sem(s) for s in (
             "dve_step zero_ready sel_ready gathered xc_ready gu_done sig_ready h_ready selT_done selT_ready "
             "hT_done hT_ready down_done yc_ready scattered y_done").split()]

        def passes(eng, body):
            body(0, 0, True, False)
            body(1, 1, False, False)
            with eng.Fori(1, n // 2 - 1) as it:
                body(2 * it, 0, False, False)
                body(2 * it + 1, 1, False, False)
            body(n - 2, 0, False, False)
            body(n - 1, 1, False, True)

        with nc.Block() as block:

            @block.sync
            def _(sp):
                def load(e, par, is_first, is_last):
                    early = isinstance(e, int) and e < 2
                    if early and main:
                        return
                    if main:
                        at = L * N_EXP + e
                    else:
                        at = L * N_EXP + sp.value_load(m.over_expert[0:1, bass.ds(e, 1)], min_val=0, max_val=N_EXP - 1)
                    if not early:
                        sp.wait_ge(gu_done, e - 1)
                    ew.load_gate_up(sp, at, par, gu_loaded[par])
                    if not early:
                        sp.wait_ge(down_done, e - 1)
                    ew.load_down(sp, at, par, d_loaded[par])

                passes(sp, load)

            @block.vector
            def _(dve):
                ch = Chain(dve, dve_step)

                def select(e, par):
                    if not (isinstance(e, int) and e < 2):
                        dve.wait_ge(selT_done, e - 1)
                    for blk in range(SB):
                        col = m.slot[:, blk, bass.ds(first + e, 1)]
                        dve.tensor_scalar(selb[:, par, blk], k.c("slots")[:, 0:SLOTS], col, None, ALU.is_equal)
                        ins = dve.tensor_scalar(selg[:, par, blk], k.c("slots"), col, m.gate[:, blk, bass.ds(first + e, 1)],
                                                ALU.is_equal, ALU.mult)
                    ins.then_inc(sel_ready, 1)

                def step(e, par, is_first, is_last):
                    if not is_last:
                        select(e + 1, 1 - par)
                    dve.wait_ge(sig_ready, e + 1)
                    dve.tensor_tensor(sig[:], sig[:], psG[:, 0:S], ALU.mult).then_inc(dve_step, 1)
                    dve.wait_ge(dve_step, e + 1)
                    dve.tensor_tensor(hh[:], sig[:], psG[:, S:2 * S], ALU.mult).then_inc(h_ready, 1)

                dve.memset(zero[:], 0.0).then_inc(zero_ready, 1)
                select(0, 0)
                passes(dve, step)
                dve.wait_ge(y_done, 1)
                xf = k.x[:].rearrange("p (b t) s -> p b (t s)", b=4)
                dve.scalar_tensor_tensor(xf, xf, base_scale, psY[:], ALU.mult, ALU.add)

            @block.scalar
            def _(act):
                def take(e):
                    act.wait_ge(gathered, e + 1)
                    act.activation(xc[:].rearrange("p t c -> p (t c)"), psX[:], ACT.Copy).then_inc(xc_ready, 1)

                def step(e, par, is_first, is_last):
                    act.wait_ge(gu_done, e + 1)
                    if not is_first:
                        act.wait_ge(h_ready, e)
                    act.activation(sig[:], psG[:, 0:S], ACT.Sigmoid).then_inc(sig_ready, 1)
                    act.wait_ge(selT_done, e + 1)
                    if not (isinstance(e, int) and e < 2):
                        act.wait_ge(scattered, e - 1)
                    act.activation(selT[:, par], psS[:, 0:S], ACT.Copy).then_inc(selT_ready, 1)
                    if not is_last:
                        take(e + 1)
                    act.wait_ge(hT_done, e + 1)
                    act.activation(hT[:].rearrange("p c n -> p (c n)"), psS[:, S:2 * S], ACT.Copy).then_inc(hT_ready, 1)
                    act.wait_ge(down_done, e + 1)
                    act.activation(yc[:], psD[:], ACT.Copy).then_inc(yc_ready, 1)

                take(0)
                passes(act, step)

            @block.tensor
            def _(pe):
                def gather(e, par):
                    pe.wait_ge(sel_ready, e + 1)
                    for t in range(DT):
                        for i in range(3):
                            for blk in range(SB):
                                ins = pe.matmul(psX[:, t * SLOTS:(t + 1) * SLOTS], m.parts[:, i, blk, t * P:(t + 1) * P],
                                                selb[:, par, blk], start=i == 0 and blk == 0, stop=i == 2 and blk == SB - 1)
                    ins.then_inc(gathered, 1)

                def scatter(par, e):
                    pe.wait_ge(yc_ready, e + 1)
                    for t in range(4):
                        for i in range(2):
                            rows = slice(SLOTS * i, SLOTS * i + SLOTS)
                            ins = pe.matmul(psY[:, 2 * i + t // 2, (t % 2) * S:(t % 2 + 1) * S],
                                            yc[rows, t * P:(t + 1) * P], selT[rows, par], start=False, stop=False)
                    ins.then_inc(scattered, 1)

                def step(e, par, is_first, is_last):
                    pe.wait_ge(gu_loaded[par], (e + (2 - par)) * 16)
                    pe.wait_ge(xc_ready, e + 1)
                    if not is_first:
                        pe.wait_ge(h_ready, e)
                    for kk in range(DT):
                        for j in range(2):
                            out = psG[SLOTS * j:SLOTS * (j + 1), :].rearrange("p (g c) -> p g c", g=2)
                            ins = pe.matmul(out, xc[:, kk], wgu[:, par, :, kk, j * S:(j + 1) * S],
                                            start=kk == 0, stop=kk == DT - 1)
                    ins.then_inc(gu_done, 1)
                    if not is_first:
                        pe.wait_ge(hT_ready, e)
                    for blk in range(SB):
                        ins = pe.transpose(psS[:, blk * P:(blk + 1) * P], selg[:, par, blk], k.c("ident"))
                    ins.then_inc(selT_done, 1)
                    if not is_last:
                        gather(e + 1, 1 - par)
                    pe.wait_ge(h_ready, e + 1)
                    pe.wait_ge(selT_ready, e + 1)
                    for c in range(2):
                        ins = pe.transpose(psS[:, S + c * P:S + (c + 1) * P], hh[:, c * P:(c + 1) * P], k.c("ident"))
                    ins.then_inc(hT_done, 1)
                    if not is_first:
                        scatter(1 - par, e - 1)
                    pe.wait_ge(d_loaded[par], half_count(e, par))
                    pe.wait_ge(hT_ready, e + 1)
                    for j in range(2):
                        for c in range(2):
                            for i in range(2):
                                rows = slice(SLOTS * i, SLOTS * i + SLOTS)
                                ins = pe.matmul(psD[rows, :], hT[:, c, j * SLOTS:(j + 1) * SLOTS],
                                                wd[:, par, 2 * j + c, i * 512:(i + 1) * 512],
                                                start=j == 0 and c == 0, stop=j == 1 and c == 1)
                    ins.then_inc(down_done, 1)

                def half_count(e, par):
                    return (e + (2 - par)) * 8

                gather(0, 0)
                pe.wait_ge(zero_ready, 1)
                for i in range(4):
                    pe.matmul(psY[:, i], zero[:, 0:P], zero[:], start=True, stop=False)
                passes(pe, step)
                scatter((n - 1) % 2, n - 1)
                for i in range(4):
                    ins = pe.matmul(psY[:, i], zero[:, 0:P], zero[:], start=False, stop=True)
                ins.then_inc(y_done, 1)




def program(nc, a, out):
    with ExitStack() as whole:
        k = Kit(nc, whole)
        stage_load(nc, k, a["x_t"], a["const"])

        with ExitStack() as first:
            def sb(name, shape):
                return first.enter_context(nc.sbuf_tensor(name, shape, F32))

            vecs, proj = sb("vecs1", [P, N_V1]), sb("proj1", [P, N_IN1_TILES, S])
            vtok, y = sb("vtok1", [P, SB, P]), sb("y1", [P, DT, S])
            with nc.Fori(0, DEPTH) as L:
                stage_project1(nc, k, L, a["w_in1"], a["vec1"], vecs, proj, vtok)
                stage_mixers1(nc, k, L, proj, vtok, vecs, a["w_uq"], a["w_ukv"], a["pool_w"], y)
                stage_output1(nc, k, L, vecs, y, a["w_o"])
                stage_ffn1(nc, k, L, vecs, a["w_gu"], a["w_dn"])
            stage_norm(nc, k, "final_norm", a["fin_g"], 0, None, DT, RMS_EPS)

        b, m = make_buffers(nc, whole), make_routes(nc, whole)
        with nc.Fori(0, DEPTH) as L:
            stage_project2(nc, k, L, a["w_in2"], a["vec2"], a["ln2"], b.vecs, b)
            stage_ssd_gla(nc, k, b.vecs, b, a["wa2"], L, b.y)
            stage_rwkv(nc, k, b.vecs, b, a["lr2"], L, b.y)
            stage_output2(nc, k, L, b.y, a["w_out"])
            with ExpertWeights(nc, L, a["moe_gate"], a["moe_up"], a["moe_down"]) as ew:
                stage_route(nc, k, L, b.vecs, a["w_route"], m, ew)
                stage_experts(nc, k, L, m, ew, 0, N_EXP, "experts", ALPHA)
                n_over = nc.values_load(m.n_over[0:1, 0:1], min_val=0, max_val=N_OVER)
                with nc.If(n_over > 0):
                    stage_plan(nc, k, m)
                    stage_experts(nc, k, L, m, ew, N_EXP, N_OVER, "further", 1.0)
                with nc.Else():
                    nc.all_engine_barrier()
        stage_norm(nc, k, "last_norm", a["ln2"][DEPTH], 0, DT, 2 * DT, LN_EPS, out)


def feat_cols(a):
    return np.swapaxes(a.reshape(*a.shape[:-1], -1, P), -1, -2)


def rows_to_all(a):
    return np.broadcast_to(a[:, None, :], (a.shape[0], P, a.shape[1]))


def tiles_kc(w, cols):
    L, K, _ = w.shape
    parts = [np.transpose(w[:, :, c].reshape(L, K // P, P, len(c)), (0, 2, 1, 3)).reshape(L, P, -1) for c in cols]
    return np.ascontiguousarray(np.concatenate(parts, 2))


def lay_out1(i):
    r = np.arange
    kr = list(r(384, 400)) + list(r(400, 416))
    kr_swapped = list(r(400, 416)) + list(r(384, 400))
    conv, pool, qs = 416, 416 + 768, 416 + 768 + 256
    head = lambda h: list(r(qs + 64 * h, qs + 64 * h + 64))
    cols = [list(r(0, 128)), list(r(128, 256)), list(r(256, 384)), kr + kr_swapped + kr + kr_swapped]
    cols += [list(r(conv + 128 * t, conv + 128 * t + 128)) for t in range(6)]
    cols += [list(r(pool + 128 * t, pool + 128 * t + 128)) for t in range(2)]
    cols += [head(0) + head(2), head(1) + head(3), list(r(qs + 256, qs + 384)), list(r(qs + 384, qs + 512))]
    uq = [96 * h + c for h in range(HEADS) for c in list(r(96)) + list(r(80, 96)) + list(r(64, 80))]
    L = DEPTH
    w_uq = np.transpose(i["w_uq"][:, :, uq].reshape(L, 2, P, 512), (0, 2, 1, 3)).reshape(L, P, -1)
    ukv = [128 * h + c for h in range(HEADS) for c in r(64)] + [128 * h + 64 + c for h in range(HEADS) for c in r(64)]
    pool_w = np.transpose(i["pool_w"].reshape(L, 2, P, 64), (0, 2, 1, 3)).reshape(L, P, -1)
    gate, up = i["w_gate_up"][:, :, :D_FF], i["w_gate_up"][:, :, D_FF:]
    gu = np.stack([gate.reshape(L, DT, P, FT, P), up.reshape(L, DT, P, FT, P)], 0)
    gu = np.transpose(gu, (1, 4, 3, 0, 2, 5)).reshape(L, FT, P, -1)
    down = np.transpose(i["w_down"].reshape(L, FT, P, DT, P), (0, 3, 2, 1, 4)).reshape(L, DT, P, -1)
    vec = [feat_cols(i["attn_norm"]), feat_cols(i["mla_q_norm"]), feat_cols(i["mla_kv_norm"]),
           *[feat_cols(i["conv_w"][:, t]) for t in range(3)], feat_cols(i["pool_scale"]), feat_cols(i["mix_norm"]),
           feat_cols(i["ffn_norm"]), rows_to_all(i["swa_sinks"])]
    c = np.ascontiguousarray
    return {
        "x_t": c(feat_cols(np.transpose(i["x"][0])[None].reshape(D, S).T).transpose(1, 2, 0).reshape(P, DT * S)),
        "w_in1": tiles_kc(i["w_in"], cols),
        "vec1": c(np.concatenate(vec, 2)),
        "w_uq": c(w_uq),
        "w_ukv": c(i["w_ukv"][:, :, ukv]),
        "pool_w": c(pool_w),
        "w_o": tiles_kc(i["w_o"], [list(r(128 * m, 128 * m + 128)) for m in range(DT)]),
        "w_gu": c(gu),
        "w_dn": c(down),
        "fin_g": c(feat_cols(i["final_norm"])),
    }


def lay_out2(i):
    r = lambda a, b: list(range(a, b))
    tiles = [r(P * t, P * t + P) for t in range(10)] + [r(1288 + P * t, 1288 + P * t + P) for t in range(7)]
    tiles += [r(2184, 2312), r(2312, 2440), r(2696, 2824), r(2824, 2952), r(2952, 2968 + P - N_GA), r(1280, 1288) + r(2440, 2696)]
    L = DEPTH
    c = np.ascontiguousarray
    vec = [*[feat_cols(i["ssd_conv_w"][:, t]) for t in range(4)], feat_cols(i["ssd_conv_b"]),
           rows_to_all(i["ssd_dt_bias"]), rows_to_all(i["ssd_a_log"]), feat_cols(np.repeat(i["ssd_d"], 64, 1)),
           feat_cols(i["ssd_norm_g"]), feat_cols(i["rwkv_mu"]), feat_cols(i["rwkv_w0"]), feat_cols(i["rwkv_a0"]),
           feat_cols(i["rwkv_k_k"]), feat_cols(i["rwkv_k_a"]), feat_cols(i["rwkv_r_k"].reshape(L, 256)),
           feat_cols(i["rwkv_ln_g"]), feat_cols(i["rwkv_ln_b"]), feat_cols(i["gla_b_a"]), feat_cols(i["gla_norm_g"]),
           feat_cols(i["ln1_g"]), feat_cols(i["ln1_b"]),
           rows_to_all(i["moe_b_rg"]), rows_to_all(i["moe_b_re"])]
    w_in = np.concatenate([i["w_in"], np.zeros((L, D, P - N_GA), np.float32)], 2)
    route = np.concatenate([i["moe_w_rg"], i["moe_w_re"]], 2)
    return {
        "w_in2": tiles_kc(w_in, tiles),
        "vec2": c(np.concatenate(vec, 2)),
        "lr2": c(np.concatenate([i["rwkv_w2"], i["rwkv_a2"], i["rwkv_g2"]], 1)),
        "wa2": c(i["gla_w_a2"]),
        "w_out": tiles_kc(i["w_out"], [r(P * m, P * m + P) for m in range(DT)]),
        "w_route": tiles_kc(route, [r(0, N_ROUTE)]),
        "ln2": c(np.concatenate([np.concatenate([feat_cols(i["ln_in_g"]), feat_cols(i["ln_in_b"])], 1)[None],
                                 np.concatenate([feat_cols(i["ln2_g"]), feat_cols(i["ln2_b"])], 2)])),
    }


def kernel(**inputs):
    import numpy as _np
    import concourse.bacc as _bacc
    from concourse import mybir as _mybir
    from concourse.bass_utils import run_bass_kernel_spmd as _run

    given = {n: _np.asarray(v) for n, v in inputs.items()}
    second = {n[:-2]: v for n, v in given.items() if n.endswith("_2")}
    arrays = {**lay_out1(given), **lay_out2(second), "const": CONST_ARRAY}
    for n in ("gate", "up", "down"):
        w = second["moe_w_" + n]
        arrays["moe_" + n] = w.reshape((-1,) + w.shape[2:])
    nc = _bacc.Bacc("TRN2", target_bir_lowering=False, num_devices=1)
    aps = {n: nc.dram_tensor(f"in_{n}", v.shape, _mybir.dt.from_np(v.dtype), kind="ExternalInput").ap()
           for n, v in arrays.items()}
    out = nc.dram_tensor("out_t", (P, DT * S), _mybir.dt.float32, kind="ExternalOutput").ap()
    program(nc, aps, out)
    r = _run(nc, [{f"in_{n}": v for n, v in arrays.items()}], core_ids=[0])
    y = r.results[0]["out_t"].reshape(P, DT, S)
    return _np.ascontiguousarray(_np.transpose(y, (2, 1, 0)).reshape(1, S, D))
```
